# Optimizing a Trainium2 kernel written in Bass

```python
import jax, jax.numpy as jnp
from jax import lax
import numpy as np

D_MODEL = 2048
BATCH = 1
SEQ = 256
DEPTH = 2

CHUNK = 64
QBLOCK = 128
N_MEM = 256
EPS = 1e-6
NEG = -1e30

FOX_HEADS = 8
FOX_HEAD_DIM = 128
FOX_WIDTH = FOX_HEADS * FOX_HEAD_DIM

MLA_HEADS = 8
MLA_NOPE = 128
MLA_ROPE = 64
MLA_V = 128
MLA_Q_RANK = 512
MLA_KV_RANK = 256
MLA_WIDTH = MLA_HEADS * MLA_V
ROPE_THETA = 10000.0

GLA_HEADS = 4
GLA_KEY_WIDTH = D_MODEL // 2
GLA_VAL_WIDTH = D_MODEL
GLA_DV = GLA_VAL_WIDTH // GLA_HEADS
GLA_GATE_RANK = 16
GLA_TAU = 16.0

MEM_HEADS = 4
MEM_HEAD_DIM = 128
MEM_WIDTH = MEM_HEADS * MEM_HEAD_DIM

EVEN_SIZES = (FOX_WIDTH, FOX_WIDTH, FOX_WIDTH, FOX_HEADS, FOX_WIDTH,
              MLA_Q_RANK, MLA_KV_RANK, MLA_ROPE, MLA_WIDTH,
              MEM_WIDTH, MEM_WIDTH)
ODD_SIZES = (GLA_KEY_WIDTH, GLA_KEY_WIDTH, GLA_VAL_WIDTH, GLA_GATE_RANK, GLA_VAL_WIDTH,
             MEM_WIDTH, MEM_WIDTH)
EVEN_IN = sum(EVEN_SIZES)
ODD_IN = sum(ODD_SIZES)
EVEN_MIX = FOX_WIDTH + MLA_WIDTH + MEM_WIDTH
ODD_MIX = GLA_VAL_WIDTH + MEM_WIDTH
N_EVEN = (DEPTH + 1) // 2
N_ODD = DEPTH // 2

kernel_name = "hybrid_fox_mla_gla_streaming_encoder"

def rms_norm(x, w):
    xf = x.astype(jnp.float32)
    y = xf * lax.rsqrt(jnp.mean(xf * xf, axis=-1, keepdims=True) + EPS)
    return (y * w.astype(jnp.float32)).astype(x.dtype)

def split_cols(t, sizes):
    idx, acc = [], 0
    for s in sizes[:-1]:
        acc += s
        idx.append(acc)
    return jnp.split(t, idx, axis=-1)

def to_heads(t, n_heads):
    b, s, w = t.shape
    return t.reshape(b, s, n_heads, w // n_heads).transpose(0, 2, 1, 3)

def from_heads(t):
    b, h, s, d = t.shape
    return t.transpose(0, 2, 1, 3).reshape(b, s, h * d)

def rotate(x, cos, sin):
    x1, x2 = jnp.split(x.astype(jnp.float32), 2, axis=-1)
    return jnp.concatenate([x1 * cos - x2 * sin, x1 * sin + x2 * cos], axis=-1).astype(x.dtype)

def forgetting_attention(q, k, v, log_f):
    seq, d = q.shape[2], q.shape[3]
    c = jnp.cumsum(log_f, axis=-1)
    scale = d ** -0.5
    outs = []
    for i in range(seq // QBLOCK):
        lo, hi = i * QBLOCK, (i + 1) * QBLOCK
        s = (jnp.einsum('bhqd,bhkd->bhqk', q[:, :, lo:hi], k[:, :, :hi]).astype(jnp.float32) * scale
             + c[:, :, lo:hi, None] - c[:, :, None, :hi])
        mask = jnp.arange(lo, hi)[:, None] >= jnp.arange(hi)[None, :]
        p = jax.nn.softmax(jnp.where(mask, s, NEG), axis=-1).astype(v.dtype)
        outs.append(jnp.einsum('bhqk,bhkd->bhqd', p, v[:, :, :hi]))
    return jnp.concatenate(outs, axis=2)

def mla_attention(q_nope, q_rope, k_nope, k_rope, v):
    seq = q_nope.shape[2]
    scale = (MLA_NOPE + MLA_ROPE) ** -0.5
    chunk_id = jnp.arange(seq) // CHUNK
    outs = []
    for i in range(seq // QBLOCK):
        lo, hi = i * QBLOCK, (i + 1) * QBLOCK
        s = (jnp.einsum('bhqd,bhkd->bhqk', q_nope[:, :, lo:hi], k_nope[:, :, :hi])
             + jnp.einsum('bhqr,bkr->bhqk', q_rope[:, :, lo:hi], k_rope[:, :hi])).astype(jnp.float32) * scale
        mask = chunk_id[lo:hi, None] >= chunk_id[None, :hi]
        p = jax.nn.softmax(jnp.where(mask, s, NEG), axis=-1).astype(v.dtype)
        outs.append(jnp.einsum('bhqk,bhkd->bhqd', p, v[:, :, :hi]))
    return jnp.concatenate(outs, axis=2)

def gla_chunked(q, k, v, log_a):
    b, h, seq, dk = q.shape
    dv = v.shape[-1]
    n = seq // CHUNK
    qf = (q.astype(jnp.float32) * dk ** -0.5).reshape(b, h, n, CHUNK, dk)
    kf = k.astype(jnp.float32).reshape(b, h, n, CHUNK, dk)
    vf = v.astype(jnp.float32).reshape(b, h, n, CHUNK, dv)
    cum = jnp.cumsum(log_a.reshape(b, h, n, CHUNK, dk), axis=3)
    cum_last = cum[:, :, :, -1:, :]
    q_dec = qf * jnp.exp(cum)
    k_inv = kf * jnp.exp(-cum)
    k_end = kf * jnp.exp(cum_last - cum)
    att = jnp.einsum('bhnqd,bhnkd->bhnqk', q_dec, k_inv)
    causal = jnp.tril(jnp.ones((CHUNK, CHUNK), dtype=bool))
    o_intra = jnp.einsum('bhnqk,bhnke->bhnqe', jnp.where(causal, att, 0.0), vf)
    chunk_decay = jnp.exp(cum_last[:, :, :, 0, :])

    def step(state, xs):
        q_c, k_c, v_c, dec_c = xs
        o_c = jnp.einsum('bhqd,bhde->bhqe', q_c, state)
        state = state * dec_c[..., None] + jnp.einsum('bhkd,bhke->bhde', k_c, v_c)
        return state, o_c

    xs = (jnp.moveaxis(q_dec, 2, 0), jnp.moveaxis(k_end, 2, 0),
          jnp.moveaxis(vf, 2, 0), jnp.moveaxis(chunk_decay, 2, 0))
    state0 = jnp.zeros((b, h, dk, dv), jnp.float32)
    _, o_inter = lax.scan(step, state0, xs)
    o = o_intra + jnp.moveaxis(o_inter, 0, 2)
    return o.reshape(b, h, seq, dv).astype(q.dtype)

def memory_branch(q, gate, mem, mem_norm_w, w_mem_kv):
    mk, mv = jnp.split(rms_norm(mem, mem_norm_w) @ w_mem_kv, 2, axis=-1)
    qh, kh, vh = to_heads(q, MEM_HEADS), to_heads(mk, MEM_HEADS), to_heads(mv, MEM_HEADS)
    s = jnp.einsum('bhqd,bhmd->bhqm', qh, kh).astype(jnp.float32) * MEM_HEAD_DIM ** -0.5
    p = jax.nn.softmax(s, axis=-1).astype(vh.dtype)
    o = from_heads(jnp.einsum('bhqm,bhmd->bhqd', p, vh))
    return o * jax.nn.silu(gate)

def even_layer(x, mem, cos, sin, norm_w, w_in, fox_b_f, mla_q_norm_w, mla_w_uq,
               mla_kv_norm_w, mla_w_ukv, mem_norm_w, w_mem_kv, w_out):
    b, s, _ = x.shape
    h = rms_norm(x, norm_w)
    (fq, fk, fv, ff, fg, cq, ckv, kr, mg, mq, memg) = split_cols(h @ w_in, EVEN_SIZES)
    log_f = jax.nn.log_sigmoid((ff + fox_b_f).astype(jnp.float32)).transpose(0, 2, 1)
    o_a = forgetting_attention(to_heads(fq, FOX_HEADS), to_heads(fk, FOX_HEADS),
                               to_heads(fv, FOX_HEADS), log_f)
    o_a = from_heads(o_a) * jax.nn.silu(fg)
    qh = (rms_norm(cq, mla_q_norm_w) @ mla_w_uq).reshape(b, s, MLA_HEADS, MLA_NOPE + MLA_ROPE)
    qh = qh.transpose(0, 2, 1, 3)
    q_nope, q_rope = qh[..., :MLA_NOPE], rotate(qh[..., MLA_NOPE:], cos[:, None], sin[:, None])
    kvh = (rms_norm(ckv, mla_kv_norm_w) @ mla_w_ukv).reshape(b, s, MLA_HEADS, MLA_NOPE + MLA_V)
    kvh = kvh.transpose(0, 2, 1, 3)
    k_nope, v_b = kvh[..., :MLA_NOPE], kvh[..., MLA_NOPE:]
    k_rope = rotate(kr, cos, sin)
    o_b = from_heads(mla_attention(q_nope, q_rope, k_nope, k_rope, v_b)) * jax.nn.silu(mg)
    o_m = memory_branch(mq, memg, mem, mem_norm_w, w_mem_kv)
    return x + jnp.concatenate([o_a, o_b, o_m], axis=-1) @ w_out

def odd_layer(x, mem, norm_w, w_in, gla_w_a2, gla_b_a, gla_norm_w, mem_norm_w, w_mem_kv, w_out):
    h = rms_norm(x, norm_w)
    (gq, gk, gv, ga, gg, mq, memg) = split_cols(h @ w_in, ODD_SIZES)
    log_a = jax.nn.log_sigmoid((ga @ gla_w_a2 + gla_b_a).astype(jnp.float32)) / GLA_TAU
    o_c = gla_chunked(to_heads(gq, GLA_HEADS), to_heads(gk, GLA_HEADS),
                      to_heads(gv, GLA_HEADS), to_heads(log_a, GLA_HEADS))
    o_c = from_heads(rms_norm(o_c, gla_norm_w)) * jax.nn.silu(gg)
    o_m = memory_branch(mq, memg, mem, mem_norm_w, w_mem_kv)
    return x + jnp.concatenate([o_c, o_m], axis=-1) @ w_out

def setup_inputs(seed: int = 0) -> dict:
    key = jax.random.key(seed)
    ks = jax.random.split(key, 24)
    f32 = jnp.float32

    def nrm(k, shape, scale):
        return jax.random.normal(k, shape, f32) * scale

    def gain(k, shape):
        return 1.0 + 0.02 * jax.random.normal(k, shape, f32)

    offset = jax.random.randint(ks[2], (BATCH, 1), 0, 4096, dtype=jnp.int32)
    positions = offset + jnp.arange(SEQ, dtype=jnp.int32)[None, :]
    return {
        "x": jax.random.normal(ks[0], (BATCH, SEQ, D_MODEL), f32),
        "mem": jax.random.normal(ks[1], (BATCH, N_MEM, D_MODEL), f32),
        "positions": positions,
        "e_norm_w": gain(ks[3], (N_EVEN, D_MODEL)),
        "e_w_in": nrm(ks[4], (N_EVEN, D_MODEL, EVEN_IN), D_MODEL ** -0.5),
        "e_fox_b_f": 2.0 + 0.1 * jax.random.normal(ks[5], (N_EVEN, FOX_HEADS), f32),
        "e_mla_q_norm_w": gain(ks[6], (N_EVEN, MLA_Q_RANK)),
        "e_mla_w_uq": nrm(ks[7], (N_EVEN, MLA_Q_RANK, MLA_HEADS * (MLA_NOPE + MLA_ROPE)), MLA_Q_RANK ** -0.5),
        "e_mla_kv_norm_w": gain(ks[8], (N_EVEN, MLA_KV_RANK)),
        "e_mla_w_ukv": nrm(ks[9], (N_EVEN, MLA_KV_RANK, MLA_HEADS * (MLA_NOPE + MLA_V)), MLA_KV_RANK ** -0.5),
        "e_mem_norm_w": gain(ks[10], (N_EVEN, D_MODEL)),
        "e_w_mem_kv": nrm(ks[11], (N_EVEN, D_MODEL, 2 * MEM_WIDTH), D_MODEL ** -0.5),
        "e_w_out": nrm(ks[12], (N_EVEN, EVEN_MIX, D_MODEL), EVEN_MIX ** -0.5),
        "o_norm_w": gain(ks[13], (N_ODD, D_MODEL)),
        "o_w_in": nrm(ks[14], (N_ODD, D_MODEL, ODD_IN), D_MODEL ** -0.5),
        "o_gla_w_a2": nrm(ks[15], (N_ODD, GLA_GATE_RANK, GLA_KEY_WIDTH), GLA_GATE_RANK ** -0.5),
        "o_gla_b_a": 0.1 * jax.random.normal(ks[16], (N_ODD, GLA_KEY_WIDTH), f32),
        "o_gla_norm_w": gain(ks[17], (N_ODD, GLA_DV)),
        "o_mem_norm_w": gain(ks[18], (N_ODD, D_MODEL)),
        "o_w_mem_kv": nrm(ks[19], (N_ODD, D_MODEL, 2 * MEM_WIDTH), D_MODEL ** -0.5),
        "o_w_out": nrm(ks[20], (N_ODD, ODD_MIX, D_MODEL), ODD_MIX ** -0.5),
        "final_norm_w": gain(ks[21], (D_MODEL,)),
    }

def reference(x, mem, positions, e_norm_w, e_w_in, e_fox_b_f, e_mla_q_norm_w, e_mla_w_uq,
              e_mla_kv_norm_w, e_mla_w_ukv, e_mem_norm_w, e_w_mem_kv, e_w_out,
              o_norm_w, o_w_in, o_gla_w_a2, o_gla_b_a, o_gla_norm_w, o_mem_norm_w,
              o_w_mem_kv, o_w_out, final_norm_w):
    inv_freq = 1.0 / (ROPE_THETA ** (jnp.arange(0, MLA_ROPE, 2, dtype=jnp.float32) / MLA_ROPE))
    ang = positions.astype(jnp.float32)[..., None] * inv_freq
    cos, sin = jnp.cos(ang), jnp.sin(ang)
    for layer in range(DEPTH):
        i = layer // 2
        if layer % 2 == 0:
            x = even_layer(x, mem, cos, sin, e_norm_w[i], e_w_in[i], e_fox_b_f[i],
                           e_mla_q_norm_w[i], e_mla_w_uq[i], e_mla_kv_norm_w[i], e_mla_w_ukv[i],
                           e_mem_norm_w[i], e_w_mem_kv[i], e_w_out[i])
        else:
            x = odd_layer(x, mem, o_norm_w[i], o_w_in[i], o_gla_w_a2[i], o_gla_b_a[i],
                          o_gla_norm_w[i], o_mem_norm_w[i], o_w_mem_kv[i], o_w_out[i])
    return rms_norm(x, final_norm_w)


_drawn_inputs = setup_inputs


def setup_inputs(seed=0):
    import zlib

    import numpy as np

    out = dict(_drawn_inputs(seed))
    spreads = {}
    factors = {'e_norm_w': 7.398,
     'e_fox_b_f': 5.652,
     'e_mla_q_norm_w': 8.0,
     'e_mla_kv_norm_w': 8.0,
     'e_mem_norm_w': 8.0,
     'o_norm_w': 9.142,
     'o_gla_b_a': 7.711,
     'o_gla_norm_w': 51.256,
     'o_mem_norm_w': 30.69,
     'final_norm_w': 7.619}
    for name, (base, spread) in spreads.items():
        noise = np.random.default_rng([zlib.crc32(name.encode()), seed]).standard_normal(out[name].shape)
        drawn = base * np.exp(spread * noise) if base else spread * noise
        out[name] = __import__('jax').numpy.asarray(drawn.astype(out[name].dtype))
    for name, factor in factors.items():
        out[name] = (out[name] * factor).astype(out[name].dtype)
    return out
```

```python
from contextlib import ExitStack

import numpy as np
import concourse.bass as bass
from concourse import mybir

F32 = mybir.dt.float32
F32R = mybir.dt.float32r
BF16 = mybir.dt.bfloat16
I32 = mybir.dt.int32
ALU = mybir.AluOpType
ACT = mybir.ActivationFunctionType
AX = mybir.AxisListType

P = 128
D = 2048
SEQ = 256
TT = SEQ // P
EPS = 1e-6
NEG = -1e30
FOX_H, MLA_H, MEM_H, GLA_H = 8, 8, 4, 4
HD = 128
ROPE = 64
QRANK, KVRANK = 512, 256
MLA_Q, MLA_KV = HD + ROPE, 2 * HD
GLA_DK, GLA_DV = 256, 512
GRANK = 16
TAU = 16.0
CHUNK = 64
MEMW = MEM_H * HD
FOXW = FOX_H * HD
MIX = 2560
MIX_KT = MIX // P

RING = 4
LAG = 4
PW = 512

E_FF = 3 * FOXW
E_FG = E_FF + FOX_H
E_CQ = E_FG + FOXW
E_CKV = E_CQ + QRANK
E_MG = E_CKV + KVRANK + ROPE
E_MQ = E_MG + MLA_H * HD
E_MEMG = E_MQ + MEMW
O_GA = 2 * GLA_H * GLA_DK + GLA_H * GLA_DV
O_GG = O_GA + GRANK
O_MQ = O_GG + GLA_H * GLA_DV
O_MEMG = O_MQ + MEMW

G_E, G_O, G_EM, G_OM, G_CQ, G_CKV, G_GLA, G_BA = 0, 16, 32, 48, 64, 68, 70, 74
G_COLS = 82

MIX_FOX, MIX_MLA, MIX_MEM = 0, FOXW, 2 * FOXW


class Stream:

    def __init__(self, name, w, ktiles, slots, cols, act, ready=None):
        self.name, self.w, self.ktiles, self.slots, self.cols = name, w, ktiles, slots, cols
        self.act, self.ready = act, ready
        self.kc = len(ktiles)
        self.n = len(cols)


def plan_streams():
    full = [2 * c for c in range(8)]
    pan = lambda c0, n: [(c0 + PW * i, PW) for i in range(n)]

    def tr(stage, js):
        return lambda c: [(stage, js[c]), (stage, js[c] + 1)]

    out1 = [0, 2, 4, 6, 16, 18]
    out2 = [8, 10, 12, 14]
    s = [
        Stream("mem_e", "e_w_mem_kv", full, full, pan(0, 2), 0, tr("mem_e", full)),
        Stream("mem_o", "o_w_mem_kv", full, full, pan(0, 2), 1, tr("mem_o", full)),
        Stream("fox", "e_w_in", full, full, pan(0, 6), 0, tr("x_e", full)),
        Stream("ff", "e_w_in", full, full, [(E_FF, FOX_H)], 0),
        Stream("fg", "e_w_in", full, full, pan(E_FG, 2), 0),
        Stream("cq", "e_w_in", full, full, pan(E_CQ, 1), 0),
        Stream("ckv", "e_w_in", full, full, [(E_CKV, KVRANK + ROPE)], 0),
        Stream("mq_e", "e_w_in", full, full, pan(E_MQ, 1), 0),
        Stream("memg_e", "e_w_in", full, full, pan(E_MEMG, 1), 0),
        Stream("mg", "e_w_in", full, full, pan(E_MG, 2), 0),
        Stream("uq", "e_mla_w_uq", [0, 2], [16, 18], pan(0, 3), 0, tr("cq", [0, 2])),
        Stream("ukv", "e_mla_w_ukv", [0], [12], pan(0, 4), 0, tr("ckv", [0])),
        Stream("out1_e", "e_w_out", out1, out1, pan(0, 4), 0, tr("mix_e", out1)),
        Stream("out2_e", "e_w_out", out2, out2, pan(0, 4), 0, tr("mix_e", out2)),
        Stream("ga", "o_w_in", full, full, [(O_GA, GRANK)], 1, tr("x_o", full)),
        Stream("gqkv", "o_w_in", full, full, pan(0, 8), 1),
        Stream("gg", "o_w_in", full, full, pan(O_GG, 4), 1),
        Stream("mq_o", "o_w_in", full, full, pan(O_MQ, 1), 1),
        Stream("memg_o", "o_w_in", full, full, pan(O_MEMG, 1), 1),
        Stream("out1_o", "o_w_out", full, full, pan(0, 4), 1, tr("mix_o", full)),
        Stream("out2_o", "o_w_out", [16, 18], [16, 18], pan(0, 4), 1, tr("mix_o", [16, 18])),
    ]
    chunk = panel = 0
    for x in s:
        x.chunk0, x.panel0 = chunk, panel
        chunk += x.kc * x.n
        panel += x.n
    return s


STREAMS = plan_streams()
AT = {s.name: s for s in STREAMS}
CHUNKS = STREAMS[-1].chunk0 + STREAMS[-1].kc * STREAMS[-1].n
GATES = ("fg", "memg_e", "mg", "gg", "memg_o")

HEADS = ([("fox", h, 0) for h in range(FOX_H)] + [("mem", h, 0) for h in range(MEM_H)]
         + [("mla", h, 0) for h in range(MLA_H)] + [("mem", h, 1) for h in range(MEM_H)])
V_MEM0, V_MLA, V_MEM1 = FOX_H, FOX_H + MEM_H, FOX_H + MEM_H + MLA_H
NH = len(HEADS)
NORMS = ["mem", "x_e", "cq", "ckv", "x_o"] + [f"gla{i}" for i in range(GLA_H * TT)] + ["final"]


def plan_schedule():
    at = []

    def put(n, step, *arg):
        at.append((n, len(at), step, arg))

    def transposes(stage, js, first, per=2):
        for i, j in enumerate(js):
            put(first + i // per, "T", stage, j)

    def head(v, n, b=1, d=3, e=4):
        put(n, "A", v)
        put(n + b, "B", v)
        put(n + d, "D", v)
        put(n + e, "E", v)

    for j in range(4):
        put(-1, "T", "mem_e", j)
    transposes("mem_e", range(4, 16), 0)
    put(0, "sq", "mem")
    transposes("mem_o", range(16), 7)
    c = AT["mem_o"].chunk0
    put(c, "sq", "x_e")
    transposes("x_e", range(16), c + 1)
    for i in range(2):
        put(c + 9 + i, "mk", 0, i)
        put(c + 11 + i, "mk", 1, i)
    c = AT["fg"].chunk0
    put(c + 2, "ffT")
    c = AT["ckv"].chunk0
    put(c + 1, "sq", "cq")
    transposes("cq", range(4), c + 2)
    c = AT["mq_e"].chunk0
    put(c + 1, "sq", "ckv")
    for v in range(FOX_H):
        head(v, c + 4 * v)
    c = AT["uq"].chunk0
    transposes("ckv", range(2), c + 1)
    transposes("mix_e", range(8), c + 3)
    for i in range(MEM_H):
        head(V_MEM0 + i, c + 1 + 2 * i, d=2, e=3)
    put(c + 5, "kr")
    c = AT["out1_e"].chunk0
    transposes("mix_e", range(16, 20), c + 1)
    for i in range(MLA_H):
        head(V_MLA + i, c + 4 + 2 * i, d=2, e=3)
    c = AT["out2_e"].chunk0
    transposes("mix_e", range(8, 14), c - 3)
    transposes("mix_e", range(14, 16), c)
    for i in range(4):
        last = c + 4 * i + 3
        put(last + 1, "sq", "x_o", i)
        transposes("x_o", range(4 * i, 4 * i + 4), last + 1)
    c = AT["gqkv"].chunk0
    put(c + 1, "gaT")
    c = AT["gg"].chunk0
    for h in range(GLA_H):
        n = c + 11 * h
        put(n, "Gz", h)
        for i, step in enumerate(("Gq", "Gk", "Ge", "Ga", "G0", "G1", "G2", "G3")):
            put(n + 4 + i, step, h)
    c = AT["out1_o"].chunk0
    for j in range(4):
        put(c - 1, "T", "mix_o", j)
    transposes("mix_o", range(4, 16), c)
    for i in range(MEM_H):
        head(V_MEM1 + i, c + 1 + 4 * i)
    transposes("mix_o", range(16, 20), AT["out2_o"].chunk0 - 4)
    for i in range(4):
        put(AT["out2_o"].chunk0 + 2 * i + 2, "sq", "final", i)
    at.sort()
    return [(n, step, arg) for n, _, step, arg in at]


SCHEDULE = plan_schedule()


def plan_banks():
    tp, sc = {}, {}

    def tp_use(*key):
        tp[key] = len(tp)

    def sc_use(*key):
        sc[key] = len(sc)

    for _, step, arg in SCHEDULE:
        if step in ("T", "mk", "ffT", "kr", "gaT", "Gz", "Gq", "Gk", "Ge", "D"):
            tp_use(step, *arg)
        elif step == "A":
            tp_use(step, *arg)
            if HEADS[arg[0]][0] == "mla" and HEADS[arg[0]][1] % 2 == 0:
                tp_use("Ar", *arg)
        elif step == "B":
            sc_use(step, *arg)
        elif step == "Ga":
            sc_use(step, *arg)
        elif step in ("G0", "G1", "G2"):
            if step in ("G0", "G2"):
                sc_use("Go", arg[0], int(step[1]) // 2)
            for kk in range(2):
                tp_use("Gs", arg[0], int(step[1]), kk)
    return tp, sc


TP, SC = plan_banks()
AFTER = {}
for _n, _step, _arg in SCHEDULE:
    if _n >= 0:
        AFTER.setdefault(_n, []).append((_step, _arg))
BEFORE = [(step, arg) for n, step, arg in SCHEDULE if n < 0]
PANEL_OF = {s.chunk0 + s.kc * (i + 1) - 1: (s, i) for s in STREAMS for i in range(s.n)}


def lin(a, coef, q):
    return a if q is None else q * coef + a


def looped(s):
    if s.n < 6 or s.kc % 2:
        return 0
    pairs = (s.n - 1) // 2
    first = s.chunk0 + s.kc
    assert not [n for n in AFTER if first - LAG <= n < first + pairs * 2 * s.kc], s.name
    return pairs


def build(nc, t_in, out):
    with ExitStack() as ctx:
        KB = 1024
        top = (nc.sbuf_base + 63) // 64 * 64

        def region(nbytes):
            nonlocal top
            at = top
            top += (nbytes + 63) // 64 * 64
            return at

        def place(name, shape, dt=F32, at=None):
            if at is None:
                at = region(int(np.prod(shape[1:])) * (2 if dt == BF16 else 4))
            return nc.alloc_sbuf_tensor_at(name, shape, dt, offset=at)

        xres = place("xres", [P, TT, D])
        raw = place("raw", [P, RING, 2, PW])
        hi = place("hi", [P, RING, 2, PW], F32R)
        lo = place("lo", [P, RING, 2, PW], F32R)
        region_1, region_2 = region(40 * KB), region(40 * KB)
        act_hi = [place(f"act_hi{i}", [P, MIX_KT, SEQ], F32R, r) for i, r in enumerate((region_1, region_2))]
        act_lo = [place(f"act_lo{i}", [P, MIX_KT, SEQ], F32R, r + 20 * KB)
                  for i, r in enumerate((region_1, region_2))]
        gate = [place("gate0", [P, TT, MIX], F32, region_2), place("gate1", [P, TT, MIX], F32, region_1)]
        s0, s1 = region_2 + 20 * KB, region_1 + 20 * KB
        qk0 = [place(f"qk0_{i}", [P, 2 * SEQ], F32, s0 + 2 * KB * i) for i in range(2)]
        p0 = [place(f"p0_{i}", [P, 2 * SEQ], F32, s0 + (4 + 2 * i) * KB) for i in range(2)]
        pt0 = [place(f"pt0_{i}", [P, 2 * SEQ], F32, s0 + (8 + 2 * i) * KB) for i in range(2)]
        q_rot = place("q_rot", [P, TT, MLA_H * ROPE], F32, s0 + 12 * KB)
        k_rot = place("k_rot", [P, TT, 2, 2, ROPE], F32, s0 + 16 * KB)
        k_rot_t = place("k_rot_t", [P, 2, SEQ], F32, s0 + 18 * KB)
        g_z = place("g_z", [P, 2 * SEQ], F32, s1)
        g_a = place("g_a", [P, 2 * SEQ], F32, s1 + 2 * KB)
        g_cum = place("g_cum", [P, 2 * SEQ], F32, s1 + 4 * KB)
        g_ep = place("g_ep", [P, 2 * SEQ], F32, s1 + 6 * KB)
        g_en = place("g_en", [P, 2 * SEQ], F32, s1 + 8 * KB)
        g_qd = place("g_qd", [P, 2 * SEQ], F32, s1 + 10 * KB)
        g_ke = place("g_ke", [P, TT, GLA_DK], F32, s1 + 12 * KB)
        g_att = place("g_att", [P, TT, P], F32, s1 + 14 * KB)
        g_st = place("g_st", [P, 2, GLA_DV], F32, s1 + 15 * KB)
        proj_at = region(32 * KB)
        proj = place("proj", [P, TT, 4096], F32, proj_at)
        gain_row = place("gain_row", [P, D], F32, proj_at)
        y = place("y", [P, TT, D], F32, proj_at + 8 * KB)
        mk_at, mv_at = [region(4 * KB) for _ in range(2)], [region(4 * KB) for _ in range(2)]
        mkt = [place(f"mkt{i}", [P, MEM_H, SEQ], F32, mk_at[i]) for i in range(2)]
        mv = [place(f"mv{i}", [P, TT, MEMW], F32, mv_at[i]) for i in range(2)]
        wa2 = place("wa2", [GRANK, GLA_H * GLA_DK], F32, mk_at[0])
        p1 = place("p1", [P, 2 * SEQ], F32, mv_at[0])
        pt1 = place("pt1", [P, 2 * SEQ], F32, mv_at[0] + 2 * KB)
        mq = place("mq", [P, TT, MEMW])
        th_at = region(4 * KB)
        th = [place(f"tanh{i}", [P, PW], F32, th_at + 2 * KB * i) for i in range(TT)]
        c_at = region(2 * KB)
        c_pos = place("c_pos", [P, SEQ], F32R, c_at)
        c_neg = place("c_neg", [P, SEQ], F32R, c_at + KB)
        q_rot_t = [place(f"q_rot_t{i}", [P, SEQ], F32, c_at + KB * i) for i in range(2)]
        qk1 = [place(f"qk1_{i}", [P, SEQ], F32, c_at + KB * i) for i in range(2)]
        junk = place("junk", [P, PW], BF16)
        ident = place("ident", [P, P])
        ident_b = place("ident_b", [P, P], BF16)
        fox_mask = place("fox_mask", [P, P], BF16)
        mla_mask = place("mla_mask", [P, P], BF16)
        gla_mask = place("gla_mask", [P, P])
        gains = place("gains", [P, G_COLS])
        half_gla = place("half_gla", [P, GLA_DV // P])
        sel_f = place("sel_f", [P, FOX_H])
        sel = place("sel", [P, FOX_H], F32R)
        fbias = place("fbias", [FOX_H, 1])
        cos = place("cos", [P, TT, ROPE // 2])
        sin = place("sin", [P, TT, ROPE // 2])
        freq = place("freq", [P, ROPE // 2])
        pos_i = place("pos_i", [P, TT], I32)
        pos_f = place("pos_f", [P, TT])
        ssq = place("ssq", [P, len(NORMS), TT, 4])
        rms = place("rms", [P, len(NORMS), TT])
        rms_half = place("rms_half", [P, len(NORMS), TT])
        ntmp = place("ntmp", [P, TT, 4])
        mhalf = place("mhalf", [P, TT])
        half_pi = place("half_pi", [P, 1])
        ones = place("ones", [P, 1])
        ff = place("ff", [P, TT, FOX_H])
        ga = place("ga", [P, TT, GRANK])
        neg_max = place("neg_max", [P, NH, TT])
        rsum = place("rsum", [P, NH, TT])
        rinv = place("rinv", [P, NH, TT])
        fz, fa, fs, fp = (place(f"fox_{n}", [FOX_H, SEQ], F32, s0 + 12 * KB + KB * i) for i, n in enumerate("zasp"))
        t_ang, t_n = (place(f"trig_{n}", [P, TT, ROPE // 2], F32, proj_at + 28 * KB + KB * i)
                      for i, n in enumerate("an"))
        rope_a, rope_b = (place(f"rope_{n}", [P, MLA_H, ROPE // 2], F32, proj_at + 14 * KB + KB * i)
                          for i, n in enumerate("ab"))
        kr_a, kr_b = (place(f"kr_{n}", [P, ROPE // 2], F32, proj_at + (4096 + 3904 + 64 * i) * 4)
                      for i, n in enumerate("ab"))
        c_zero = place("c_zero", [P, SEQ], BF16, th_at)
        ga_t = place("ga_t", [GRANK, SEQ], F32, c_at)
        reset = place("reset", [P, 2 * SEQ], BF16, s1 + 19 * KB)
        assert top <= nc.sbuf_usable_end, (top, nc.sbuf_usable_end)

        bank = [ctx.enter_context(nc.psum_tensor(f"bank{i}", [P, PW], F32)) for i in range(8)]
        acc = [bank[0:2], bank[2:4]]

        def tp(*key):
            return bank[4 + TP[key] % 2]

        def sc(*key):
            return bank[6 + SC[key] % 2]

        def sem(name):
            return ctx.enter_context(nc.semaphore(name))

        mem_in, x_in, small_in, wa2_in, row_in, out_done = map(
            sem, ("mem_in", "x_in", "small_in", "wa2_in", "row_in", "out_done"))
        raw_in = [sem(f"raw_in{i}") for i in range(RING)]
        hi_ready, lo_ready = sem("hi_ready"), sem("lo_ready")
        chunk_used = sem("chunk_used")
        acc_free = [sem(f"acc_free{i}") for i in range(2)]
        tanh_ready = sem("tanh_ready")
        tp_ready = sem("tp_ready")
        tp_free = [sem(f"tp_free{i}") for i in range(2)]
        t_hi_ready = sem("t_hi_ready")
        score_ready, max_ready, exp_ready, out_ready = map(
            sem, ("score_ready", "max_ready", "exp_ready", "out_ready"))
        sc_free = [sem(f"sc_free{i}") for i in range(2)]
        consts_ready, masks_ready, sel_ready = sem("consts_ready"), sem("masks_ready"), sem("sel_ready")
        sq_ready, rms_ready = sem("sq_ready"), sem("rms_ready")
        angle_ready, trig_ready = sem("angle_ready"), sem("trig_ready")
        rope_k_ready, rope_q_ready = sem("rope_k_ready"), sem("rope_q_ready")
        fox_abs_ready, fox_exp_ready, c_ready = sem("fox_abs_ready"), sem("fox_exp_ready"), sem("c_ready")
        gla_log_ready, gla_cum_ready, gla_exp_ready = (
            sem("gla_log_ready"), sem("gla_cum_ready"), sem("gla_exp_ready"))
        gla_end_ready, gla_decay_ready = sem("gla_end_ready"), sem("gla_decay_ready")
        gla_ops_ready, gla_att_ready = sem("gla_ops_ready"), sem("gla_att_ready")
        gla_out_ready = sem("gla_out_ready")
        final_ready = sem("final_ready")
        act_step, dve_step, pool_step = sem("act_step"), sem("dve_step"), sem("pool_step")

        def linker(eng, s):
            count = [0]

            def link(ins):
                count[0] += 1
                ins.then_inc(s, 1)
                eng.wait_ge(s, count[0])
            return link

        def wait_tp_free(eng, *key):
            eng.wait_ge(tp_free[TP[key] % 2], TP[key] // 2 + 1)

        def wait_evac(eng, name, i=None):
            s = AT[name]
            m = s.panel0 + (s.n - 1 if i is None else i)
            eng.wait_ge(acc_free[m % 2], 2 * (m // 2) + 2)

        def slot_of(stage, j):
            return {"cq": 16, "ckv": 12}.get(stage, 0) + j

        def region_of(stage):
            return 1 if stage in ("mem_o", "x_o", "mix_o") else 0

        T_ORDER = [arg for _, step, arg in SCHEDULE if step == "T"]
        T_INDEX = {key: i for i, key in enumerate(T_ORDER)}

        def gain_of(stage, j):
            col = {"mem_e": G_EM, "mem_o": G_OM, "x_e": G_E, "x_o": G_O, "cq": G_CQ, "ckv": G_CKV}
            if stage in col:
                return gains[:, col[stage] + j:col[stage] + j + 1]
            if stage == "mix_o" and j < GLA_H * 4:
                return half_gla[:, j % 4:j % 4 + 1]
            return 0.5

        def source(stage, j, t):
            a, base = {"mem_e": (proj, 0), "mem_o": (proj, 0), "x_e": (xres, 0), "x_o": (xres, 0),
                       "cq": (proj, 3 * FOXW), "ckv": (proj, 3 * FOXW + QRANK),
                       "mix_e": (gate[0], 0), "mix_o": (gate[1], 0)}[stage]
            return a[:, t, base + j * P:base + (j + 1) * P]

        def spans(v):
            if HEADS[v][0] == "mem":
                return [(0, 0, SEQ), (1, SEQ, SEQ)]
            return [(0, 0, P), (1, P, SEQ)]

        def blocks(v):
            return [(t, k) for t, _, n in spans(v) for k in range(n // P)]

        def depth(v):
            return 1 if v >= V_MEM1 else 2

        def buf(v, two, one):
            return two[v % 2] if v < V_MEM1 else one

        def p_of(v):
            return buf(v, p0, p1)

        def pt_of(v):
            return buf(v, pt0, pt1)

        def qk_of(v):
            return (qk0 if v < V_MEM1 else qk1)[v % 2]

        def values(v, k):
            kind, h, layer = HEADS[v]
            if kind == "fox":
                return proj[:, k, 2 * FOXW + h * HD:2 * FOXW + (h + 1) * HD]
            if kind == "mla":
                c = MLA_H * MLA_Q + h * MLA_KV + HD
                return proj[:, k, c:c + HD]
            return mv[layer][:, k, h * HD:(h + 1) * HD]

        def mix_col(v):
            kind, h, _ = HEADS[v]
            return {"fox": MIX_FOX, "mla": MIX_MLA, "mem": MIX_MEM}[kind] + h * HD

        gate_panels = [(s, i) for s in STREAMS if s.name in GATES for i in range(s.n)]
        gate_index = {(s.name, i): k for k, (s, i) in enumerate(gate_panels)}

        def gate_dst(s, i):
            layer = 0 if s.chunk0 < AT["ga"].chunk0 else 1
            c = {"fg": MIX_FOX, "mg": MIX_MLA, "memg_e": MIX_MEM, "gg": 0, "memg_o": MIX_MEM}[s.name] + i * PW
            return gate[layer][:, :, c:c + PW]

        def norm_of(s):
            return NORMS.index({"e_w_mem_kv": "mem", "o_w_mem_kv": "mem", "e_w_in": "x_e", "o_w_in": "x_o",
                                "e_mla_w_uq": "cq", "e_mla_w_ukv": "ckv"}[s.w])

        def copy_dst(s, i, t, q):
            w = s.cols[0][1]
            if s.name in ("mem_e", "mem_o"):
                layer = int(s.name == "mem_o")
                if i == 1:
                    return mv[layer][:, t, :]
                return proj[:, t, D + layer * MEMW:D + (layer + 1) * MEMW]
            if s.name in ("mq_e", "mq_o"):
                return mq[:, t, :]
            if s.name == "ff":
                return ff[:, t, :]
            if s.name == "ga":
                return ga[:, t, :]
            base = {"fox": 0, "gqkv": 0, "uq": 0, "ukv": MLA_H * MLA_Q, "cq": 3 * FOXW,
                    "ckv": 3 * FOXW + QRANK}[s.name]
            return proj[:, t, bass.ds(lin(base + i * PW, 2 * PW, q), w)]

        def run_streams(eng, chunk, side_work, lag):
            for s in STREAMS:
                pairs = looped(s)

                def panel(i, q):
                    for c in range(s.kc):
                        chunk(s, i, c, q)
                        back = c - lag
                        if q is None:
                            side_work(s.chunk0 + i * s.kc + back, None)
                        elif back in (-1, s.kc - 1):
                            side_work(s.chunk0 + i * s.kc + back, q)
                i = 0
                while i < s.n:
                    if i == 1 and pairs:
                        with eng.Fori(0, pairs) as q:
                            panel(1, q)
                            panel(2, q)
                        i += 2 * pairs
                    else:
                        panel(i, None)
                        i += 1
            for n in range(CHUNKS - lag, CHUNKS + 1):
                side_work(n, None)

        def chunk_no(s, i, c, q):
            return lin(s.chunk0 + i * s.kc + c, 2 * s.kc, q)

        def ring_slot(s, i, c):
            return (s.chunk0 + i * s.kc + c) % RING

        block = ctx.enter_context(nc.Block())

        @block.sync
        def _(sp):
            for t in range(TT):
                sp.dma_start(proj[:, t, 0:D], t_in["mem"][0, t * P:(t + 1) * P, :]).then_inc(mem_in, 16)

            def load(s, i, c, q):
                n = s.chunk0 + i * s.kc + c
                if n >= RING:
                    sp.wait_ge(lo_ready, chunk_no(s, i, c, q) - RING + 1)
                c0, w = s.cols[i]
                kt = s.ktiles[c]
                src = t_in[s.w][0, kt * P:(kt + 2) * P, bass.ds(lin(c0, 2 * PW, q), w)]
                sp.dma_start(raw[:, n % RING, :, 0:w],
                             src.rearrange("(k p) n -> p k n", p=P)).then_inc(raw_in[n % RING], 16)

            def side_work(n, q):
                if n == 3:
                    for t in range(TT):
                        sp.dma_start(xres[:, t, :], t_in["x"][0, t * P:(t + 1) * P, :]).then_inc(x_in, 16)
                if n == AT["ga"].chunk0 - 4:
                    sp.wait_ge(score_ready, V_MLA)
                    sp.dma_start(wa2[:, :], t_in["o_gla_w_a2"][0]).then_inc(wa2_in, 16)
                if n == AT["out2_o"].chunk0:
                    sp.wait_ge(gla_out_ready, GLA_H * TT)
                    sp.dma_start(gain_row[:, :], t_in["final_norm_w"].partition_broadcast(P)).then_inc(row_in, 16)

            run_streams(sp, load, side_work, 0)
            for t in range(TT):
                sp.wait_ge(final_ready, t + 1)
                sp.dma_start(out[0, t * P:(t + 1) * P, :], y[:, t, :]).then_inc(out_done, 16)
            sp.wait_ge(out_done, 16 * TT)

        @block.gpsimd
        def _(pool):
            link = linker(pool, pool_step)
            g = nc.gpsimd
            link(g.memset(ident[:, :], 0.0))
            link(g.affine_select(out=ident[:, :], in_=ident[:, :], compare_op=ALU.not_equal, fill=1.0, base=0,
                                 pattern=[[-1, P]], channel_multiplier=1))
            g.memset(mhalf[:, :], -0.5)
            g.memset(half_pi[:, :], float(np.pi / 2))
            g.memset(ones[:, :], 1.0).then_inc(consts_ready, 1)
            link(g.memset(fox_mask[:, :], 0.0))
            link(g.affine_select(out=fox_mask[:, :], in_=fox_mask[:, :], compare_op=ALU.is_ge, fill=NEG, base=0,
                                 pattern=[[-1, P]], channel_multiplier=1))
            link(g.memset(mla_mask[:, :], 0.0))
            link(g.memset(mla_mask[0:CHUNK, CHUNK:P], NEG))
            link(g.memset(gla_mask[:, :], 1.0))
            link(g.affine_select(out=gla_mask[:, :], in_=gla_mask[:, :], compare_op=ALU.is_ge, fill=0.0, base=0,
                                 pattern=[[1, P]], channel_multiplier=-1))
            link(g.memset(gla_mask[0:CHUNK, CHUNK:P], 0.0))
            link(g.memset(sel_f[:, :], 0.0))
            for base in (0, -32):
                link(g.affine_select(out=sel_f[:, :], in_=sel_f[:, :], compare_op=ALU.not_equal, fill=1.0,
                                     base=base, pattern=[[-1, FOX_H]], channel_multiplier=1))
            g.memset(c_zero[:, :], 0.0).then_inc(masks_ready, 1)

            def norm(k, n, width, times=None):
                pool.wait_ge(sq_ready, k + 1)
                total = ssq[:, k, :, 0:1]
                if n == 4:
                    link(g.tensor_tensor(ntmp[:, :, 0:2], ssq[:, k, :, 0:2], ssq[:, k, :, 2:4], ALU.add))
                    link(g.tensor_tensor(ntmp[:, :, 2:3], ntmp[:, :, 0:1], ntmp[:, :, 1:2], ALU.add))
                    total = ntmp[:, :, 2:3]
                link(g.tensor_scalar(ntmp[:, :, 3:4], total, 1.0 / width, EPS, ALU.mult, ALU.add))
                link(g.tensor_tensor(rms[:, k, :], ntmp[:, :, 3], mhalf[:, :], ALU.pow))
                g.tensor_scalar(rms_half[:, k, :], rms[:, k, :], 0.5, 0.0, ALU.mult,
                                ALU.add).then_inc(rms_ready, 1)

            def rotate(dst1, dst2, x1, x2, c, s, a, b):
                link(g.tensor_tensor(a, x1, c, ALU.mult))
                link(g.tensor_tensor(b, x2, s, ALU.mult))
                link(g.tensor_tensor(dst1, a, b, ALU.subtract))
                link(g.tensor_tensor(a, x1, s, ALU.mult))
                link(g.tensor_tensor(b, x2, c, ALU.mult))
                return g.tensor_tensor(dst2, a, b, ALU.add)

            H2 = ROPE // 2
            norm(0, 4, D)
            norm(1, 4, D)
            norm(2, 1, QRANK)
            norm(3, 1, KVRANK)
            pool.wait_ge(trig_ready, 1)
            link(g.memset(k_rot[:, :, :, :, :], 0.0))
            wait_evac(pool, "ckv")
            kc = 3 * FOXW + QRANK + KVRANK
            for t in range(TT):
                for z in range(2):
                    last = rotate(k_rot[:, t, z, z, 0:H2], k_rot[:, t, z, z, H2:ROPE],
                                  proj[:, t, kc:kc + H2], proj[:, t, kc + H2:kc + ROPE],
                                  cos[:, t, :], sin[:, t, :], kr_a[:, :], kr_b[:, :])
                    if (t, z) == (TT - 1, 1):
                        last.then_inc(rope_k_ready, 1)
                    else:
                        link(last)
            wait_evac(pool, "uq")
            wait_evac(pool, "uq", 1)
            for t in range(TT):
                q4 = proj[:, t, 0:MLA_H * MLA_Q].rearrange("p (h d) -> p h d", h=MLA_H)
                r4 = q_rot[:, t, :].rearrange("p (h d) -> p h d", h=MLA_H)
                last = rotate(r4[:, :, 0:H2], r4[:, :, H2:ROPE], q4[:, :, HD:HD + H2], q4[:, :, HD + H2:MLA_Q],
                              cos[:, t:t + 1, :].to_broadcast([P, MLA_H, H2]),
                              sin[:, t:t + 1, :].to_broadcast([P, MLA_H, H2]),
                              rope_a[:, :, :], rope_b[:, :, :])
                if t == TT - 1:
                    last.then_inc(rope_q_ready, 1)
                else:
                    link(last)
            norm(4, 4, D)
            k = NORMS.index("gla0")
            for i in range(GLA_H * TT):
                pool.wait_ge(sq_ready, k + i + 1)
                link(g.tensor_scalar(ntmp[:, 0, 3:4], ssq[:, k + i, 0, 0:1], 1.0 / GLA_DV, EPS, ALU.mult, ALU.add))
                link(g.tensor_tensor(ntmp[:, 0, 2:3], ntmp[:, 0, 3:4], mhalf[:, 0:1], ALU.pow))
                g.tensor_tensor(rms[:, k + i, 0:1], ntmp[:, 0, 2:3], rms[:, 4, i % TT:i % TT + 1],
                                ALU.mult).then_inc(rms_ready, 1)
            norm(len(NORMS) - 1, 4, D)

        @block.scalar
        def _(act):
            link = linker(act, act_step)
            a = nc.scalar
            a.dma_start(gains[:, :], t_in["gains"]).then_inc(small_in, 16)
            a.dma_start(pos_i[:, :], t_in["pos"]).then_inc(small_in, 16)
            a.dma_start(freq[:, :], t_in["freq"]).then_inc(small_in, 16)
            a.dma_start(fbias[:, :], t_in["e_fox_b_f"].rearrange("a h -> h a")).then_inc(small_in, 16)
            act.wait_ge(angle_ready, 1)
            act.wait_ge(consts_ready, 1)
            a.activation(sin[:, :, :], t_ang[:, :, :], ACT.Sin)
            a.activation(cos[:, :, :], t_n[:, :, :], ACT.Sin, bias=half_pi[:, 0:1],
                         scale=-1.0).then_inc(trig_ready, 1)

            def split_hi(s, i, c, q):
                n = s.chunk0 + i * s.kc + c
                w = s.cols[i][1]
                act.wait_ge(raw_in[n % RING], lin(16 * (n // RING + 1), 16 * 2 * s.kc // RING, q))
                if n >= RING:
                    act.wait_ge(chunk_used, chunk_no(s, i, c, q) - RING + 1)
                a.activation(hi[:, n % RING, :, 0:w], raw[:, n % RING, :, 0:w], ACT.Copy).then_inc(hi_ready, 1)

            def move_out(s, i, q):
                if s.name.startswith("out"):
                    return
                act.wait_ge(chunk_used, chunk_no(s, i, s.kc - 1, q) + 1)
                k = norm_of(s)
                act.wait_ge(rms_ready, k + 1)
                b = acc[(s.panel0 + i) % 2]
                w = s.cols[i][1]
                if s.name in GATES:
                    g = gate_index[s.name, i]
                    if g:
                        s1_, i1_ = gate_panels[g - 1]
                        wait_evac(act, s1_.name, i1_)
                    for t in range(TT):
                        a.activation(th[t][:, :], b[t][:, :], ACT.Tanh,
                                     scale=rms_half[:, k, t:t + 1]).then_inc(tanh_ready, 1)
                    return
                if s.name == "uq" and i == 0:
                    act.wait_ge(out_ready, FOX_H)
                for t in range(TT):
                    a.activation(copy_dst(s, i, t, q), b[t][:, 0:w], ACT.Copy,
                                 scale=rms[:, k, t:t + 1]).then_inc(acc_free[(s.panel0 + i) % 2], 1)

            def squares(name, *part):
                k = NORMS.index(name)
                if name in ("cq", "ckv"):
                    wait_evac(act, name)
                    c, w = {"cq": (3 * FOXW, QRANK), "ckv": (3 * FOXW + QRANK, KVRANK)}[name]
                    act.wait_ge(sq_ready, k)
                    link(a.activation(junk[:, 0:w], proj[:, 0, c:c + w], ACT.Square, accum_out=ssq[:, k, 0, 0:1]))
                    a.activation(junk[:, 0:w], proj[:, 1, c:c + w], ACT.Square,
                                 accum_out=ssq[:, k, 1, 0:1]).then_inc(sq_ready, 1)
                    return
                src = proj if name == "mem" else xres
                if name == "mem":
                    act.wait_ge(mem_in, 16 * TT)
                elif name == "x_e":
                    act.wait_ge(x_in, 16 * TT)
                else:
                    wait_evac(act, "out2_e" if name == "x_o" else "out2_o", part[0])
                if k:
                    act.wait_ge(sq_ready, k)
                for j in (part or range(4)):
                    for t in range(TT):
                        ins = a.activation(junk[:, :], src[:, t, j * PW:(j + 1) * PW], ACT.Square,
                                           accum_out=ssq[:, k, t, j:j + 1])
                        if (j, t) == (3, TT - 1):
                            ins.then_inc(sq_ready, 1)
                        else:
                            link(ins)

            def step_t(stage, j):
                u = TP["T", stage, j]
                if u == 0:
                    act.wait_ge(small_in, 16 * 4)
                act.wait_ge(tp_ready, u + 1)
                if stage == "mix_o" and j == 0:
                    act.wait_ge(sel_ready, 1)
                a.activation(act_hi[region_of(stage)][:, slot_of(stage, j), :], tp("T", stage, j)[:, 0:SEQ],
                             ACT.Copy, scale=gain_of(stage, j)).then_inc(t_hi_ready, 1)

            def step_a(v):
                kind, h, _ = HEADS[v]
                scale = float((HD + ROPE) ** -0.5 if kind == "mla" else HD ** -0.5)
                if v >= 2:
                    act.wait_ge(score_ready, v - 1)
                act.wait_ge(tp_ready, TP["A", v] + 1)
                ps, dst = tp("A", v), qk_of(v)
                q = a.activation(dst[:, 0:SEQ], ps[:, 0:SEQ], ACT.Copy, scale=scale)
                if kind == "mem":
                    q.then_inc(tp_free[TP["A", v] % 2], 1)
                    return
                a.activation(dst[:, SEQ:2 * SEQ], ps[:, SEQ:2 * SEQ],
                             ACT.Copy).then_inc(tp_free[TP["A", v] % 2], 1)
                if ("Ar", v) in TP:
                    act.wait_ge(tp_ready, TP["Ar", v] + 1)
                    if h >= 4:
                        act.wait_ge(score_ready, v - 2)
                    a.activation(q_rot_t[h // 2 % 2][:, :], tp("Ar", v)[:, 0:SEQ], ACT.Copy,
                                 scale=scale).then_inc(tp_free[TP["Ar", v] % 2], 1)

            def step_b(v):
                act.wait_ge(max_ready, v + 1)
                d = depth(v)
                if v == V_MEM1:
                    act.wait_ge(out_ready, V_MLA)
                elif v >= d:
                    act.wait_ge(tp_ready, TP["D", v - d] + 1)
                for t, c, n in spans(v):
                    last = a.activation(p_of(v)[:, c:c + n], sc("B", v)[:, c:c + n], ACT.Exp,
                                        bias=neg_max[:, v, t:t + 1], accum_out=rsum[:, v, t:t + 1])
                last.then_inc(exp_ready, 1)

            def step_ff():
                act.wait_ge(fox_abs_ready, 1)
                a.activation(fs[:, :], fa[:, :], ACT.Exp, scale=-1.0).then_inc(fox_exp_ready, 1)

            def step_gz(h):
                u = TP["Gz", h]
                act.wait_ge(tp_ready, u + 1)
                if h:
                    for kk in range(2):
                        wait_tp_free(act, "Gs", h - 1, 2, kk)
                for kk in range(2):
                    k = G_BA + 2 * h + kk
                    z = a.activation(g_z[:, kk * SEQ:(kk + 1) * SEQ], tp("Gz", h)[:, kk * SEQ:(kk + 1) * SEQ],
                                     ACT.Identity, bias=gains[:, k:k + 1])
                z.then_inc(tp_free[u % 2], 1)
                act.wait_ge(tp_free[u % 2], u // 2 + 1)
                link(a.activation(g_a[:, :], g_z[:, :], ACT.Abs))
                link(a.activation(g_a[:, :], g_a[:, :], ACT.Exp, scale=-1.0))
                a.activation(g_a[:, :], g_a[:, :], ACT.Ln, bias=ones[:, 0:1]).then_inc(gla_log_ready, 1)
                act.wait_ge(gla_cum_ready, h + 1)
                a.activation(g_ep[:, :], g_cum[:, :], ACT.Exp, scale=1.0 / TAU)
                a.activation(g_en[:, :], g_cum[:, :], ACT.Exp, scale=-1.0 / TAU).then_inc(gla_exp_ready, 1)
                act.wait_ge(gla_end_ready, h + 1)
                a.activation(g_a[:, :], g_a[:, :], ACT.Exp, scale=1.0 / TAU).then_inc(gla_decay_ready, 1)

            def step_ge(h):
                u = TP["Ge", h]
                act.wait_ge(tp_ready, u + 1)
                a.activation(g_ke[:, :, :].rearrange("p t d -> p (t d)"), tp("Ge", h)[:, :],
                             ACT.Copy).then_inc(tp_free[u % 2], 1)

            def step_go(h, t):
                i = TT * h + t
                act.wait_ge(gla_out_ready, i + 1)
                act.wait_ge(sq_ready, NORMS.index("gla0") + i)
                a.activation(junk[:, :], sc("Go", h, t)[:, :], ACT.Square,
                             accum_out=ssq[:, NORMS.index("gla0") + i, 0, 0:1]).then_inc(sq_ready, 1)

            steps = {"T": step_t, "A": step_a, "B": step_b, "ffT": step_ff, "Gz": step_gz, "Ge": step_ge,
                     "sq": squares, "G1": lambda h: step_go(h, 0), "G3": lambda h: step_go(h, 1)}

            def side_work(n, q):
                if n in PANEL_OF:
                    move_out(*PANEL_OF[n], q)
                if q is None:
                    for step, arg in AFTER.get(n, ()):
                        if step in steps:
                            steps[step](*arg)

            for step, arg in BEFORE:
                steps[step](*arg)
            run_streams(act, split_hi, side_work, LAG)

        @block.vector
        def _(dve):
            link = linker(dve, dve_step)
            d = nc.vector
            dve.wait_ge(small_in, 16 * 4)
            link(d.tensor_copy(pos_f[:, :], pos_i[:, :]))
            for t in range(TT):
                last = d.tensor_scalar(t_ang[:, t, :], freq[:, :], pos_f[:, t:t + 1], None, ALU.mult)
            link(last)
            link(d.tensor_scalar(t_n[:, :, :], t_ang[:, :, :], float(1 / (2 * np.pi)), None, ALU.mult))
            magic = float(1.5 * 2 ** 23)
            link(d.tensor_scalar(t_n[:, :, :], t_n[:, :, :], magic, magic, ALU.add, ALU.subtract))
            rest, parts = 2 * np.pi, []
            for i in range(5):
                grid = 2.0 ** (-3 - 6 * i)
                part = np.floor(rest / grid) * grid if i < 4 else rest
                parts.append(float(part))
                rest -= part
            for part in parts:
                link(d.scalar_tensor_tensor(t_ang[:, :, :], t_n[:, :, :], -part, t_ang[:, :, :],
                                            ALU.mult, ALU.add))
            top_angle = 3.1415925
            link(d.tensor_scalar(t_ang[:, :, :], t_ang[:, :, :], top_angle, -top_angle, ALU.min, ALU.max))
            d.scalar_tensor_tensor(t_n[:, :, :], t_ang[:, :, :], -1.0, t_ang[:, :, :], ALU.mult,
                                   ALU.max).then_inc(angle_ready, 1)
            d.tensor_scalar(half_gla[:, :], gains[:, G_GLA:G_GLA + 4], 0.5, None, ALU.mult).then_inc(sel_ready, 1)

            def split_lo(s, i, c, q):
                n = s.chunk0 + i * s.kc + c
                w = s.cols[i][1]
                dve.wait_ge(hi_ready, chunk_no(s, i, c, q) + 1)
                if n >= RING:
                    dve.wait_ge(chunk_used, chunk_no(s, i, c, q) - RING + 1)
                d.tensor_tensor(lo[:, n % RING, :, 0:w], raw[:, n % RING, :, 0:w],
                                hi[:, n % RING, :, 0:w].bitcast(F32), ALU.subtract).then_inc(lo_ready, 1)

            def move_out(s, i, q):
                m = (s.panel0 + i) % 2
                if s.name in GATES:
                    g = gate_index[s.name, i]
                    dst = gate_dst(s, i)
                    for t in range(TT):
                        dve.wait_ge(tanh_ready, TT * g + t + 1)
                        d.scalar_tensor_tensor(dst[:, t, :], th[t][:, :], 1.0, acc[m][t][:, :], ALU.add,
                                               ALU.mult).then_inc(acc_free[m], 1)
                elif s.name.startswith("out"):
                    dve.wait_ge(chunk_used, chunk_no(s, i, s.kc - 1, q) + 1)
                    if s.name[3] == "2":
                        wait_evac(dve, s.name.replace("2", "1"), i)
                    for t in range(TT):
                        x = xres[:, t, i * PW:(i + 1) * PW]
                        d.tensor_tensor(x, acc[m][t][:, :], x, ALU.add).then_inc(acc_free[m], 1)

            def step_t(stage, j):
                r, at = region_of(stage), slot_of(stage, j)
                dve.wait_ge(t_hi_ready, T_INDEX[stage, j] + 1)
                d.scalar_tensor_tensor(act_lo[r][:, at, :], tp("T", stage, j)[:, 0:SEQ], gain_of(stage, j),
                                       act_hi[r][:, at, :].bitcast(F32), ALU.mult,
                                       ALU.subtract).then_inc(tp_free[TP["T", stage, j] % 2], 1)

            def step_mk(layer, i):
                u = TP["mk", layer, i]
                dve.wait_ge(tp_ready, u + 1)
                d.tensor_copy(mkt[layer][:, 2 * i:2 * i + 2, :].rearrange("p h m -> p (h m)"),
                              tp("mk", layer, i)[:, :]).then_inc(tp_free[u % 2], 1)

            def step_kr():
                u = TP["kr",]
                dve.wait_ge(tp_ready, u + 1)
                d.tensor_copy(k_rot_t[:, :, :].rearrange("p z m -> p (z m)"),
                              tp("kr")[:, :]).then_inc(tp_free[u % 2], 1)

            def step_ff():
                u = TP["ffT",]
                dve.wait_ge(tp_ready, u + 1)
                d.tensor_scalar(fz[:, :], tp("ffT")[0:FOX_H, 0:SEQ], fbias[:, 0:1], None,
                                ALU.add).then_inc(tp_free[u % 2], 1)
                dve.wait_ge(tp_free[u % 2], u // 2 + 1)
                d.scalar_tensor_tensor(fa[:, :], fz[:, :], -1.0, fz[:, :], ALU.mult,
                                       ALU.max).then_inc(fox_abs_ready, 1)
                dve.wait_ge(fox_exp_ready, 1)
                link(d.tensor_scalar(fa[:, :], fs[:, :], 2.0, None, ALU.add))
                link(d.reciprocal(fa[:, :], fa[:, :]))
                link(d.tensor_tensor(fs[:, :], fs[:, :], fa[:, :], ALU.mult))
                link(d.tensor_tensor(fa[:, :], fs[:, :], fs[:, :], ALU.mult))
                link(d.tensor_scalar(fp[:, :], fa[:, :], 1.0 / 17, None, ALU.mult))
                for odd in range(15, 1, -2):
                    link(d.scalar_tensor_tensor(fp[:, :], fp[:, :], 1.0 / odd, fa[:, :], ALU.add, ALU.mult))
                link(d.scalar_tensor_tensor(fp[:, :], fp[:, :], 1.0, fs[:, :], ALU.add, ALU.mult))
                link(d.tensor_scalar(fz[:, :], fz[:, :], 0.0, None, ALU.min))
                link(d.scalar_tensor_tensor(fz[:, :], fp[:, :], -2.0, fz[:, :], ALU.mult, ALU.add))
                link(d.memset(fa[:, :], 1.0))
                link(d.tensor_tensor_scan(fp[:, :], fa[:, :], fz[:, :], 0.0, ALU.mult, ALU.add))
                dve.wait_ge(masks_ready, 1)
                link(d.tensor_copy(c_pos[:, :], c_zero[:, :]))
                link(d.tensor_copy(c_pos[0:FOX_H, :], fp[:, :]))
                link(d.tensor_tensor(c_pos[32:32 + FOX_H, :], fp[:, :], c_pos[0:FOX_H, :].bitcast(F32),
                                     ALU.subtract))
                link(d.tensor_scalar(c_neg[:, :], c_pos[:, :].bitcast(F32), -1.0, None, ALU.mult))
                d.tensor_copy(ident_b[:, :], ident[:, :])
                d.tensor_copy(sel[:, :], sel_f[:, :]).then_inc(c_ready, 1)

            def step_b(v):
                dve.wait_ge(score_ready, v + 1)
                for t, c, n in spans(v):
                    last = d.tensor_reduce(neg_max[:, v, t:t + 1], sc("B", v)[:, c:c + n], AX.X, ALU.max,
                                           negate=True)
                last.then_inc(max_ready, 1)

            def step_d(v):
                u, n = TP["D", v], len(blocks(v)) * P
                dve.wait_ge(tp_ready, u + 1)
                if v >= depth(v):
                    dve.wait_ge(out_ready, v - depth(v) + 1)
                d.tensor_copy(pt_of(v)[:, 0:n], tp("D", v)[:, 0:n]).then_inc(tp_free[u % 2], 1)

            def step_e(v):
                layer = HEADS[v][2]
                k = NORMS.index("x_o" if layer else "x_e")
                dve.wait_ge(exp_ready, v + 1)
                dve.wait_ge(rms_ready, k + 1)
                link(d.reciprocal(rinv[:, v, :], rsum[:, v, :]))
                link(d.tensor_tensor(rinv[:, v, :], rinv[:, v, :], rms[:, k, :], ALU.mult))
                dve.wait_ge(out_ready, v + 1)
                c = mix_col(v)
                for t in range(TT):
                    g = gate[layer][:, t, c:c + HD]
                    last = d.scalar_tensor_tensor(g, sc("B", v)[:, t * P:(t + 1) * P], rinv[:, v, t:t + 1], g,
                                                  ALU.mult, ALU.mult)
                last.then_inc(sc_free[SC["B", v] % 2], 1)

            def step_ga_t():
                u = TP["gaT",]
                dve.wait_ge(tp_ready, u + 1)
                d.tensor_copy(ga_t[:, :], tp("gaT")[0:GRANK, 0:SEQ]).then_inc(tp_free[u % 2], 1)
                link(d.memset(reset[:, :], 1.0))
                link(d.memset(reset[:, :].rearrange("p (c k) -> p c k", k=CHUNK)[:, :, 0:1], 0.0))

            def step_gz(h):
                dve.wait_ge(gla_log_ready, h + 1)
                link(d.scalar_tensor_tensor(g_z[:, :], g_z[:, :], 0.0, g_a[:, :], ALU.min, ALU.subtract))
                d.tensor_tensor_scan(g_cum[:, :], reset[:, :], g_z[:, :], 0.0, ALU.mult,
                                     ALU.add).then_inc(gla_cum_ready, 1)
                dve.wait_ge(gla_cum_ready, h + 1)
                cum = g_cum[:, :].rearrange("p (c k) -> p c k", k=CHUNK)
                d.tensor_tensor(g_a[:, :].rearrange("p (c k) -> p c k", k=CHUNK),
                                cum[:, :, CHUNK - 1:CHUNK].to_broadcast([P, 2 * SEQ // CHUNK, CHUNK]), cum,
                                ALU.subtract).then_inc(gla_end_ready, 1)

            def step_gq(h):
                u = TP["Gq", h]
                dve.wait_ge(tp_ready, u + 1)
                dve.wait_ge(gla_exp_ready, h + 1)
                d.scalar_tensor_tensor(g_qd[:, :], tp("Gq", h)[:, :], float(GLA_DK ** -0.5), g_ep[:, :],
                                       ALU.mult, ALU.mult).then_inc(tp_free[u % 2], 1)

            def step_gk(h):
                u = TP["Gk", h]
                dve.wait_ge(tp_ready, u + 1)
                dve.wait_ge(gla_decay_ready, h + 1)
                d.tensor_tensor(g_a[:, :], tp("Gk", h)[:, :], g_a[:, :], ALU.mult).then_inc(gla_ops_ready, 1)
                d.tensor_tensor(g_en[:, :], tp("Gk", h)[:, :], g_en[:, :], ALU.mult).then_inc(tp_free[u % 2], 1)

            def step_ga(h):
                b = sc("Ga", h)
                dve.wait_ge(gla_att_ready, h + 1)
                for t in range(TT):
                    last = d.tensor_tensor(g_att[:, t, :], b[:, t * P:(t + 1) * P], gla_mask[:, :], ALU.mult)
                last.then_inc(sc_free[SC["Ga", h] % 2], 1)

            def step_state(h, c):
                for kk in range(2):
                    u = TP["Gs", h, c, kk]
                    dve.wait_ge(tp_ready, u + 1)
                    if c == 0:
                        ins = d.tensor_copy(g_st[:, kk, :], tp("Gs", h, c, kk)[:, :])
                    else:
                        at = kk * SEQ + c * CHUNK + CHUNK - 1
                        ins = d.scalar_tensor_tensor(g_st[:, kk, :], g_st[:, kk, :], g_ep[:, at:at + 1],
                                                     tp("Gs", h, c, kk)[:, :], ALU.mult, ALU.add)
                    ins.then_inc(tp_free[u % 2], 1)

            def step_go(h, t):
                i = TT * h + t
                k = NORMS.index("gla0") + i
                dve.wait_ge(rms_ready, k + 1)
                g = gate[1][:, t, h * GLA_DV:(h + 1) * GLA_DV]
                d.scalar_tensor_tensor(g, sc("Go", h, t)[:, :], rms[:, k, 0:1], g, ALU.mult,
                                       ALU.mult).then_inc(sc_free[SC["Go", h, t] % 2], 1)

            def step_g1(h):
                step_state(h, 1)
                step_go(h, 0)

            steps = {"T": step_t, "mk": step_mk, "kr": step_kr, "ffT": step_ff, "B": step_b, "D": step_d,
                     "E": step_e, "gaT": step_ga_t, "Gz": step_gz, "Gq": step_gq, "Gk": step_gk, "Ga": step_ga,
                     "G0": lambda h: step_state(h, 0), "G1": step_g1, "G2": lambda h: step_state(h, 2),
                     "G3": lambda h: step_go(h, 1)}

            def side_work(n, q):
                if n in PANEL_OF:
                    move_out(*PANEL_OF[n], q)
                if q is None:
                    for step, arg in AFTER.get(n, ()):
                        if step in steps:
                            steps[step](*arg)

            for step, arg in BEFORE:
                steps[step](*arg)
            run_streams(dve, split_lo, side_work, LAG)
            k = len(NORMS) - 1
            dve.wait_ge(rms_ready, k + 1)
            dve.wait_ge(row_in, 16)
            for t in range(TT):
                d.scalar_tensor_tensor(y[:, t, :], xres[:, t, :], rms[:, k, t:t + 1], gain_row[:, :], ALU.mult,
                                       ALU.mult).then_inc(final_ready, 1)

        @block.tensor
        def _(pe):
            mm = nc.tensor.matmul
            pe.wait_ge(consts_ready, 1)

            def tr(dst, src):
                return nc.tensor.transpose(dst, src, ident[:, :])

            def take_tp(*key):
                u = TP[key]
                if u >= 2:
                    pe.wait_ge(tp_free[u % 2], u // 2)
                return tp(*key)

            def take_sc(*key):
                u = SC[key]
                if u >= 2:
                    pe.wait_ge(sc_free[u % 2], u // 2)
                return sc(*key)

            def project(s, i, c, q):
                n = s.chunk0 + i * s.kc + c
                w = s.cols[i][1]
                m = s.panel0 + i
                if c == 0 and m >= 2:
                    pe.wait_ge(acc_free[m % 2], lin(2 * (m // 2), 2, q))
                if i == 0 and s.ready and q is None:
                    for key in s.ready(c):
                        wait_tp_free(pe, "T", *key)
                pe.wait_ge(lo_ready, chunk_no(s, i, c, q) + 1)
                for j in range(2):
                    k = s.slots[c] + j
                    first, end = (c == 0 and j == 0), (c == s.kc - 1 and j == 1)
                    wh, wl = hi[:, n % RING, j, 0:w], lo[:, n % RING, j, 0:w]
                    for t in range(TT):
                        xh = act_hi[s.act][:, k, t * P:(t + 1) * P]
                        xl = act_lo[s.act][:, k, t * P:(t + 1) * P]
                        o = acc[m % 2][t][:, 0:w]
                        mm(o, xh, wh, start=first, stop=False)
                        mm(o, xh, wl, start=False, stop=False)
                        last = mm(o, xl, wh, start=False, stop=end)
                last.then_inc(chunk_used, 1)

            def step_t(stage, j):
                b = take_tp("T", stage, j)
                if stage == "mem_e" and j == 0:
                    pe.wait_ge(mem_in, 16 * TT)
                if stage == "x_e" and j == 0:
                    pe.wait_ge(x_in, 16 * TT)
                if stage == "x_o":
                    pe_wait_resid(j)
                if stage in ("cq", "ckv"):
                    wait_evac(pe, stage)
                if stage == "mix_e":
                    v = (j if j < FOX_H else V_MLA + j - FOX_H if j < 16 else V_MEM0 + j - 16)
                    pe.wait_ge(sc_free[SC["B", v] % 2], SC["B", v] // 2 + 1)
                if stage == "mix_o" and j < 16:
                    for t in range(TT):
                        u = SC["Go", j // 4, t]
                        pe.wait_ge(sc_free[u % 2], u // 2 + 1)
                if stage == "mix_o" and j >= 16:
                    u = SC["B", V_MEM1 + j - 16]
                    pe.wait_ge(sc_free[u % 2], u // 2 + 1)
                for t in range(TT):
                    last = tr(b[:, t * P:(t + 1) * P], source(stage, j, t))
                last.then_inc(tp_ready, 1)

            def pe_wait_resid(j):
                wait_evac(pe, "out2_e", j // 4)

            def step_mk(layer, i):
                b = take_tp("mk", layer, i)
                wait_evac(pe, "mem_o" if layer else "mem_e", 0)
                for h in range(2):
                    for t in range(TT):
                        c = D + layer * MEMW + (2 * i + h) * HD
                        last = tr(b[:, h * SEQ + t * P:h * SEQ + (t + 1) * P], proj[:, t, c:c + HD])
                last.then_inc(tp_ready, 1)

            def step_ff():
                b = take_tp("ffT")
                wait_evac(pe, "ff")
                for t in range(TT):
                    last = tr(b[0:FOX_H, t * P:(t + 1) * P], ff[:, t, :])
                last.then_inc(tp_ready, 1)

            def step_kr():
                b = take_tp("kr")
                pe.wait_ge(rope_k_ready, 1)
                for z in range(2):
                    for t in range(TT):
                        last = tr(b[:, z * SEQ + t * P:z * SEQ + (t + 1) * P],
                                  k_rot[:, t, z, :, :].rearrange("p z d -> p (z d)"))
                last.then_inc(tp_ready, 1)

            def step_a(v):
                kind, h, layer = HEADS[v]
                b = take_tp("A", v)
                if kind == "fox":
                    wait_evac(pe, "fox")
                    q, k = (proj, h * HD), (proj, FOXW + h * HD)
                elif kind == "mla":
                    wait_evac(pe, "ukv")
                    wait_evac(pe, "ukv", 2)
                    q, k = (proj, h * MLA_Q), (proj, MLA_H * MLA_Q + h * MLA_KV)
                else:
                    wait_evac(pe, "mq_o" if layer else "mq_e")
                    q, k = (mq, h * HD), None
                for t in range(TT):
                    last = tr(b[:, t * P:(t + 1) * P], q[0][:, t, q[1]:q[1] + HD])
                if k:
                    for t in range(TT):
                        last = tr(b[:, SEQ + t * P:SEQ + (t + 1) * P], k[0][:, t, k[1]:k[1] + HD])
                last.then_inc(tp_ready, 1)
                if ("Ar", v) in TP:
                    b = take_tp("Ar", v)
                    pe.wait_ge(rope_q_ready, 1)
                    for t in range(TT):
                        last = tr(b[:, t * P:(t + 1) * P], q_rot[:, t, h // 2 * P:(h // 2 + 1) * P])
                    last.then_inc(tp_ready, 1)

            def step_b(v):
                kind, h, layer = HEADS[v]
                b = take_sc("B", v)
                wait_tp_free(pe, "A", v)
                qk = qk_of(v)
                if kind == "fox":
                    pe.wait_ge(c_ready, 1)
                if kind == "mla":
                    wait_tp_free(pe, "Ar", v - h % 2)
                    wait_tp_free(pe, "kr")
                for t, c, n in spans(v):
                    o, q = b[:, c:c + n], qk[:, t * P:(t + 1) * P]
                    if kind == "mem":
                        last = mm(o, q, mkt[layer][:, h, :], start=True, stop=True)
                        continue
                    mm(o, q, qk[:, SEQ:SEQ + n], start=True, stop=False)
                    mm(b[:, c + n - P:c + n], ident_b[:, :], (fox_mask if kind == "fox" else mla_mask)[:, :],
                       start=False, stop=False)
                    if kind == "fox":
                        one = sel[:, h:h + 1]
                        mm(o, c_pos[:, t * P:(t + 1) * P], one.to_broadcast([P, n]), start=False, stop=False)
                        last = mm(o, one.to_broadcast([P, P]), c_neg[:, 0:n], start=False, stop=True)
                    else:
                        last = mm(o, q_rot_t[h // 2 % 2][:, t * P:(t + 1) * P], k_rot_t[:, h % 2, 0:n],
                                  start=False, stop=True)
                last.then_inc(score_ready, 1)

            def step_d(v):
                b = take_tp("D", v)
                pe.wait_ge(exp_ready, v + 1)
                for i in range(len(blocks(v))):
                    last = tr(b[:, i * P:(i + 1) * P], p_of(v)[:, i * P:(i + 1) * P])
                last.then_inc(tp_ready, 1)

            def step_e(v):
                wait_tp_free(pe, "D", v)
                b, bl = sc("B", v), blocks(v)
                for i, (t, k) in enumerate(bl):
                    last = mm(b[:, t * P:(t + 1) * P], pt_of(v)[:, i * P:(i + 1) * P], values(v, k),
                              start=(k == 0), stop=(i + 1 == len(bl) or bl[i + 1][0] != t))
                last.then_inc(out_ready, 1)

            def step_ga_t():
                b = take_tp("gaT")
                wait_evac(pe, "ga")
                for t in range(TT):
                    last = tr(b[0:GRANK, t * P:(t + 1) * P], ga[:, t, :])
                last.then_inc(tp_ready, 1)

            def step_gz(h):
                b = take_tp("Gz", h)
                wait_tp_free(pe, "gaT")
                pe.wait_ge(wa2_in, 16)
                for kk in range(2):
                    c = h * GLA_DK + kk * P
                    last = mm(b[:, kk * SEQ:(kk + 1) * SEQ], wa2[:, c:c + P], ga_t[:, :], start=True, stop=True)
                last.then_inc(tp_ready, 1)

            def step_gqk(step, h, base):
                b = take_tp(step, h)
                wait_evac(pe, "gqkv")
                wait_evac(pe, "gqkv", 6)
                for kk in range(2):
                    for t in range(TT):
                        c = base + h * GLA_DK + kk * P
                        last = tr(b[:, kk * SEQ + t * P:kk * SEQ + (t + 1) * P], proj[:, t, c:c + P])
                last.then_inc(tp_ready, 1)

            def step_ge(h):
                b = take_tp("Ge", h)
                pe.wait_ge(gla_ops_ready, h + 1)
                for t in range(TT):
                    for kk in range(2):
                        last = tr(b[:, t * GLA_DK + kk * P:t * GLA_DK + (kk + 1) * P],
                                  g_a[:, kk * SEQ + t * P:kk * SEQ + (t + 1) * P])
                last.then_inc(tp_ready, 1)

            def step_ga(h):
                b = take_sc("Ga", h)
                wait_tp_free(pe, "Gq", h)
                wait_tp_free(pe, "Gk", h)
                for t in range(TT):
                    for kk in range(2):
                        at = kk * SEQ + t * P
                        last = mm(b[:, t * P:(t + 1) * P], g_en[:, at:at + P], g_qd[:, at:at + P],
                                  start=(kk == 0), stop=(kk == 1))
                last.then_inc(gla_att_ready, 1)

            def gla_values(h, c):
                r = c % 2 * CHUNK
                at = 2 * GLA_H * GLA_DK + h * GLA_DV
                return proj[r:r + CHUNK, c // 2, at:at + GLA_DV]

            def step_g(h, c):
                t, r = c // 2, c % 2 * CHUNK
                if r == 0:
                    b = take_sc("Go", h, t)
                    pe.wait_ge(sc_free[SC["Ga", h] % 2], SC["Ga", h] // 2 + 1)
                    at = 2 * GLA_H * GLA_DK + h * GLA_DV
                    mm(b[:, :], g_att[:, t, :], proj[:, t, at:at + GLA_DV], start=True, stop=True)
                b = sc("Go", h, t)
                if c:
                    for kk in range(2):
                        wait_tp_free(pe, "Gs", h, c - 1, kk)
                        at = kk * SEQ + c * CHUNK
                        last = mm(b[r:r + CHUNK, :], g_qd[:, at:at + CHUNK], g_st[:, kk, :], start=False,
                                  stop=(kk == 1), skip_group_check=True)
                if r:
                    last.then_inc(gla_out_ready, 1)
                if c < 3:
                    wait_tp_free(pe, "Ge", h)
                    for kk in range(2):
                        s = take_tp("Gs", h, c, kk)
                        mm(s[:, :], g_ke[r:r + CHUNK, t, kk * P:(kk + 1) * P], gla_values(h, c), start=True,
                           stop=True).then_inc(tp_ready, 1)

            steps = {"T": step_t, "mk": step_mk, "ffT": step_ff, "kr": step_kr, "A": step_a, "B": step_b,
                     "D": step_d, "E": step_e, "gaT": step_ga_t, "Gz": step_gz,
                     "Gq": lambda h: step_gqk("Gq", h, 0),
                     "Gk": lambda h: step_gqk("Gk", h, GLA_H * GLA_DK), "Ge": step_ge, "Ga": step_ga,
                     "G0": lambda h: step_g(h, 0), "G1": lambda h: step_g(h, 1),
                     "G2": lambda h: step_g(h, 2), "G3": lambda h: step_g(h, 3)}

            def side_work(n, q):
                if q is None:
                    for step, arg in AFTER.get(n, ()):
                        if step in steps:
                            steps[step](*arg)

            for step, arg in BEFORE:
                steps[step](*arg)
            run_streams(pe, project, side_work, 0)


WEIGHTS = ["x", "mem", "e_w_in", "e_fox_b_f", "e_mla_w_uq", "e_mla_w_ukv", "e_w_mem_kv", "e_w_out",
           "o_w_in", "o_gla_w_a2", "o_w_mem_kv", "o_w_out", "final_norm_w"]


def kernel(**inputs):
    import concourse.bacc as bacc
    from concourse.bass_utils import run_bass_kernel_spmd

    arrays = {name: np.ascontiguousarray(inputs[name]) for name in WEIGHTS}

    def columns(name):
        return np.asarray(inputs[name])[0].reshape(-1, P).T

    arrays["gains"] = np.ascontiguousarray(np.concatenate([columns(n) for n in (
        "e_norm_w", "o_norm_w", "e_mem_norm_w", "o_mem_norm_w", "e_mla_q_norm_w", "e_mla_kv_norm_w",
        "o_gla_norm_w", "o_gla_b_a")], axis=1))
    arrays["pos"] = np.ascontiguousarray(np.asarray(inputs["positions"]).reshape(TT, P).T)
    f = np.float32(1.0) / (np.float32(10000.0) ** (np.arange(0, ROPE, 2, dtype=np.float32) / np.float32(ROPE)))
    arrays["freq"] = np.ascontiguousarray(np.broadcast_to(f.astype(np.float32), (P, ROPE // 2)))

    nc = bacc.Bacc("TRN2", target_bir_lowering=False, num_devices=1)
    t_in = {name: nc.dram_tensor(f"in_{name}", a.shape, mybir.dt.from_np(a.dtype), kind="ExternalInput").ap()
            for name, a in arrays.items()}
    out = nc.dram_tensor("out_0", (1, SEQ, D), F32, kind="ExternalOutput").ap()
    build(nc, t_in, out)
    r = run_bass_kernel_spmd(nc, [{f"in_{name}": a for name, a in arrays.items()}], core_ids=[0])
    return r.results[0]["out_0"]
```

```python
from contextlib import ExitStack

import numpy as np
import concourse.bass as bass
from concourse import mybir

F32 = mybir.dt.float32
F32R = mybir.dt.float32r
BF16 = mybir.dt.bfloat16
I32 = mybir.dt.int32
ALU = mybir.AluOpType
ACT = mybir.ActivationFunctionType
AX = mybir.AxisListType

P = 128
D = 2048
SEQ = 256
TT = SEQ // P
EPS = 1e-6
NEG = -1e30
FOX_H, MLA_H, MEM_H, GLA_H = 8, 8, 4, 4
HD = 128
ROPE = 64
QRANK, KVRANK = 512, 256
MLA_Q, MLA_KV = HD + ROPE, 2 * HD
GLA_DK, GLA_DV = 256, 512
GRANK = 16
TAU = 16.0
CHUNK = 64
MEMW = MEM_H * HD
FOXW = FOX_H * HD
MIX = 2560
MIX_KT = MIX // P

RING = 4
LAG = 4
PW = 512

E_FF = 3 * FOXW
E_FG = E_FF + FOX_H
E_CQ = E_FG + FOXW
E_CKV = E_CQ + QRANK
E_MG = E_CKV + KVRANK + ROPE
E_MQ = E_MG + MLA_H * HD
E_MEMG = E_MQ + MEMW
O_GA = 2 * GLA_H * GLA_DK + GLA_H * GLA_DV
O_GG = O_GA + GRANK
O_MQ = O_GG + GLA_H * GLA_DV
O_MEMG = O_MQ + MEMW

G_E, G_O, G_EM, G_OM, G_CQ, G_CKV, G_GLA, G_BA = 0, 16, 32, 48, 64, 68, 70, 74
G_COLS = 82

MIX_FOX, MIX_MLA, MIX_MEM = 0, FOXW, 2 * FOXW


class Stream:

    def __init__(self, name, w, ktiles, slots, cols, act, ready=None, per=2):
        self.name, self.w, self.ktiles, self.slots, self.cols = name, w, ktiles, slots, cols
        self.per = per
        self.act, self.ready = act, ready
        self.kc = len(ktiles)
        self.n = len(cols)


def plan_streams():
    full = [2 * c for c in range(8)]
    pan = lambda c0, n: [(c0 + PW * i, PW) for i in range(n)]

    def tr(stage, js):
        return lambda c: [(stage, js[c]), (stage, js[c] + 1)]

    def all_of(stage):
        return lambda c: [(stage, j) for j in range(16)]

    out1 = [0, 2, 4, 6, 16, 18]
    out2 = [8, 10, 12, 14]
    s = [
        Stream("mem_e", "e_w_mem_kv", full, full, pan(0, 2), 0, tr("mem_e", full)),
        Stream("mem_o", "o_w_mem_kv", full, full, pan(0, 2), 1, tr("mem_o", full)),
        Stream("fox", "e_w_in", full, full, pan(0, 6), 0, tr("x_e", full)),
        Stream("ff", "e_ff_w", [0], [0], [(0, FOX_H)], 0, per=16),
        Stream("fg", "e_w_in", full, full, pan(E_FG, 2), 0),
        Stream("cq", "e_w_in", full, full, pan(E_CQ, 1), 0),
        Stream("ckv", "e_w_in", full, full, [(E_CKV, KVRANK + ROPE)], 0),
        Stream("mq_e", "e_w_in", full, full, pan(E_MQ, 1), 0),
        Stream("memg_e", "e_w_in", full, full, pan(E_MEMG, 1), 0),
        Stream("mg", "e_w_in", full, full, pan(E_MG, 2), 0),
        Stream("uq", "e_mla_w_uq", [0, 2], [16, 18], pan(0, 3), 0, tr("cq", [0, 2])),
        Stream("ukv", "e_mla_w_ukv", [0], [12], pan(0, 4), 0, tr("ckv", [0])),
        Stream("out1_e", "e_w_out", out1, out1, pan(0, 4), 0, tr("mix_e", out1)),
        Stream("out2_e", "e_w_out", out2, out2, pan(0, 4), 0, tr("mix_e", out2)),
        Stream("ga", "o_ga_w", [0], [0], [(0, GRANK)], 1, all_of("x_o"), per=16),
        Stream("gqkv", "o_w_in", full, full, pan(0, 8), 1),
        Stream("gg", "o_w_in", full, full, pan(O_GG, 4), 1),
        Stream("mq_o", "o_w_in", full, full, pan(O_MQ, 1), 1),
        Stream("memg_o", "o_w_in", full, full, pan(O_MEMG, 1), 1),
        Stream("out1_o", "o_w_out", full, full, pan(0, 4), 1, tr("mix_o", full)),
        Stream("out2_o", "o_w_out", [16, 18], [16, 18], pan(0, 4), 1, tr("mix_o", [16, 18])),
    ]
    chunk = panel = 0
    for x in s:
        x.chunk0, x.panel0 = chunk, panel
        chunk += x.kc * x.n
        panel += x.n
    return s


STREAMS = plan_streams()
AT = {s.name: s for s in STREAMS}
CHUNKS = STREAMS[-1].chunk0 + STREAMS[-1].kc * STREAMS[-1].n
GATES = ("fg", "memg_e", "mg", "gg", "memg_o")

HEADS = ([("fox", h, 0) for h in range(FOX_H)] + [("mem", h, 0) for h in range(MEM_H)]
         + [("mla", h, 0) for h in range(MLA_H)] + [("mem", h, 1) for h in range(MEM_H)])
V_MEM0, V_MLA, V_MEM1 = FOX_H, FOX_H + MEM_H, FOX_H + MEM_H + MLA_H
NH = len(HEADS)
NORMS = ["mem", "x_e", "cq", "ckv", "x_o"] + [f"gla{i}" for i in range(GLA_H * TT)] + ["final"]


def plan_schedule():
    at = []

    def put(n, step, *arg):
        at.append((n, len(at), step, arg))

    def transposes(stage, js, first, per=2):
        for i, j in enumerate(js):
            put(first + i // per, "T", stage, j)

    def head(v, n, b=1, d=3, e=4):
        put(n, "A", v)
        put(n + b, "B", v)
        put(n + d, "D", v)
        put(n + e, "E", v)

    for j in range(16):
        put(j // 2 - LAG - 1, "S", "mem_e", j)
        put(4 + j // 2, "S", "mem_o", j)
    put(3, "sq", "mem")
    c = AT["mem_o"].chunk0
    put(c, "sq", "x_e")
    for j in range(16):
        put(c + j // 2, "S", "x_e", j)
    for i in range(2):
        put(c + 3 + i, "mk", 0, i)
        put(c + 12 + i, "mk", 1, i)
    c = AT["fg"].chunk0
    put(c + 5, "ffT")
    c = AT["ckv"].chunk0
    put(c + 1, "sq", "cq")
    transposes("cq", range(4), c + 2)
    c = AT["mq_e"].chunk0
    put(c + 1, "sq", "ckv")
    for v in range(FOX_H + MEM_H):
        head(v, c - 1 + (5 * v + 1) // 2)
    c = AT["uq"].chunk0
    transposes("ckv", range(2), c, 1)
    transposes("mix_e", range(8), c + 1)
    transposes("mix_e", range(16, 20), c + 5)
    put(c + 3, "kr")
    c = AT["out1_e"].chunk0
    for i in range(MLA_H):
        head(V_MLA + i, c + 2 + (5 * i + 1) // 2)
    c = AT["out2_e"].chunk0
    transposes("mix_e", range(8, 14), c - 3)
    transposes("mix_e", range(14, 16), c + 1, 1)
    for i in range(4):
        last = c + 4 * i + 3
        put(last + (i < 3), "sq", "x_o", i)
        if i < 3:
            transposes("x_o", range(4 * i, 4 * i + 4), last + 1)
    for j in range(12, 16):
        put(last, "T", "x_o", j)
    c = AT["gqkv"].chunk0
    put(c + 1, "gaT")
    c = AT["gg"].chunk0
    for h in range(GLA_H):
        n = c + 11 * h
        put(n, "Gz", h)
        for i, step in enumerate(("Gq", "Gk", "Ge", "Ga", "G0", "G1")):
            put(n + 4 + i, step, h)
    c = AT["out1_o"].chunk0
    for j in range(4):
        put(c - 1, "T", "mix_o", j)
    transposes("mix_o", range(4, 16), c)
    for i in range(MEM_H):
        head(V_MEM1 + i, c + 1 + 4 * i)
    transposes("mix_o", range(16, 20), AT["out2_o"].chunk0 - 4)
    for i in range(4):
        put(AT["out2_o"].chunk0 + 2 * i + 2, "sq", "final", i)
    at.sort()
    return [(n, step, arg) for n, _, step, arg in at]


SCHEDULE = plan_schedule()


def plan_banks():
    tp, sc = {}, {}

    def tp_use(*key):
        tp[key] = len(tp)

    def sc_use(*key):
        sc[key] = len(sc)

    for _, step, arg in SCHEDULE:
        if step in ("T", "mk", "ffT", "kr", "gaT", "Gz", "Gq", "Gk", "Ge", "D"):
            tp_use(step, *arg)
        elif step == "A":
            tp_use(step, *arg)
            if HEADS[arg[0]][0] == "mla" and HEADS[arg[0]][1] % 2 == 0:
                tp_use("Ar", *arg)
        elif step == "B":
            sc_use(step, *arg)
        elif step == "Ga":
            sc_use(step, *arg)
        elif step in ("G0", "G1"):
            sc_use("Go", arg[0], int(step[1]))
            if step == "G0":
                for kk in range(2):
                    tp_use("Gs", arg[0], kk)
    return tp, sc


TP, SC = plan_banks()
AFTER = {}
for _n, _step, _arg in SCHEDULE:
    if _n >= -LAG:
        AFTER.setdefault(_n, []).append((_step, _arg))
BEFORE = [(step, arg) for n, step, arg in SCHEDULE if n < -LAG]
PANEL_OF = {s.chunk0 + s.kc * (i + 1) - 1: (s, i) for s in STREAMS for i in range(s.n)}


def lin(a, coef, q):
    return a if q is None else q * coef + a


def looped(s):
    if s.n < 6 or s.kc % 2:
        return 0
    pairs = (s.n - 1) // 2
    first = s.chunk0 + s.kc
    assert not [n for n in AFTER if first - LAG <= n < first + pairs * 2 * s.kc], s.name
    return pairs


def build(nc, t_in, out):
    with ExitStack() as ctx:
        KB = 1024
        top = (nc.sbuf_base + 63) // 64 * 64

        def region(nbytes):
            nonlocal top
            at = top
            top += (nbytes + 63) // 64 * 64
            return at

        def place(name, shape, dt=F32, at=None):
            if at is None:
                at = region(int(np.prod(shape[1:])) * (2 if dt == BF16 else 4))
            return nc.alloc_sbuf_tensor_at(name, shape, dt, offset=at)

        xres = place("xres", [P, TT, D])
        raw = place("raw", [P, RING, 2 * PW])
        hi = place("hi", [P, RING, 2 * PW], F32R)
        lo = place("lo", [P, RING, 2 * PW], F32R)
        region_1, region_2 = region(40 * KB), region(40 * KB)
        act_hi = [place(f"act_hi{i}", [P, MIX_KT, SEQ], F32R, r) for i, r in enumerate((region_1, region_2))]
        act_lo = [place(f"act_lo{i}", [P, MIX_KT, SEQ], F32R, r + 20 * KB)
                  for i, r in enumerate((region_1, region_2))]
        gate = [place("gate0", [P, TT, MIX], F32, region_2), place("gate1", [P, TT, MIX], F32, region_1)]
        s0, s1 = region_2 + 20 * KB, region_1 + 20 * KB
        qk0 = [place(f"qk0_{i}", [P, 2 * SEQ], F32, s0 + 2 * KB * i) for i in range(2)]
        p0 = [place(f"p0_{i}", [P, 2 * SEQ], F32, s0 + (4 + 2 * i) * KB) for i in range(2)]
        pt0 = [place(f"pt0_{i}", [P, 2 * SEQ], F32, s0 + (8 + 2 * i) * KB) for i in range(2)]
        q_rot = place("q_rot", [P, TT, MLA_H * ROPE], F32, s0 + 12 * KB)
        k_rot = place("k_rot", [P, TT, 2, 2, ROPE], F32, s0 + 16 * KB)
        k_rot_t = place("k_rot_t", [P, 2, SEQ], F32, s0 + 18 * KB)
        g_z = place("g_z", [P, 2 * SEQ], F32, s1)
        g_a = place("g_a", [P, 2 * SEQ], F32, s1 + 2 * KB)
        g_cum = place("g_cum", [P, 2 * SEQ], F32, s1 + 4 * KB)
        g_ep = place("g_ep", [P, 2 * SEQ], F32, s1 + 6 * KB)
        g_en = place("g_en", [P, 2 * SEQ], F32, s1 + 8 * KB)
        g_qd = place("g_qd", [P, 2 * SEQ], F32, s1 + 10 * KB)
        g_ke = place("g_ke", [P, GLA_DK], F32, s1 + 12 * KB)
        g_ke_t = place("g_ke_t", [P, 2 * P], F32, s1 + 13 * KB)
        g_qs = place("g_qs", [P, 2 * P], F32, s1)
        g_att = place("g_att", [P, TT, P], F32, s1 + 14 * KB)
        g_st = place("g_st", [P, 2, GLA_DV], F32, s1 + 15 * KB)
        proj_at = region(32 * KB)
        proj = place("proj", [P, TT, 4096], F32, proj_at)
        mem_t = place("mem_t", [P, D // P, SEQ], F32, proj_at)
        mem_rows = place("mem_rows", [P, TT, D], F32, proj_at + 16 * KB)
        x_t = place("x_t", [P, D // P, SEQ], F32, proj_at + 16 * KB)
        mk = [place(f"mk{i}", [P, TT, MEMW], F32, region_1 + (16 + 20 * i) * KB) for i in range(2)]
        gain_row = place("gain_row", [P, D], F32, proj_at)
        y = place("y", [P, TT, D], F32, proj_at + 8 * KB)
        mk_at, mv_at = [region(4 * KB) for _ in range(2)], [region(4 * KB) for _ in range(2)]
        mkt = [place(f"mkt{i}", [P, MEM_H, SEQ], F32, mk_at[i]) for i in range(2)]
        mv = [place(f"mv{i}", [P, TT, MEMW], F32, mv_at[i]) for i in range(2)]
        wa2 = place("wa2", [GRANK, GLA_H * GLA_DK], F32, mk_at[0])
        p1 = place("p1", [P, 2 * SEQ], F32, mv_at[0])
        pt1 = place("pt1", [P, 2 * SEQ], F32, mv_at[0] + 2 * KB)
        mq = place("mq", [P, TT, MEMW])
        th_at = region(4 * KB)
        th = [place(f"tanh{i}", [P, PW], F32, th_at + 2 * KB * i) for i in range(TT)]
        c_at = region(2 * KB)
        c_pos = place("c_pos", [P, SEQ], F32R, c_at)
        c_neg = place("c_neg", [P, SEQ], F32R, c_at + KB)
        q_rot_t = [place(f"q_rot_t{i}", [P, SEQ], F32, c_at + KB * i) for i in range(2)]
        qk1 = [place(f"qk1_{i}", [P, SEQ], F32, c_at + KB * i) for i in range(2)]
        junk = place("junk", [P, PW], BF16)
        ident = place("ident", [P, P])
        ident_b = place("ident_b", [P, P], BF16)
        fox_mask = place("fox_mask", [P, P], BF16)
        mla_mask = place("mla_mask", [P, P], BF16)
        gla_mask = place("gla_mask", [P, CHUNK])
        gains = place("gains", [P, G_COLS])
        half_gla = place("half_gla", [P, GLA_DV // P])
        sel_f = place("sel_f", [P, FOX_H])
        sel = place("sel", [P, FOX_H], F32R)
        fbias = place("fbias", [FOX_H, 1])
        cos = place("cos", [P, TT, ROPE // 2])
        sin = place("sin", [P, TT, ROPE // 2])
        freq = place("freq", [P, ROPE // 2])
        pos_i = place("pos_i", [P, TT], I32)
        pos_f = place("pos_f", [P, TT])
        ssq = place("ssq", [P, len(NORMS), TT, 4])
        rms = place("rms", [P, len(NORMS), TT])
        rms_half = place("rms_half", [P, len(NORMS), TT])
        ntmp = place("ntmp", [P, TT, 4])
        mhalf = place("mhalf", [P, TT])
        half_pi = place("half_pi", [P, 1])
        ones = place("ones", [P, 1])
        ff = place("ff", [P, TT, FOX_H])
        ga = place("ga", [P, TT, GRANK])
        neg_max = place("neg_max", [P, NH, TT])
        rsum = place("rsum", [P, NH, TT])
        rinv = place("rinv", [P, NH, TT])
        fz, fa, fs, fp = (place(f"fox_{n}", [FOX_H, SEQ], F32, s0 + 12 * KB + KB * i) for i, n in enumerate("zasp"))
        t_ang, t_n = (place(f"trig_{n}", [P, TT, ROPE // 2], F32, s0 + 18 * KB + KB * i)
                      for i, n in enumerate("an"))
        rope_a, rope_b = (place(f"rope_{n}", [P, MLA_H, ROPE // 2], F32, proj_at + 14 * KB + KB * i)
                          for i, n in enumerate("ab"))
        kr_a, kr_b = (place(f"kr_{n}", [P, ROPE // 2], F32, proj_at + (4096 + 3904 + 64 * i) * 4)
                      for i, n in enumerate("ab"))
        c_zero = place("c_zero", [P, SEQ], BF16, c_at + KB)
        ga_t = place("ga_t", [GRANK, SEQ], F32, c_at)
        reset = place("reset", [P, 2 * SEQ], BF16, s1 + 19 * KB)
        assert top <= nc.sbuf_usable_end, (top, nc.sbuf_usable_end)

        bank = [ctx.enter_context(nc.psum_tensor(f"bank{i}", [P, PW], F32)) for i in range(8)]
        acc = [bank[0:2], bank[2:4]]

        def tp(*key):
            return bank[4 + TP[key] % 2]

        def sc(*key):
            return bank[6 + SC[key] % 2]

        def sem(name):
            return ctx.enter_context(nc.semaphore(name))

        mem_rows_in, x_in, small_in, wa2_in, row_in, out_done = map(
            sem, ("mem_rows_in", "x_in", "small_in", "wa2_in", "row_in", "out_done"))
        mem_t_in = [sem(f"mem_t_in{i}") for i in range(4)]
        x_t_in = sem("x_t_in")
        staged_hi, staged_lo = sem("staged_hi"), sem("staged_lo")
        raw_in = [sem(f"raw_in{i}") for i in range(RING)]
        hi_ready, lo_ready = sem("hi_ready"), sem("lo_ready")
        chunk_used = sem("chunk_used")
        acc_free = [sem(f"acc_free{i}") for i in range(2)]
        tanh_ready = sem("tanh_ready")
        tp_ready = sem("tp_ready")
        tp_free = [sem(f"tp_free{i}") for i in range(2)]
        t_hi_ready = sem("t_hi_ready")
        score_ready, max_ready, exp_ready, out_ready = map(
            sem, ("score_ready", "max_ready", "exp_ready", "out_ready"))
        sc_free = [sem(f"sc_free{i}") for i in range(2)]
        consts_ready, masks_ready, sel_ready = sem("consts_ready"), sem("masks_ready"), sem("sel_ready")
        sq_ready, rms_ready = sem("sq_ready"), sem("rms_ready")
        angle_ready, trig_ready = sem("angle_ready"), sem("trig_ready")
        rope_k_ready, rope_q_ready = sem("rope_k_ready"), sem("rope_q_ready")
        fox_abs_ready, fox_exp_ready, c_ready = sem("fox_abs_ready"), sem("fox_exp_ready"), sem("c_ready")
        gla_log_ready, gla_cum_ready, gla_exp_ready = (
            sem("gla_log_ready"), sem("gla_cum_ready"), sem("gla_exp_ready"))
        gla_end_ready, gla_decay_ready = sem("gla_end_ready"), sem("gla_decay_ready")
        gla_q_ready, gla_ops_ready, gla_att_ready = (
            sem("gla_q_ready"), sem("gla_ops_ready"), sem("gla_att_ready"))
        gla_out_ready = sem("gla_out_ready")
        final_ready = sem("final_ready")
        act_step, dve_step, pool_step = sem("act_step"), sem("dve_step"), sem("pool_step")

        def linker(eng, s):
            count = [0]

            def link(ins):
                count[0] += 1
                ins.then_inc(s, 1)
                eng.wait_ge(s, count[0])
            return link

        def wait_tp_free(eng, *key):
            eng.wait_ge(tp_free[TP[key] % 2], TP[key] // 2 + 1)

        def wait_evac(eng, name, i=None):
            s = AT[name]
            m = s.panel0 + (s.n - 1 if i is None else i)
            eng.wait_ge(acc_free[m % 2], 2 * (m // 2) + 2)

        def slot_of(stage, j):
            return {"cq": 16, "ckv": 12}.get(stage, 0) + j

        def region_of(stage):
            return 1 if stage in ("mem_o", "x_o", "mix_o") else 0

        S_ORDER = [arg for _, step, arg in SCHEDULE if step == "S"]
        S_INDEX = {key: i for i, key in enumerate(S_ORDER)}
        T_ORDER = [arg for _, step, arg in SCHEDULE if step == "T"]
        T_INDEX = {key: i for i, key in enumerate(T_ORDER)}

        def gain_of(stage, j):
            col = {"mem_e": G_EM, "mem_o": G_OM, "x_e": G_E, "x_o": G_O, "cq": G_CQ, "ckv": G_CKV}
            if stage in col:
                return gains[:, col[stage] + j:col[stage] + j + 1]
            if stage == "mix_o" and j < GLA_H * 4:
                return half_gla[:, j % 4:j % 4 + 1]
            return 0.5

        def source(stage, j, t):
            a, base = {"x_o": (xres, 0), "cq": (proj, 3 * FOXW), "ckv": (proj, 3 * FOXW + QRANK),
                       "mix_e": (gate[0], 0), "mix_o": (gate[1], 0)}[stage]
            return a[:, t, base + j * P:base + (j + 1) * P]

        def spans(v):
            if HEADS[v][0] == "mem":
                return [(0, 0, SEQ), (1, SEQ, SEQ)]
            return [(0, 0, P), (1, P, SEQ)]

        def blocks(v):
            return [(t, k) for t, _, n in spans(v) for k in range(n // P)]

        def depth(v):
            return 1 if v >= V_MEM1 else 2

        def buf(v, two, one):
            return two[v % 2] if v < V_MEM1 else one

        def p_of(v):
            return buf(v, p0, p1)

        def pt_of(v):
            return buf(v, pt0, pt1)

        def qk_of(v):
            return (qk0 if v < V_MEM1 else qk1)[v % 2]

        def values(v, k):
            kind, h, layer = HEADS[v]
            if kind == "fox":
                return proj[:, k, 2 * FOXW + h * HD:2 * FOXW + (h + 1) * HD]
            if kind == "mla":
                c = MLA_H * MLA_Q + h * MLA_KV + HD
                return proj[:, k, c:c + HD]
            return mv[layer][:, k, h * HD:(h + 1) * HD]

        def mix_col(v):
            kind, h, _ = HEADS[v]
            return {"fox": MIX_FOX, "mla": MIX_MLA, "mem": MIX_MEM}[kind] + h * HD

        gate_panels = [(s, i) for s in STREAMS if s.name in GATES for i in range(s.n)]
        gate_index = {(s.name, i): k for k, (s, i) in enumerate(gate_panels)}

        def gate_dst(s, i):
            layer = 0 if s.chunk0 < AT["ga"].chunk0 else 1
            c = {"fg": MIX_FOX, "mg": MIX_MLA, "memg_e": MIX_MEM, "gg": 0, "memg_o": MIX_MEM}[s.name] + i * PW
            return gate[layer][:, :, c:c + PW]

        def norm_of(s):
            return NORMS.index({"e_w_mem_kv": "mem", "o_w_mem_kv": "mem", "e_w_in": "x_e", "o_w_in": "x_o",
                                "e_ff_w": "x_e", "o_ga_w": "x_o",
                                "e_mla_w_uq": "cq", "e_mla_w_ukv": "ckv"}[s.w])

        def copy_dst(s, i, t, q):
            w = s.cols[0][1]
            if s.name in ("mem_e", "mem_o"):
                layer = int(s.name == "mem_o")
                if i == 1:
                    return mv[layer][:, t, :]
                return mk[layer][:, t, :]
            if s.name in ("mq_e", "mq_o"):
                return mq[:, t, :]
            if s.name == "ff":
                return ff[:, t, :]
            if s.name == "ga":
                return ga[:, t, :]
            base = {"fox": 0, "gqkv": 0, "uq": 0, "ukv": MLA_H * MLA_Q, "cq": 3 * FOXW,
                    "ckv": 3 * FOXW + QRANK}[s.name]
            return proj[:, t, bass.ds(lin(base + i * PW, 2 * PW, q), w)]

        def run_streams(eng, chunk, side_work, lag):
            def side(s, i, c, q):
                back = c - lag
                if q is None:
                    side_work(s.chunk0 + i * s.kc + back, None)
                elif back in (-1, s.kc - 1):
                    side_work(s.chunk0 + i * s.kc + back, q)

            for s in STREAMS:
                pairs = looped(s)

                def panel(i, q):
                    for c in range(s.kc):
                        if lag:
                            side(s, i, c, q)
                        chunk(s, i, c, q)
                        if not lag:
                            side(s, i, c, q)
                i = 0
                while i < s.n:
                    if i == 1 and pairs:
                        with eng.Fori(0, pairs) as q:
                            panel(1, q)
                            panel(2, q)
                        i += 2 * pairs
                    else:
                        panel(i, None)
                        i += 1
            for n in range(CHUNKS - lag, CHUNKS + 1):
                side_work(n, None)

        def chunk_no(s, i, c, q):
            return lin(s.chunk0 + i * s.kc + c, 2 * s.kc, q)

        def slot(ring, s, i, c):
            n, w = s.chunk0 + i * s.kc + c, s.cols[i][1]
            return ring[:, n % RING, 0:s.per * w].rearrange("p (k n) -> p k n", k=s.per)

        block = ctx.enter_context(nc.Block())

        @block.sync
        def _(sp):
            def load_mem_t(i):
                sp.dma_start(mem_t[:, 4 * i:4 * i + 4, :],
                             t_in["mem_t"][4 * P * i:4 * P * (i + 1), :].rearrange("(k p) m -> p k m", p=P)
                             ).then_inc(mem_t_in[i], 16)

            def load(s, i, c, q):
                n = s.chunk0 + i * s.kc + c
                if n >= RING:
                    sp.wait_ge(lo_ready, chunk_no(s, i, c, q) - RING + 1)
                c0, w = s.cols[i]
                if s.per == 2:
                    kt = s.ktiles[c]
                    src = t_in[s.w][0, kt * P:(kt + 2) * P, bass.ds(lin(c0, 2 * PW, q), w)]
                    src = src.rearrange("(k p) n -> p k n", p=P)
                else:
                    src = t_in[s.w]
                sp.dma_start(slot(raw, s, i, c), src).then_inc(raw_in[n % RING], 16)

            def side_work(n, q):
                if 0 <= n < 3:
                    load_mem_t(n + 1)
                if n == 4:
                    for t in range(TT):
                        sp.dma_start(mem_rows[:, t, :],
                                     t_in["mem"][0, t * P:(t + 1) * P, :]).then_inc(mem_rows_in, 16)
                if n == 13:
                    sp.wait_ge(sq_ready, 1)
                    sp.dma_start(x_t[:, :, :], t_in["x_t"].rearrange("(k p) m -> p k m", p=P)).then_inc(x_t_in, 16)
                if n == 17:
                    for t in range(TT):
                        sp.dma_start(xres[:, t, :], t_in["x"][0, t * P:(t + 1) * P, :]).then_inc(x_in, 16)
                if n == AT["ga"].chunk0 - 4:
                    sp.wait_ge(score_ready, V_MLA)
                    sp.dma_start(wa2[:, :], t_in["o_gla_w_a2"][0]).then_inc(wa2_in, 16)
                if n == AT["out2_o"].chunk0 - 8:
                    sp.wait_ge(gla_out_ready, GLA_H * TT)
                    sp.dma_start(gain_row[:, :], t_in["final_norm_w"].partition_broadcast(P)).then_inc(row_in, 16)

            load_mem_t(0)
            run_streams(sp, load, side_work, 0)
            for t in range(TT):
                sp.wait_ge(final_ready, t + 1)
                sp.dma_start(out[0, t * P:(t + 1) * P, :], y[:, t, :]).then_inc(out_done, 16)
            sp.wait_ge(out_done, 16 * TT)

        @block.gpsimd
        def _(pool):
            link = linker(pool, pool_step)
            g = nc.gpsimd
            link(g.memset(ident[:, :], 0.0))
            link(g.affine_select(out=ident[:, :], in_=ident[:, :], compare_op=ALU.not_equal, fill=1.0, base=0,
                                 pattern=[[-1, P]], channel_multiplier=1))
            g.memset(mhalf[:, :], -0.5)
            g.memset(half_pi[:, :], float(np.pi / 2))
            g.memset(ones[:, :], 1.0).then_inc(consts_ready, 1)
            link(g.memset(fox_mask[:, :], 0.0))
            link(g.affine_select(out=fox_mask[:, :], in_=fox_mask[:, :], compare_op=ALU.is_ge, fill=NEG, base=0,
                                 pattern=[[-1, P]], channel_multiplier=1))
            link(g.memset(mla_mask[:, :], 0.0))
            link(g.memset(mla_mask[0:CHUNK, CHUNK:P], NEG))
            link(g.memset(gla_mask[:, :], 1.0))
            for r in range(0, P, CHUNK):
                link(g.affine_select(out=gla_mask[r:r + CHUNK, :], in_=gla_mask[r:r + CHUNK, :],
                                     compare_op=ALU.is_ge, fill=0.0, base=0, pattern=[[1, CHUNK]],
                                     channel_multiplier=-1))
            link(g.memset(sel_f[:, :], 0.0))
            for base in (0, -32):
                link(g.affine_select(out=sel_f[:, :], in_=sel_f[:, :], compare_op=ALU.not_equal, fill=1.0,
                                     base=base, pattern=[[-1, FOX_H]], channel_multiplier=1))
            g.memset(c_zero[:, :], 0.0).then_inc(masks_ready, 1)

            def norm(k, n, width, times=None):
                pool.wait_ge(sq_ready, k + 1)
                total = ssq[:, k, :, 0:1]
                if n == 4:
                    link(g.tensor_tensor(ntmp[:, :, 0:2], ssq[:, k, :, 0:2], ssq[:, k, :, 2:4], ALU.add))
                    link(g.tensor_tensor(ntmp[:, :, 2:3], ntmp[:, :, 0:1], ntmp[:, :, 1:2], ALU.add))
                    total = ntmp[:, :, 2:3]
                link(g.tensor_scalar(ntmp[:, :, 3:4], total, 1.0 / width, EPS, ALU.mult, ALU.add))
                link(g.tensor_tensor(rms[:, k, :], ntmp[:, :, 3], mhalf[:, :], ALU.pow))
                g.tensor_scalar(rms_half[:, k, :], rms[:, k, :], 0.5, 0.0, ALU.mult,
                                ALU.add).then_inc(rms_ready, 1)

            def rotate(dst1, dst2, x1, x2, c, s, a, b):
                link(g.tensor_tensor(a, x1, c, ALU.mult))
                link(g.tensor_tensor(b, x2, s, ALU.mult))
                link(g.tensor_tensor(dst1, a, b, ALU.subtract))
                link(g.tensor_tensor(a, x1, s, ALU.mult))
                link(g.tensor_tensor(b, x2, c, ALU.mult))
                return g.tensor_tensor(dst2, a, b, ALU.add)

            H2 = ROPE // 2
            norm(0, 4, D)
            norm(1, 4, D)
            norm(2, 1, QRANK)
            norm(3, 1, KVRANK)
            pool.wait_ge(trig_ready, 1)
            link(g.memset(k_rot[:, :, :, :, :], 0.0))
            wait_evac(pool, "ckv")
            kc = 3 * FOXW + QRANK + KVRANK
            for t in range(TT):
                for z in range(2):
                    last = rotate(k_rot[:, t, z, z, 0:H2], k_rot[:, t, z, z, H2:ROPE],
                                  proj[:, t, kc:kc + H2], proj[:, t, kc + H2:kc + ROPE],
                                  cos[:, t, :], sin[:, t, :], kr_a[:, :], kr_b[:, :])
                    if (t, z) == (TT - 1, 1):
                        last.then_inc(rope_k_ready, 1)
                    else:
                        link(last)
            wait_evac(pool, "uq")
            wait_evac(pool, "uq", 1)
            for t in range(TT):
                q4 = proj[:, t, 0:MLA_H * MLA_Q].rearrange("p (h d) -> p h d", h=MLA_H)
                r4 = q_rot[:, t, :].rearrange("p (h d) -> p h d", h=MLA_H)
                last = rotate(r4[:, :, 0:H2], r4[:, :, H2:ROPE], q4[:, :, HD:HD + H2], q4[:, :, HD + H2:MLA_Q],
                              cos[:, t:t + 1, :].to_broadcast([P, MLA_H, H2]),
                              sin[:, t:t + 1, :].to_broadcast([P, MLA_H, H2]),
                              rope_a[:, :, :], rope_b[:, :, :])
                if t == TT - 1:
                    last.then_inc(rope_q_ready, 1)
                else:
                    link(last)
            norm(4, 4, D)
            k = NORMS.index("gla0")
            for i in range(GLA_H * TT):
                pool.wait_ge(sq_ready, k + i + 1)
                link(g.tensor_scalar(ntmp[:, 0, 3:4], ssq[:, k + i, 0, 0:1], 1.0 / GLA_DV, EPS, ALU.mult, ALU.add))
                link(g.tensor_tensor(ntmp[:, 0, 2:3], ntmp[:, 0, 3:4], mhalf[:, 0:1], ALU.pow))
                g.tensor_tensor(rms[:, k + i, 0:1], ntmp[:, 0, 2:3], rms[:, 4, i % TT:i % TT + 1],
                                ALU.mult).then_inc(rms_ready, 1)
            norm(len(NORMS) - 1, 4, D)

        @block.scalar
        def _(act):
            link = linker(act, act_step)
            a = nc.scalar
            a.dma_start(gains[:, :], t_in["gains"]).then_inc(small_in, 16)
            a.dma_start(pos_i[:, :], t_in["pos"]).then_inc(small_in, 16)
            a.dma_start(freq[:, :], t_in["freq"]).then_inc(small_in, 16)
            a.dma_start(fbias[:, :], t_in["e_fox_b_f"].rearrange("a h -> h a")).then_inc(small_in, 16)
            act.wait_ge(angle_ready, 1)
            act.wait_ge(consts_ready, 1)
            a.activation(sin[:, :, :], t_ang[:, :, :], ACT.Sin)
            a.activation(cos[:, :, :], t_n[:, :, :], ACT.Sin, bias=half_pi[:, 0:1],
                         scale=-1.0).then_inc(trig_ready, 1)

            def split_hi(s, i, c, q):
                n = s.chunk0 + i * s.kc + c
                act.wait_ge(raw_in[n % RING], lin(16 * (n // RING + 1), 16 * 2 * s.kc // RING, q))
                if n >= RING:
                    act.wait_ge(chunk_used, chunk_no(s, i, c, q) - RING + 1)
                a.activation(slot(hi, s, i, c), slot(raw, s, i, c), ACT.Copy).then_inc(hi_ready, 1)

            def move_out(s, i, q):
                if s.name.startswith("out"):
                    return
                act.wait_ge(chunk_used, chunk_no(s, i, s.kc - 1, q) + 1)
                k = norm_of(s)
                act.wait_ge(rms_ready, k + 1)
                b = acc[(s.panel0 + i) % 2]
                w = s.cols[i][1]
                if s.name in GATES:
                    g = gate_index[s.name, i]
                    if g:
                        s1_, i1_ = gate_panels[g - 1]
                        wait_evac(act, s1_.name, i1_)
                    for t in range(TT):
                        a.activation(th[t][:, :], b[t][:, :], ACT.Tanh,
                                     scale=rms_half[:, k, t:t + 1]).then_inc(tanh_ready, 1)
                    return
                if s.name == "uq" and i == 0:
                    act.wait_ge(out_ready, FOX_H)
                for t in range(TT):
                    a.activation(copy_dst(s, i, t, q), b[t][:, 0:w], ACT.Copy,
                                 scale=rms[:, k, t:t + 1]).then_inc(acc_free[(s.panel0 + i) % 2], 1)

            def squares(name, *part):
                k = NORMS.index(name)
                if name in ("cq", "ckv"):
                    wait_evac(act, name)
                    c, w = {"cq": (3 * FOXW, QRANK), "ckv": (3 * FOXW + QRANK, KVRANK)}[name]
                    act.wait_ge(sq_ready, k)
                    link(a.activation(junk[:, 0:w], proj[:, 0, c:c + w], ACT.Square, accum_out=ssq[:, k, 0, 0:1]))
                    a.activation(junk[:, 0:w], proj[:, 1, c:c + w], ACT.Square,
                                 accum_out=ssq[:, k, 1, 0:1]).then_inc(sq_ready, 1)
                    return
                src = mem_rows if name == "mem" else xres
                if name == "mem":
                    act.wait_ge(mem_rows_in, 16 * TT)
                elif name == "x_e":
                    act.wait_ge(x_in, 16 * TT)
                else:
                    wait_evac(act, "out2_e" if name == "x_o" else "out2_o", part[0])
                if k:
                    act.wait_ge(sq_ready, k)
                for j in (part or range(4)):
                    for t in range(TT):
                        ins = a.activation(junk[:, :], src[:, t, j * PW:(j + 1) * PW], ACT.Square,
                                           accum_out=ssq[:, k, t, j:j + 1])
                        if (j, t) == (3, TT - 1):
                            ins.then_inc(sq_ready, 1)
                        else:
                            link(ins)

            def step_t(stage, j):
                u = TP["T", stage, j]
                act.wait_ge(tp_ready, u + 1)
                if stage == "mix_o" and j == 0:
                    act.wait_ge(sel_ready, 1)
                a.activation(act_hi[region_of(stage)][:, slot_of(stage, j), :], tp("T", stage, j)[:, 0:SEQ],
                             ACT.Copy, scale=gain_of(stage, j)).then_inc(t_hi_ready, 1)

            def step_s(stage, j):
                if S_INDEX[stage, j] == 0:
                    act.wait_ge(small_in, 16 * 4)
                src = mem_t
                if stage == "x_e":
                    act.wait_ge(chunk_used, AT["mem_o"].chunk0)
                    act.wait_ge(x_t_in, 16)
                    src = x_t
                else:
                    act.wait_ge(mem_t_in[j // 4], 16)
                a.activation(act_hi[int(stage == "mem_o")][:, j, :], src[:, j, :], ACT.Copy,
                             scale=gain_of(stage, j)).then_inc(staged_hi, 1)

            def step_a(v):
                kind, h, _ = HEADS[v]
                scale = float((HD + ROPE) ** -0.5 if kind == "mla" else HD ** -0.5)
                if v >= 2:
                    act.wait_ge(score_ready, v - 1)
                act.wait_ge(tp_ready, TP["A", v] + 1)
                ps, dst = tp("A", v), qk_of(v)
                q = a.activation(dst[:, 0:SEQ], ps[:, 0:SEQ], ACT.Copy, scale=scale)
                if kind == "mem":
                    q.then_inc(tp_free[TP["A", v] % 2], 1)
                    return
                a.activation(dst[:, SEQ:2 * SEQ], ps[:, SEQ:2 * SEQ],
                             ACT.Copy).then_inc(tp_free[TP["A", v] % 2], 1)
                if ("Ar", v) in TP:
                    act.wait_ge(tp_ready, TP["Ar", v] + 1)
                    if h >= 4:
                        act.wait_ge(score_ready, v - 2)
                    a.activation(q_rot_t[h // 2 % 2][:, :], tp("Ar", v)[:, 0:SEQ], ACT.Copy,
                                 scale=scale).then_inc(tp_free[TP["Ar", v] % 2], 1)

            def step_b(v):
                act.wait_ge(max_ready, v + 1)
                d = depth(v)
                if v == V_MEM1:
                    act.wait_ge(out_ready, V_MLA)
                elif v >= d:
                    act.wait_ge(tp_ready, TP["D", v - d] + 1)
                for t, c, n in spans(v):
                    last = a.activation(p_of(v)[:, c:c + n], sc("B", v)[:, c:c + n], ACT.Exp,
                                        bias=neg_max[:, v, t:t + 1], accum_out=rsum[:, v, t:t + 1])
                last.then_inc(exp_ready, 1)

            def step_ff():
                act.wait_ge(fox_abs_ready, 1)
                a.activation(fs[:, :], fa[:, :], ACT.Exp, scale=-1.0).then_inc(fox_exp_ready, 1)

            def step_gz(h):
                u = TP["Gz", h]
                act.wait_ge(tp_ready, u + 1)
                if h:
                    act.wait_ge(gla_out_ready, TT * h)
                for kk in range(2):
                    k = G_BA + 2 * h + kk
                    z = a.activation(g_z[:, kk * SEQ:(kk + 1) * SEQ], tp("Gz", h)[:, kk * SEQ:(kk + 1) * SEQ],
                                     ACT.Identity, bias=gains[:, k:k + 1])
                z.then_inc(tp_free[u % 2], 1)
                act.wait_ge(tp_free[u % 2], u // 2 + 1)
                link(a.activation(g_a[:, :], g_z[:, :], ACT.Abs))
                link(a.activation(g_a[:, :], g_a[:, :], ACT.Exp, scale=-1.0))
                a.activation(g_a[:, :], g_a[:, :], ACT.Ln, bias=ones[:, 0:1]).then_inc(gla_log_ready, 1)
                act.wait_ge(gla_cum_ready, h + 1)
                a.activation(g_ep[:, :], g_cum[:, :], ACT.Exp, scale=1.0 / TAU)
                a.activation(g_en[:, :], g_cum[:, :], ACT.Exp, scale=-1.0 / TAU).then_inc(gla_exp_ready, 1)
                act.wait_ge(gla_end_ready, h + 1)
                a.activation(g_a[:, :], g_a[:, :], ACT.Exp, scale=1.0 / TAU).then_inc(gla_decay_ready, 1)

            def step_ge(h):
                u = TP["Ge", h]
                act.wait_ge(tp_ready, u + 1)
                a.activation(g_ke[:, :], tp("Ge", h)[:, 0:GLA_DK], ACT.Copy).then_inc(tp_free[u % 2], 1)

            def step_go(h, t):
                i = TT * h + t
                act.wait_ge(gla_out_ready, i + 1)
                act.wait_ge(sq_ready, NORMS.index("gla0") + i)
                a.activation(junk[:, :], sc("Go", h, t)[:, :], ACT.Square,
                             accum_out=ssq[:, NORMS.index("gla0") + i, 0, 0:1]).then_inc(sq_ready, 1)

            steps = {"T": step_t, "S": step_s, "A": step_a, "B": step_b, "ffT": step_ff, "Gz": step_gz,
                     "Ge": step_ge, "sq": squares, "G0": lambda h: step_go(h, 0), "G1": lambda h: step_go(h, 1)}

            def side_work(n, q):
                if n in PANEL_OF:
                    move_out(*PANEL_OF[n], q)
                if q is None:
                    for step, arg in AFTER.get(n, ()):
                        if step in steps:
                            steps[step](*arg)

            for step, arg in BEFORE:
                if step in steps:
                    steps[step](*arg)
            run_streams(act, split_hi, side_work, LAG)

        @block.vector
        def _(dve):
            link = linker(dve, dve_step)
            d = nc.vector
            dve.wait_ge(small_in, 16 * 4)
            link(d.tensor_copy(pos_f[:, :], pos_i[:, :]))
            for t in range(TT):
                last = d.tensor_scalar(t_ang[:, t, :], freq[:, :], pos_f[:, t:t + 1], None, ALU.mult)
            link(last)
            link(d.tensor_scalar(t_n[:, :, :], t_ang[:, :, :], float(1 / (2 * np.pi)), None, ALU.mult))
            magic = float(1.5 * 2 ** 23)
            link(d.tensor_scalar(t_n[:, :, :], t_n[:, :, :], magic, magic, ALU.add, ALU.subtract))
            rest, parts = 2 * np.pi, []
            for i in range(5):
                grid = 2.0 ** (-3 - 6 * i)
                part = np.floor(rest / grid) * grid if i < 4 else rest
                parts.append(float(part))
                rest -= part
            for part in parts:
                link(d.scalar_tensor_tensor(t_ang[:, :, :], t_n[:, :, :], -part, t_ang[:, :, :],
                                            ALU.mult, ALU.add))
            top_angle = 3.1415925
            link(d.tensor_scalar(t_ang[:, :, :], t_ang[:, :, :], top_angle, -top_angle, ALU.min, ALU.max))
            d.scalar_tensor_tensor(t_n[:, :, :], t_ang[:, :, :], -1.0, t_ang[:, :, :], ALU.mult,
                                   ALU.max).then_inc(angle_ready, 1)
            d.tensor_scalar(half_gla[:, :], gains[:, G_GLA:G_GLA + 4], 0.5, None, ALU.mult).then_inc(sel_ready, 1)

            def split_lo(s, i, c, q):
                n = s.chunk0 + i * s.kc + c
                dve.wait_ge(hi_ready, chunk_no(s, i, c, q) + 1)
                if n >= RING:
                    dve.wait_ge(chunk_used, chunk_no(s, i, c, q) - RING + 1)
                d.tensor_tensor(slot(lo, s, i, c), slot(raw, s, i, c), slot(hi, s, i, c).bitcast(F32),
                                ALU.subtract).then_inc(lo_ready, 1)

            def move_out(s, i, q):
                m = (s.panel0 + i) % 2
                if s.name in GATES:
                    g = gate_index[s.name, i]
                    dst = gate_dst(s, i)
                    for t in range(TT):
                        dve.wait_ge(tanh_ready, TT * g + t + 1)
                        d.scalar_tensor_tensor(dst[:, t, :], th[t][:, :], 1.0, acc[m][t][:, :], ALU.add,
                                               ALU.mult).then_inc(acc_free[m], 1)
                elif s.name.startswith("out"):
                    dve.wait_ge(chunk_used, chunk_no(s, i, s.kc - 1, q) + 1)
                    if s.name[3] == "2":
                        wait_evac(dve, s.name.replace("2", "1"), i)
                    for t in range(TT):
                        x = xres[:, t, i * PW:(i + 1) * PW]
                        d.tensor_tensor(x, acc[m][t][:, :], x, ALU.add).then_inc(acc_free[m], 1)

            def step_t(stage, j):
                r, at = region_of(stage), slot_of(stage, j)
                dve.wait_ge(t_hi_ready, T_INDEX[stage, j] + 1)
                d.scalar_tensor_tensor(act_lo[r][:, at, :], tp("T", stage, j)[:, 0:SEQ], gain_of(stage, j),
                                       act_hi[r][:, at, :].bitcast(F32), ALU.mult,
                                       ALU.subtract).then_inc(tp_free[TP["T", stage, j] % 2], 1)

            def step_s(stage, j):
                r, src = int(stage == "mem_o"), x_t if stage == "x_e" else mem_t
                dve.wait_ge(staged_hi, S_INDEX[stage, j] + 1)
                d.scalar_tensor_tensor(act_lo[r][:, j, :], src[:, j, :], gain_of(stage, j),
                                       act_hi[r][:, j, :].bitcast(F32), ALU.mult,
                                       ALU.subtract).then_inc(staged_lo, 1)

            def step_mk(layer, i):
                u = TP["mk", layer, i]
                dve.wait_ge(tp_ready, u + 1)
                d.tensor_copy(mkt[layer][:, 2 * i:2 * i + 2, :].rearrange("p h m -> p (h m)"),
                              tp("mk", layer, i)[:, :]).then_inc(tp_free[u % 2], 1)

            def step_kr():
                u = TP["kr",]
                dve.wait_ge(tp_ready, u + 1)
                d.tensor_copy(k_rot_t[:, :, :].rearrange("p z m -> p (z m)"),
                              tp("kr")[:, :]).then_inc(tp_free[u % 2], 1)

            def step_ff():
                u = TP["ffT",]
                dve.wait_ge(tp_ready, u + 1)
                d.tensor_scalar(fz[:, :], tp("ffT")[0:FOX_H, 0:SEQ], fbias[:, 0:1], None,
                                ALU.add).then_inc(tp_free[u % 2], 1)
                dve.wait_ge(tp_free[u % 2], u // 2 + 1)
                d.scalar_tensor_tensor(fa[:, :], fz[:, :], -1.0, fz[:, :], ALU.mult,
                                       ALU.max).then_inc(fox_abs_ready, 1)
                dve.wait_ge(fox_exp_ready, 1)
                link(d.tensor_scalar(fa[:, :], fs[:, :], 2.0, None, ALU.add))
                link(d.reciprocal(fa[:, :], fa[:, :]))
                link(d.tensor_tensor(fs[:, :], fs[:, :], fa[:, :], ALU.mult))
                link(d.tensor_tensor(fa[:, :], fs[:, :], fs[:, :], ALU.mult))
                link(d.tensor_scalar(fp[:, :], fa[:, :], 1.0 / 17, None, ALU.mult))
                for odd in range(15, 1, -2):
                    link(d.scalar_tensor_tensor(fp[:, :], fp[:, :], 1.0 / odd, fa[:, :], ALU.add, ALU.mult))
                link(d.scalar_tensor_tensor(fp[:, :], fp[:, :], 1.0, fs[:, :], ALU.add, ALU.mult))
                link(d.tensor_scalar(fz[:, :], fz[:, :], 0.0, None, ALU.min))
                link(d.scalar_tensor_tensor(fz[:, :], fp[:, :], -2.0, fz[:, :], ALU.mult, ALU.add))
                link(d.memset(fa[:, :], 1.0))
                link(d.tensor_tensor_scan(fp[:, :], fa[:, :], fz[:, :], 0.0, ALU.mult, ALU.add))
                dve.wait_ge(masks_ready, 1)
                link(d.tensor_copy(c_pos[:, :], c_zero[:, :]))
                link(d.tensor_copy(c_pos[0:FOX_H, :], fp[:, :]))
                link(d.tensor_tensor(c_pos[32:32 + FOX_H, :], fp[:, :], c_pos[0:FOX_H, :].bitcast(F32),
                                     ALU.subtract))
                link(d.tensor_scalar(c_neg[:, :], c_pos[:, :].bitcast(F32), -1.0, None, ALU.mult))
                d.tensor_copy(ident_b[:, :], ident[:, :])
                d.tensor_copy(sel[:, :], sel_f[:, :]).then_inc(c_ready, 1)

            def step_b(v):
                dve.wait_ge(score_ready, v + 1)
                for t, c, n in spans(v):
                    last = d.tensor_reduce(neg_max[:, v, t:t + 1], sc("B", v)[:, c:c + n], AX.X, ALU.max,
                                           negate=True)
                last.then_inc(max_ready, 1)

            def step_d(v):
                u, n = TP["D", v], len(blocks(v)) * P
                dve.wait_ge(tp_ready, u + 1)
                if v >= depth(v):
                    dve.wait_ge(out_ready, v - depth(v) + 1)
                d.tensor_copy(pt_of(v)[:, 0:n], tp("D", v)[:, 0:n]).then_inc(tp_free[u % 2], 1)

            def step_e(v):
                layer = HEADS[v][2]
                k = NORMS.index("x_o" if layer else "x_e")
                dve.wait_ge(exp_ready, v + 1)
                dve.wait_ge(rms_ready, k + 1)
                link(d.reciprocal(rinv[:, v, :], rsum[:, v, :]))
                link(d.tensor_tensor(rinv[:, v, :], rinv[:, v, :], rms[:, k, :], ALU.mult))
                dve.wait_ge(out_ready, v + 1)
                c = mix_col(v)
                for t in range(TT):
                    g = gate[layer][:, t, c:c + HD]
                    last = d.scalar_tensor_tensor(g, sc("B", v)[:, t * P:(t + 1) * P], rinv[:, v, t:t + 1], g,
                                                  ALU.mult, ALU.mult)
                last.then_inc(sc_free[SC["B", v] % 2], 1)

            def step_ga_t():
                u = TP["gaT",]
                dve.wait_ge(tp_ready, u + 1)
                d.tensor_copy(ga_t[:, :], tp("gaT")[0:GRANK, 0:SEQ]).then_inc(tp_free[u % 2], 1)
                link(d.memset(reset[:, :], 1.0))
                link(d.memset(reset[:, :].rearrange("p (c k) -> p c k", k=CHUNK)[:, :, 0:1], 0.0))
                link(d.memset(g_att[CHUNK:P, :, 0:CHUNK], 0.0))

            def step_gz(h):
                dve.wait_ge(gla_log_ready, h + 1)
                link(d.scalar_tensor_tensor(g_z[:, :], g_z[:, :], 0.0, g_a[:, :], ALU.min, ALU.subtract))
                d.tensor_tensor_scan(g_cum[:, :], reset[:, :], g_z[:, :], 0.0, ALU.mult,
                                     ALU.add).then_inc(gla_cum_ready, 1)
                dve.wait_ge(gla_cum_ready, h + 1)
                cum = g_cum[:, :].rearrange("p (c k) -> p c k", k=CHUNK)
                d.tensor_tensor(g_a[:, :].rearrange("p (c k) -> p c k", k=CHUNK),
                                cum[:, :, CHUNK - 1:CHUNK].to_broadcast([P, 2 * SEQ // CHUNK, CHUNK]), cum,
                                ALU.subtract).then_inc(gla_end_ready, 1)

            def decay_of(kk, c):
                at = kk * SEQ + (c + 1) * CHUNK - 1
                return g_ep[:, at:at + 1]

            def step_gq(h):
                u = TP["Gq", h]
                dve.wait_ge(tp_ready, u + 1)
                dve.wait_ge(gla_exp_ready, h + 1)
                d.scalar_tensor_tensor(g_qd[:, :], tp("Gq", h)[:, :], float(GLA_DK ** -0.5), g_ep[:, :],
                                       ALU.mult, ALU.mult).then_inc(tp_free[u % 2], 1)
                dve.wait_ge(tp_free[u % 2], u // 2 + 1)
                qd = g_qd[:, :].rearrange("p (k c n) -> p k c n", k=2, n=CHUNK)
                qs = g_qs[:, :].rearrange("p (k c n) -> p k c n", k=2, n=CHUNK)
                d.tensor_copy(qs[:, :, 0, :], qd[:, :, 2, :])
                for kk in range(2):
                    last = d.tensor_scalar(qs[:, kk, 1, :], qd[:, kk, 3, :], decay_of(kk, 2), None, ALU.mult)
                last.then_inc(gla_q_ready, 1)

            def step_gk(h):
                u = TP["Gk", h]
                dve.wait_ge(tp_ready, u + 1)
                dve.wait_ge(gla_decay_ready, h + 1)
                link(d.tensor_tensor(g_a[:, :], tp("Gk", h)[:, :], g_a[:, :], ALU.mult))
                ke = g_a[:, :].rearrange("p (k c n) -> p k c n", k=2, n=CHUNK)
                kt = g_ke_t[:, :].rearrange("p (k c n) -> p k c n", k=2, n=CHUNK)
                d.tensor_copy(kt[:, :, 1, :], ke[:, :, 1, :])
                for kk in range(2):
                    last = d.tensor_scalar(kt[:, kk, 0, :], ke[:, kk, 0, :], decay_of(kk, 1), None, ALU.mult)
                last.then_inc(gla_ops_ready, 1)
                d.tensor_tensor(g_en[:, :], tp("Gk", h)[:, :], g_en[:, :], ALU.mult).then_inc(tp_free[u % 2], 1)

            def step_ga(h):
                b = sc("Ga", h)[:, 0:TT * P].rearrange("p (t n) -> p t n", t=TT)
                dve.wait_ge(gla_att_ready, h + 1)
                for r in (0, CHUNK):
                    rows, cols = slice(r, r + CHUNK), slice(r, r + CHUNK)
                    d.tensor_tensor(g_att[rows, :, cols], b[rows, :, cols],
                                    gla_mask[rows, :].unsqueeze(1).to_broadcast([CHUNK, TT, CHUNK]), ALU.mult)
                d.tensor_copy(g_att[0:CHUNK, :, CHUNK:P], b[0:CHUNK, :, CHUNK:P]).then_inc(sc_free[SC["Ga", h] % 2], 1)

            def step_state(h):
                for kk in range(2):
                    u = TP["Gs", h, kk]
                    dve.wait_ge(tp_ready, u + 1)
                    d.tensor_copy(g_st[:, kk, :], tp("Gs", h, kk)[:, :]).then_inc(tp_free[u % 2], 1)

            def step_go(h, t):
                i = TT * h + t
                k = NORMS.index("gla0") + i
                dve.wait_ge(rms_ready, k + 1)
                g = gate[1][:, t, h * GLA_DV:(h + 1) * GLA_DV]
                d.scalar_tensor_tensor(g, sc("Go", h, t)[:, :], rms[:, k, 0:1], g, ALU.mult,
                                       ALU.mult).then_inc(sc_free[SC["Go", h, t] % 2], 1)

            def step_g0(h):
                step_state(h)
                step_go(h, 0)

            steps = {"T": step_t, "S": step_s, "mk": step_mk, "kr": step_kr, "ffT": step_ff, "B": step_b, "D": step_d,
                     "E": step_e, "gaT": step_ga_t, "Gz": step_gz, "Gq": step_gq, "Gk": step_gk, "Ga": step_ga,
                     "G0": step_g0, "G1": lambda h: step_go(h, 1)}

            def side_work(n, q):
                if n in PANEL_OF:
                    move_out(*PANEL_OF[n], q)
                if q is None:
                    for step, arg in AFTER.get(n, ()):
                        if step in steps:
                            steps[step](*arg)

            for step, arg in BEFORE:
                if step in steps:
                    steps[step](*arg)
            run_streams(dve, split_lo, side_work, LAG)
            k = len(NORMS) - 1
            dve.wait_ge(rms_ready, k + 1)
            dve.wait_ge(row_in, 16)
            for t in range(TT):
                d.scalar_tensor_tensor(y[:, t, :], xres[:, t, :], rms[:, k, t:t + 1], gain_row[:, :], ALU.mult,
                                       ALU.mult).then_inc(final_ready, 1)

        @block.tensor
        def _(pe):
            mm = nc.tensor.matmul
            pe.wait_ge(consts_ready, 1)

            def tr(dst, src):
                return nc.tensor.transpose(dst, src, ident[:, :])

            def take_tp(*key):
                u = TP[key]
                if u >= 2:
                    pe.wait_ge(tp_free[u % 2], u // 2)
                return tp(*key)

            def take_sc(*key):
                u = SC[key]
                if u >= 2:
                    pe.wait_ge(sc_free[u % 2], u // 2)
                return sc(*key)

            def project(s, i, c, q):
                w = s.cols[i][1]
                m = s.panel0 + i
                if c == 0 and m >= 2:
                    pe.wait_ge(acc_free[m % 2], lin(2 * (m // 2), 2, q))
                if i == 0 and s.ready and q is None:
                    for key in s.ready(c):
                        if key in S_INDEX:
                            pe.wait_ge(staged_lo, S_INDEX[key] + 1)
                        else:
                            wait_tp_free(pe, "T", *key)
                pe.wait_ge(lo_ready, chunk_no(s, i, c, q) + 1)
                for j in range(s.per):
                    k = s.slots[c] + j
                    first, end = (c == 0 and j == 0), (c == s.kc - 1 and j == s.per - 1)
                    wh, wl = slot(hi, s, i, c)[:, j, :], slot(lo, s, i, c)[:, j, :]
                    for t in range(TT):
                        xh = act_hi[s.act][:, k, t * P:(t + 1) * P]
                        xl = act_lo[s.act][:, k, t * P:(t + 1) * P]
                        o = acc[m % 2][t][:, 0:w]
                        mm(o, xh, wh, start=first, stop=False)
                        mm(o, xh, wl, start=False, stop=False)
                        last = mm(o, xl, wh, start=False, stop=end)
                last.then_inc(chunk_used, 1)

            def step_t(stage, j):
                b = take_tp("T", stage, j)
                if stage == "x_o":
                    pe_wait_resid(j)
                if stage in ("cq", "ckv"):
                    wait_evac(pe, stage)
                if stage == "mix_e":
                    v = (j if j < FOX_H else V_MLA + j - FOX_H if j < 16 else V_MEM0 + j - 16)
                    pe.wait_ge(sc_free[SC["B", v] % 2], SC["B", v] // 2 + 1)
                if stage == "mix_o" and j < 16:
                    for t in range(TT):
                        u = SC["Go", j // 4, t]
                        pe.wait_ge(sc_free[u % 2], u // 2 + 1)
                if stage == "mix_o" and j >= 16:
                    u = SC["B", V_MEM1 + j - 16]
                    pe.wait_ge(sc_free[u % 2], u // 2 + 1)
                for t in range(TT):
                    last = tr(b[:, t * P:(t + 1) * P], source(stage, j, t))
                last.then_inc(tp_ready, 1)

            def pe_wait_resid(j):
                wait_evac(pe, "out2_e", j // 4)

            def step_mk(layer, i):
                b = take_tp("mk", layer, i)
                wait_evac(pe, "mem_o" if layer else "mem_e", 0)
                for h in range(2):
                    for t in range(TT):
                        c = (2 * i + h) * HD
                        last = tr(b[:, h * SEQ + t * P:h * SEQ + (t + 1) * P], mk[layer][:, t, c:c + HD])
                last.then_inc(tp_ready, 1)

            def step_ff():
                b = take_tp("ffT")
                wait_evac(pe, "ff")
                for t in range(TT):
                    last = tr(b[0:FOX_H, t * P:(t + 1) * P], ff[:, t, :])
                last.then_inc(tp_ready, 1)

            def step_kr():
                b = take_tp("kr")
                pe.wait_ge(rope_k_ready, 1)
                for z in range(2):
                    for t in range(TT):
                        last = tr(b[:, z * SEQ + t * P:z * SEQ + (t + 1) * P],
                                  k_rot[:, t, z, :, :].rearrange("p z d -> p (z d)"))
                last.then_inc(tp_ready, 1)

            def step_a(v):
                kind, h, layer = HEADS[v]
                b = take_tp("A", v)
                if kind == "fox":
                    wait_evac(pe, "fox")
                    q, k = (proj, h * HD), (proj, FOXW + h * HD)
                elif kind == "mla":
                    wait_evac(pe, "ukv")
                    wait_evac(pe, "ukv", 2)
                    q, k = (proj, h * MLA_Q), (proj, MLA_H * MLA_Q + h * MLA_KV)
                else:
                    wait_evac(pe, "mq_o" if layer else "mq_e")
                    q, k = (mq, h * HD), None
                for t in range(TT):
                    last = tr(b[:, t * P:(t + 1) * P], q[0][:, t, q[1]:q[1] + HD])
                if k:
                    for t in range(TT):
                        last = tr(b[:, SEQ + t * P:SEQ + (t + 1) * P], k[0][:, t, k[1]:k[1] + HD])
                last.then_inc(tp_ready, 1)
                if ("Ar", v) in TP:
                    b = take_tp("Ar", v)
                    pe.wait_ge(rope_q_ready, 1)
                    for t in range(TT):
                        last = tr(b[:, t * P:(t + 1) * P], q_rot[:, t, h // 2 * P:(h // 2 + 1) * P])
                    last.then_inc(tp_ready, 1)

            def step_b(v):
                kind, h, layer = HEADS[v]
                b = take_sc("B", v)
                wait_tp_free(pe, "A", v)
                qk = qk_of(v)
                if kind == "fox":
                    pe.wait_ge(c_ready, 1)
                if kind == "mla":
                    wait_tp_free(pe, "Ar", v - h % 2)
                    wait_tp_free(pe, "kr")
                for t, c, n in spans(v):
                    o, q = b[:, c:c + n], qk[:, t * P:(t + 1) * P]
                    if kind == "mem":
                        last = mm(o, q, mkt[layer][:, h, :], start=True, stop=True)
                        continue
                    mm(o, q, qk[:, SEQ:SEQ + n], start=True, stop=False)
                    mm(b[:, c + n - P:c + n], ident_b[:, :], (fox_mask if kind == "fox" else mla_mask)[:, :],
                       start=False, stop=False)
                    if kind == "fox":
                        one = sel[:, h:h + 1]
                        mm(o, c_pos[:, t * P:(t + 1) * P], one.to_broadcast([P, n]), start=False, stop=False)
                        last = mm(o, one.to_broadcast([P, P]), c_neg[:, 0:n], start=False, stop=True)
                    else:
                        last = mm(o, q_rot_t[h // 2 % 2][:, t * P:(t + 1) * P], k_rot_t[:, h % 2, 0:n],
                                  start=False, stop=True)
                last.then_inc(score_ready, 1)

            def step_d(v):
                b = take_tp("D", v)
                pe.wait_ge(exp_ready, v + 1)
                for i in range(len(blocks(v))):
                    last = tr(b[:, i * P:(i + 1) * P], p_of(v)[:, i * P:(i + 1) * P])
                last.then_inc(tp_ready, 1)

            def step_e(v):
                wait_tp_free(pe, "D", v)
                b, bl = sc("B", v), blocks(v)
                for i, (t, k) in enumerate(bl):
                    last = mm(b[:, t * P:(t + 1) * P], pt_of(v)[:, i * P:(i + 1) * P], values(v, k),
                              start=(k == 0), stop=(i + 1 == len(bl) or bl[i + 1][0] != t))
                last.then_inc(out_ready, 1)

            def step_ga_t():
                b = take_tp("gaT")
                wait_evac(pe, "ga")
                for t in range(TT):
                    last = tr(b[0:GRANK, t * P:(t + 1) * P], ga[:, t, :])
                last.then_inc(tp_ready, 1)

            def step_gz(h):
                b = take_tp("Gz", h)
                wait_tp_free(pe, "gaT")
                pe.wait_ge(wa2_in, 16)
                for kk in range(2):
                    c = h * GLA_DK + kk * P
                    last = mm(b[:, kk * SEQ:(kk + 1) * SEQ], wa2[:, c:c + P], ga_t[:, :], start=True, stop=True)
                last.then_inc(tp_ready, 1)

            def step_gqk(step, h, base):
                b = take_tp(step, h)
                wait_evac(pe, "gqkv")
                wait_evac(pe, "gqkv", 6)
                for kk in range(2):
                    for t in range(TT):
                        c = base + h * GLA_DK + kk * P
                        last = tr(b[:, kk * SEQ + t * P:kk * SEQ + (t + 1) * P], proj[:, t, c:c + P])
                last.then_inc(tp_ready, 1)

            def step_ge(h):
                b = take_tp("Ge", h)
                pe.wait_ge(gla_ops_ready, h + 1)
                for kk in range(2):
                    last = tr(b[:, kk * P:(kk + 1) * P], g_ke_t[:, kk * P:(kk + 1) * P])
                last.then_inc(tp_ready, 1)

            def step_ga(h):
                b = take_sc("Ga", h)
                wait_tp_free(pe, "Gq", h)
                wait_tp_free(pe, "Gk", h)
                for t in range(TT):
                    for keys, r, n in ((g_en, 0, 0), (g_a, 0, CHUNK), (g_en, CHUNK, CHUNK)):
                        for kk in range(2):
                            at = kk * SEQ + t * P
                            last = mm(b[r:r + CHUNK, t * P + n:t * P + n + CHUNK],
                                      keys[:, at + r:at + r + CHUNK], g_qd[:, at + n:at + n + CHUNK],
                                      start=(kk == 0), stop=(kk == 1))
                last.then_inc(gla_att_ready, 1)

            def step_g0(h):
                at = 2 * GLA_H * GLA_DK + h * GLA_DV
                b = take_sc("Go", h, 0)
                pe.wait_ge(sc_free[SC["Ga", h] % 2], SC["Ga", h] // 2 + 1)
                mm(b[:, :], g_att[:, 0, :], proj[:, 0, at:at + GLA_DV], start=True,
                   stop=True).then_inc(gla_out_ready, 1)
                wait_tp_free(pe, "Ge", h)
                for kk in range(2):
                    s = take_tp("Gs", h, kk)
                    mm(s[:, :], g_ke[:, kk * P:(kk + 1) * P], proj[:, 0, at:at + GLA_DV], start=True,
                       stop=True).then_inc(tp_ready, 1)

            def step_g1(h):
                at = 2 * GLA_H * GLA_DK + h * GLA_DV
                b = take_sc("Go", h, 1)
                mm(b[:, :], g_att[:, 1, :], proj[:, 1, at:at + GLA_DV], start=True, stop=False)
                pe.wait_ge(gla_q_ready, h + 1)
                for kk in range(2):
                    wait_tp_free(pe, "Gs", h, kk)
                    last = mm(b[:, :], g_qs[:, kk * P:(kk + 1) * P], g_st[:, kk, :], start=False,
                              stop=(kk == 1))
                last.then_inc(gla_out_ready, 1)

            steps = {"T": step_t, "mk": step_mk, "ffT": step_ff, "kr": step_kr, "A": step_a, "B": step_b,
                     "D": step_d, "E": step_e, "gaT": step_ga_t, "Gz": step_gz,
                     "Gq": lambda h: step_gqk("Gq", h, 0),
                     "Gk": lambda h: step_gqk("Gk", h, GLA_H * GLA_DK), "Ge": step_ge, "Ga": step_ga,
                     "G0": step_g0, "G1": step_g1}

            def side_work(n, q):
                if q is None:
                    for step, arg in AFTER.get(n, ()):
                        if step in steps:
                            steps[step](*arg)

            for step, arg in BEFORE:
                if step in steps:
                    steps[step](*arg)
            run_streams(pe, project, side_work, 0)


WEIGHTS = ["x", "mem", "e_w_in", "e_fox_b_f", "e_mla_w_uq", "e_mla_w_ukv", "e_w_mem_kv", "e_w_out",
           "o_w_in", "o_gla_w_a2", "o_w_mem_kv", "o_w_out", "final_norm_w"]


def kernel(**inputs):
    import concourse.bacc as bacc
    from concourse.bass_utils import run_bass_kernel_spmd

    arrays = {name: np.ascontiguousarray(inputs[name]) for name in WEIGHTS}

    def columns(name):
        return np.asarray(inputs[name])[0].reshape(-1, P).T

    arrays["gains"] = np.ascontiguousarray(np.concatenate([columns(n) for n in (
        "e_norm_w", "o_norm_w", "e_mem_norm_w", "o_mem_norm_w", "e_mla_q_norm_w", "e_mla_kv_norm_w",
        "o_gla_norm_w", "o_gla_b_a")], axis=1))
    arrays["pos"] = np.ascontiguousarray(np.asarray(inputs["positions"]).reshape(TT, P).T)
    arrays["x_t"] = np.ascontiguousarray(arrays["x"][0].T)
    arrays["mem_t"] = np.ascontiguousarray(arrays["mem"][0].T)

    def narrow(w, c, n):
        return np.ascontiguousarray(w[0][:, c:c + n].reshape(D // P, P, n).transpose(1, 0, 2))

    arrays["e_ff_w"] = narrow(arrays["e_w_in"], E_FF, FOX_H)
    arrays["o_ga_w"] = narrow(arrays["o_w_in"], O_GA, GRANK)
    f = np.float32(1.0) / (np.float32(10000.0) ** (np.arange(0, ROPE, 2, dtype=np.float32) / np.float32(ROPE)))
    arrays["freq"] = np.ascontiguousarray(np.broadcast_to(f.astype(np.float32), (P, ROPE // 2)))

    nc = bacc.Bacc("TRN2", target_bir_lowering=False, num_devices=1)
    t_in = {name: nc.dram_tensor(f"in_{name}", a.shape, mybir.dt.from_np(a.dtype), kind="ExternalInput").ap()
            for name, a in arrays.items()}
    out = nc.dram_tensor("out_0", (1, SEQ, D), F32, kind="ExternalOutput").ap()
    build(nc, t_in, out)
    r = run_bass_kernel_spmd(nc, [{f"in_{name}": a for name, a in arrays.items()}], core_ids=[0])
    return r.results[0]["out_0"]
```

```python
from contextlib import ExitStack

import numpy as np
import concourse.bass as bass
from concourse import mybir

F32 = mybir.dt.float32
F32R = mybir.dt.float32r
BF16 = mybir.dt.bfloat16
I32 = mybir.dt.int32
ALU = mybir.AluOpType
ACT = mybir.ActivationFunctionType
AX = mybir.AxisListType

P = 128
D = 2048
SEQ = 256
TT = SEQ // P
EPS = 1e-6
NEG = -1e30
FOX_H, MLA_H, MEM_H, GLA_H = 8, 8, 4, 4
HD = 128
ROPE = 64
QRANK, KVRANK = 512, 256
MLA_Q, MLA_KV = HD + ROPE, 2 * HD
GLA_DK, GLA_DV = 256, 512
GRANK = 16
TAU = 16.0
CHUNK = 64
MEMW = MEM_H * HD
FOXW = FOX_H * HD
MIX = 2560
MIX_KT = MIX // P
CKVW = KVRANK + ROPE + FOX_H
MQGA = MEMW + GRANK

MEM_T_CUT = (0, 2, 4, 8, 12, 16)
RING = 4
LAG = 4
PW = 512

E_FF = 3 * FOXW
E_FG = E_FF + FOX_H
E_CQ = E_FG + FOXW
E_CKV = E_CQ + QRANK
E_MG = E_CKV + KVRANK + ROPE
E_MQ = E_MG + MLA_H * HD
E_MEMG = E_MQ + MEMW
O_GA = 2 * GLA_H * GLA_DK + GLA_H * GLA_DV
O_GG = O_GA + GRANK
O_MQ = O_GG + GLA_H * GLA_DV
O_MEMG = O_MQ + MEMW

G_E, G_O, G_EM, G_OM, G_CQ, G_CKV, G_GLA, G_BA = 0, 16, 32, 48, 64, 68, 70, 74
G_COLS = 82

KR_AT = 3 * FOXW + QRANK + KVRANK
FF_AT = KR_AT + ROPE
KR_SCRATCH = FF_AT + FOX_H

MIX_FOX, MIX_MLA, MIX_MEM = 0, FOXW, 2 * FOXW


LAST = D // PW - 1


class Stream:

    def __init__(self, name, w, ktiles, slots, cols, act, ready=None):
        self.name, self.w, self.ktiles, self.slots, self.cols = name, w, ktiles, slots, cols
        self.act, self.ready = act, ready
        self.kc = len(ktiles)
        self.n = len(cols)


def plan_streams():
    full = [2 * c for c in range(8)]
    pan = lambda c0, n: [(c0 + PW * i, PW) for i in range(n)]

    def tr(stage, js):
        return lambda c: [(stage, js[c]), (stage, js[c] + 1)]

    out1 = [0, 2, 4, 6, 16, 18]
    out2 = [8, 10, 12, 14]
    first_o = [16, 18, 0, 2, 4, 6, 8, 10]
    s = [
        Stream("mem_e", "e_w_mem_kv", full, full, pan(0, 2), 0, tr("mem_e", full)),
        Stream("mem_o", "o_w_mem_kv", full, full, pan(0, 2), 1, tr("mem_o", full)),
        Stream("fox", "e_w_in", full, full, pan(0, 6), 0, tr("x_e", full)),
        Stream("fg", "e_w_in", full, full, pan(E_FG, 2), 0),
        Stream("ckv", "e_ckv_ff", full, full, [(0, CKVW)], 0),
        Stream("cq", "e_w_in", full, full, pan(E_CQ, 1), 0),
        Stream("mq_e", "e_w_in", full, full, pan(E_MQ, 1), 0),
        Stream("memg_e", "e_w_in", full, full, pan(E_MEMG, 1), 0),
        Stream("mg", "e_w_in", full, full, pan(E_MG, 2), 0),
        Stream("uq", "e_mla_w_uq", [0, 2], [16, 18], pan(0, 3), 0, tr("cq", [0, 2])),
        Stream("ukv", "e_mla_w_ukv", [0], [12], pan(0, 4), 0, tr("ckv", [0])),
        Stream("out1_e", "e_w_out", out1, out1, pan(0, 4), 0, tr("mix_e", out1)),
        Stream("out2_e", "e_w_out", out2, out2, pan(0, 4), 0, tr("mix_e", out2)),
        Stream("mq_o", "o_mq_ga", full, full, [(0, MQGA // 2), (MQGA // 2, MQGA // 2)], 1, tr("x_o", full)),
        Stream("memg_o", "o_w_in", full, full, pan(O_MEMG, 1), 1),
        Stream("gqkv", "o_w_in", full, full, pan(0, 8), 1),
        Stream("gg", "o_w_in", full, full, pan(O_GG, 4), 1),
        Stream("out1_o", "o_w_out", first_o, first_o, pan(0, 4), 1, tr("mix_o", first_o)),
        Stream("out2_o", "o_w_out", [12, 14], [12, 14], pan(0, 4), 1, tr("mix_o", [12, 14])),
    ]
    chunk = panel = 0
    for x in s:
        x.chunk0, x.panel0 = chunk, panel
        chunk += x.kc * x.n
        panel += x.n
    return s


STREAMS = plan_streams()
AT = {s.name: s for s in STREAMS}
CHUNKS = STREAMS[-1].chunk0 + STREAMS[-1].kc * STREAMS[-1].n
GATES = ("fg", "memg_e", "mg", "gg", "memg_o")

HEADS = ([("fox", h, 0) for h in range(FOX_H)] + [("mem", h, 0) for h in range(MEM_H)]
         + [("mla", h, 0) for h in range(MLA_H)] + [("mem", h, 1) for h in range(MEM_H)])
V_MEM0, V_MLA, V_MEM1 = FOX_H, FOX_H + MEM_H, FOX_H + MEM_H + MLA_H
NH = len(HEADS)
NORMS = ["mem", "x_e", "ckv", "cq", "x_o"] + [f"gla{i}" for i in range(GLA_H * TT)] + ["final"]


def plan_schedule():
    at = []

    def put(n, step, *arg):
        at.append((n, len(at), step, arg))

    def transposes(stage, js, first, per=2):
        for i, j in enumerate(js):
            put(first + i // per, "T", stage, j)

    def head(v, n, b=1, d=3, e=4):
        put(n, "A", v)
        put(n + b, "B", v)
        put(n + d, "D", v)
        put(n + e, "E", v)

    for j in range(16):
        put(j // 2 - LAG - (j < 2), "S", "mem_e", j)
        put(7 + j // 2, "S", "mem_o", j)
    for i in range(4):
        put(3 + i, "sq", "mem", i)
    c = AT["mem_o"].chunk0
    for i in range(4):
        put(c + 8 + 2 * i, "sq", "x_e", i)
    for j in range(16):
        put(c + j // 2, "S", "x_e", j)
    for i in range(2):
        put(c + 3 + i, "mk", 0, i)
        put(c + 12 + i, "mk", 1, i)
    put(AT["fg"].chunk0 + 2, "trig")
    c = AT["cq"].chunk0
    for i in range(4):
        put(c + i, "ff", i)
    put(c + 4, "sq", "ckv")
    c = AT["mq_e"].chunk0
    put(c + 1, "sq", "cq")
    transposes("cq", range(4), c + 4)
    head(0, c - 4, b=2, d=4, e=5)
    for v in range(1, FOX_H + MEM_H):
        head(v, c - 3 + 3 * v)
    c = AT["uq"].chunk0
    transposes("ckv", range(2), c)
    put(c + 1, "T", "mix_e", 0)
    transposes("mix_e", range(1, 8), c + 2)
    put(c + 5, "kr")
    transposes("mix_e", range(16, 20), c + 6)
    c = AT["out1_e"].chunk0
    for i in range(MLA_H):
        n = c + 1 + (5 * i + 1) // 2
        head(V_MLA + i, n)
        put(n + 6, "T", "mix_e", FOX_H + i)
    c = AT["out2_e"].chunk0
    for i in range(4):
        last = c + 4 * i + 3
        put(last + (i < 3), "sq", "x_o", i)
        transposes("x_o", range(4 * i, 4 * i + 4), last + 1)
    c = AT["memg_o"].chunk0
    put(c + 1, "gaT")
    for i in range(MEM_H):
        head(V_MEM1 + i, c + 5 + 3 * i)
    c = AT["gg"].chunk0
    transposes("mix_o", range(16, 20), c - 2)
    for h in range(GLA_H):
        n = c + 8 * h
        for i, step in zip((0, 1, 4, 5, 7, 8, 9), ("Gz", "Gd", "Gq", "Gk", "Ga", "G0", "G1")):
            put(n + i, step, h)
    c = AT["out1_o"].chunk0
    transposes("mix_o", range(2), c - 1)
    put(c, "T", "mix_o", 2)
    transposes("mix_o", range(3, 16), c + 1)
    for i in range(LAST):
        put(AT["out2_o"].chunk0 + 2 * i + 1, "y", i)
        put(AT["out2_o"].chunk0 + 2 * i + 1, "sq", "final", i)
    at.sort()
    return [(n, step, arg) for n, _, step, arg in at]


SCHEDULE = plan_schedule()


def plan_banks():
    tp, sc = {}, {}

    def tp_use(*key):
        tp[key] = len(tp)

    def sc_use(*key):
        sc[key] = len(sc)

    for _, step, arg in SCHEDULE:
        if step in ("T", "mk", "kr", "gaT", "Gz", "Gq", "Gk", "D"):
            tp_use(step, *arg)
        elif step == "ff" and arg[0] == 0:
            tp_use("ffT")
        elif step == "A":
            tp_use(step, *arg)
            if HEADS[arg[0]][0] == "mla" and HEADS[arg[0]][1] % 2 == 0:
                tp_use("Ar", *arg)
        elif step == "B":
            sc_use(step, *arg)
        elif step == "Ga":
            sc_use(step, *arg)
        elif step in ("G0", "G1"):
            sc_use("Go", arg[0], int(step[1]))
    return tp, sc


TP, SC = plan_banks()
AFTER = {}
for _n, _step, _arg in SCHEDULE:
    if _n >= -LAG:
        AFTER.setdefault(_n, []).append((_step, _arg))
BEFORE = [(step, arg) for n, step, arg in SCHEDULE if n < -LAG]
PANEL_OF = {s.chunk0 + s.kc * (i + 1) - 1: (s, i) for s in STREAMS for i in range(s.n)}


def lin(a, coef, q):
    return a if q is None else q * coef + a


def looped(s):
    if s.n < 6 or s.kc % 2:
        return 0, 0
    begin = 2 if s.name == "gqkv" else 1
    pairs = (s.n - 1 - begin) // 2
    first = s.chunk0 + begin * s.kc
    assert not [n for n in AFTER if first - LAG <= n < first + pairs * 2 * s.kc], s.name
    return begin, pairs


def build(nc, t_in, out):
    with ExitStack() as ctx:
        KB = 1024
        top = (nc.sbuf_base + 63) // 64 * 64

        def region(nbytes):
            nonlocal top
            at = top
            top += (nbytes + 63) // 64 * 64
            return at

        def place(name, shape, dt=F32, at=None):
            if at is None:
                at = region(int(np.prod(shape[1:])) * (2 if dt == BF16 else 4))
            return nc.alloc_sbuf_tensor_at(name, shape, dt, offset=at)

        xres = place("xres", [P, TT, D])
        raw = place("raw", [P, RING, 2 * PW])
        hi = place("hi", [P, RING, 2 * PW], F32R)
        lo = place("lo", [P, RING, 2 * PW], F32R)
        region_1, region_2 = region(40 * KB), region(40 * KB)
        act_hi = [place(f"act_hi{i}", [P, MIX_KT, SEQ], F32R, r) for i, r in enumerate((region_1, region_2))]
        act_lo = [place(f"act_lo{i}", [P, MIX_KT, SEQ], F32R, r + 20 * KB)
                  for i, r in enumerate((region_1, region_2))]
        gate = [place("gate0", [P, TT, MIX], F32, region_2), place("gate1", [P, TT, MIX], F32, region_1)]
        s0, s1 = region_2 + 20 * KB, region_1 + 20 * KB
        qk0 = [place(f"qk0_{i}", [P, 2 * SEQ], F32, s0 + 2 * KB * i) for i in range(2)]
        p0 = [place(f"p0_{i}", [P, 2 * SEQ], F32, s0 + (4 + 2 * i) * KB) for i in range(2)]
        pt0 = [place(f"pt0_{i}", [P, 2 * SEQ], F32, s0 + (8 + 2 * i) * KB) for i in range(2)]
        q_rot = place("q_rot", [P, TT, MLA_H * ROPE], F32, s0 + 12 * KB)
        k_rot = place("k_rot", [P, TT, 2, 2, ROPE], F32, s0 + 16 * KB)
        k_rot_t = place("k_rot_t", [P, 2, SEQ], F32, s0 + 18 * KB)
        c_at = region(2 * KB)
        g_z = place("g_z", [P, 2 * SEQ], F32, s1)
        g_a = place("g_a", [P, 2 * SEQ], F32, s1 + 2 * KB)
        g_cum = place("g_cum", [P, 2 * SEQ], F32, s1 + 4 * KB)
        g_ep = place("g_ep", [P, 2 * SEQ], F32, s1 + 6 * KB)
        g_en = place("g_en", [P, 2 * SEQ], F32, s1 + 8 * KB)
        g_qd = place("g_qd", [P, 2 * SEQ], F32, s1 + 10 * KB)
        g_ke_t = place("g_ke_t", [P, 2 * P], F32, s1 + 13 * KB)
        g_qs = place("g_qs", [P, 2 * P], F32, c_at)
        g_att = place("g_att", [P, 3, P], F32, s1 + 14 * KB)
        proj_at = region(32 * KB)
        proj = place("proj", [P, TT, 4096], F32, proj_at)
        mem_t = place("mem_t", [P, D // P, SEQ], F32, proj_at)
        mem_rows = place("mem_rows", [P, TT, D], F32, proj_at + 16 * KB)
        x_t = place("x_t", [P, D // P, SEQ], F32, proj_at + 16 * KB)
        mk = [place(f"mk{i}", [P, TT, MEMW], F32, region_1 + (16 + 20 * i) * KB) for i in range(2)]
        gain_row = place("gain_row", [P, D], F32, proj_at)
        y = place("y", [P, TT, D], F32, proj_at + 8 * KB)
        mk_at, mv_at = [region(4 * KB) for _ in range(2)], [region(4 * KB) for _ in range(2)]
        mkt = [place(f"mkt{i}", [P, MEM_H, SEQ], F32, mk_at[i]) for i in range(2)]
        mv = [place(f"mv{i}", [P, TT, MEMW], F32, mv_at[i]) for i in range(2)]
        wa2 = place("wa2", [GRANK, GLA_H * GLA_DK], F32, mk_at[0])
        p1 = place("p1", [P, 2 * SEQ], F32, mv_at[0])
        pt1 = place("pt1", [P, 2 * SEQ], F32, mv_at[0] + 2 * KB)
        mq = place("mq", [P, TT, MQGA])
        th_at = region(4 * KB)
        th = [place(f"tanh{i}", [P, PW], F32, th_at + 2 * KB * i) for i in range(TT)]
        c_pos = place("c_pos", [P, SEQ], F32R, c_at)
        c_neg = place("c_neg", [P, SEQ], F32R, c_at + KB)
        q_rot_t = [place(f"q_rot_t{i}", [P, SEQ], F32, c_at + KB * i) for i in range(2)]
        qk1 = [place(f"qk1_{i}", [P, SEQ], F32, c_at + KB * i) for i in range(2)]
        junk = place("junk", [P, PW], BF16)
        ident = place("ident", [P, P])
        layer_0_at = region(KB)
        ident_b = place("ident_b", [P, P], BF16, layer_0_at)
        fox_mask = place("fox_mask", [P, P], BF16, layer_0_at + KB // 4)
        mla_mask = place("mla_mask", [P, P], BF16, layer_0_at + KB // 2)
        cos = place("cos", [P, TT, ROPE // 2], F32, layer_0_at + 3 * KB // 4)
        gla_mask = place("gla_mask", [P, CHUNK])
        gains = place("gains", [P, G_COLS])
        half_gla = place("half_gla", [P, GLA_DV // P])
        sel_f = place("sel_f", [P, FOX_H])
        sel = place("sel", [P, FOX_H], F32R)
        fbias = place("fbias", [FOX_H, 1])
        sin = place("sin", [P, TT, ROPE // 2])
        freq = place("freq", [P, ROPE // 2])
        pos_i = place("pos_i", [P, TT], I32)
        pos_f = place("pos_f", [P, TT])
        ssq = place("ssq", [P, len(NORMS), TT, 4])
        rms = place("rms", [P, len(NORMS), TT])
        rms_half = place("rms_half", [P, len(NORMS), TT])
        ntmp = place("ntmp", [P, TT, 4])
        mean = place("mean", [P, TT])
        mhalf = place("mhalf", [P, TT])
        half_pi = place("half_pi", [P, 1])
        ones = place("ones", [P, 1])
        neg_max = place("neg_max", [P, NH, TT])
        rsum = place("rsum", [P, NH, TT])
        rinv = place("rinv", [P, NH, TT])
        fz, fa, fs, fp = (place(f"fox_{n}", [FOX_H, SEQ], F32, s0 + 12 * KB + KB * i) for i, n in enumerate("zasp"))
        t_ang, t_n = (place(f"trig_{n}", [P, TT, ROPE // 2], F32, s0 + 18 * KB + KB * i)
                      for i, n in enumerate("an"))
        rope_a, rope_b = (place(f"rope_{n}", [P, MLA_H, ROPE // 2], F32, proj_at + 14 * KB + KB * i)
                          for i, n in enumerate("ab"))
        kr_a, kr_b = (place(f"kr_{n}", [P, ROPE // 2], F32, proj_at + (4096 + KR_SCRATCH + 64 * i) * 4)
                      for i, n in enumerate("ab"))
        c_zero = place("c_zero", [P, SEQ], BF16, c_at + KB)
        ga_t = place("ga_t", [GRANK, SEQ], F32, layer_0_at)
        reset = place("reset", [P, 2 * SEQ], BF16, s1 + 19 * KB)
        assert top <= nc.sbuf_usable_end, (top, nc.sbuf_usable_end)

        bank = [ctx.enter_context(nc.psum_tensor(f"bank{i}", [P, PW], F32)) for i in range(8)]
        acc = [bank[0:2], bank[2:4]]

        def tp(*key):
            return bank[4 + TP[key] % 2]

        def sc(*key):
            return bank[6 + SC[key] % 2]

        def sem(name):
            return ctx.enter_context(nc.semaphore(name))

        gains_in = sem("gains_in")
        small_in, wa2_in, row_in, out_done = map(sem, ("small_in", "wa2_in", "row_in", "out_done"))
        mem_rows_in = [sem(f"mem_rows_in{i}") for i in range(4)]
        x_in = [sem(f"x_in{i}") for i in range(4)]
        mem_t_in = [sem(f"mem_t_in{i}") for i in range(len(MEM_T_CUT) - 1)]
        x_t_in = [sem(f"x_t_in{i}") for i in range(4)]
        staged_hi, staged_lo = sem("staged_hi"), sem("staged_lo")
        raw_in = [sem(f"raw_in{i}") for i in range(RING)]
        hi_ready, lo_ready = sem("hi_ready"), sem("lo_ready")
        chunk_used = sem("chunk_used")
        acc_free = [sem(f"acc_free{i}") for i in range(2)]
        tanh_ready = sem("tanh_ready")
        tp_ready = sem("tp_ready")
        tp_free = [sem(f"tp_free{i}") for i in range(2)]
        t_hi_ready = sem("t_hi_ready")
        score_ready, max_ready, exp_ready, out_ready = map(
            sem, ("score_ready", "max_ready", "exp_ready", "out_ready"))
        sc_free = [sem(f"sc_free{i}") for i in range(2)]
        consts_ready, masks_ready, sel_ready = sem("consts_ready"), sem("masks_ready"), sem("sel_ready")
        sq_ready, rms_ready = sem("sq_ready"), sem("rms_ready")
        angle_ready, trig_ready = sem("angle_ready"), sem("trig_ready")
        rope_k_ready, rope_q_ready = sem("rope_k_ready"), sem("rope_q_ready")
        fox_abs_ready, fox_exp_ready, c_ready = sem("fox_abs_ready"), sem("fox_exp_ready"), sem("c_ready")
        gla_log_ready, gla_cum_ready, gla_exp_ready = (
            sem("gla_log_ready"), sem("gla_cum_ready"), sem("gla_exp_ready"))
        gla_end_ready, gla_decay_ready = sem("gla_end_ready"), sem("gla_decay_ready")
        gla_q_ready, gla_att_ready = sem("gla_q_ready"), sem("gla_att_ready")
        gla_out_ready = sem("gla_out_ready")
        last_sum_ready, resid_ready = sem("last_sum_ready"), sem("resid_ready")
        final_sq_ready, mean_ready = sem("final_sq_ready"), sem("mean_ready")
        y_ready, left_ready, right_ready = sem("y_ready"), sem("left_ready"), sem("right_ready")
        act_step, dve_step, pool_step = sem("act_step"), sem("dve_step"), sem("pool_step")

        def linker(eng, s):
            count = [0]

            def link(ins):
                count[0] += 1
                ins.then_inc(s, 1)
                eng.wait_ge(s, count[0])
            return link

        def wait_tp_free(eng, *key):
            eng.wait_ge(tp_free[TP[key] % 2], TP[key] // 2 + 1)

        def wait_evac(eng, name, i=None):
            s = AT[name]
            m = s.panel0 + (s.n - 1 if i is None else i)
            eng.wait_ge(acc_free[m % 2], 2 * (m // 2) + 2)

        def slot_of(stage, j):
            return {"cq": 16, "ckv": 12}.get(stage, 0) + j

        def region_of(stage):
            return 1 if stage in ("mem_o", "x_o", "mix_o") else 0

        S_ORDER = [arg for _, step, arg in SCHEDULE if step == "S"]
        S_INDEX = {key: i for i, key in enumerate(S_ORDER)}
        T_ORDER = [arg for _, step, arg in SCHEDULE if step == "T"]
        T_INDEX = {key: i for i, key in enumerate(T_ORDER)}

        def gain_of(stage, j):
            col = {"mem_e": G_EM, "mem_o": G_OM, "x_e": G_E, "x_o": G_O, "cq": G_CQ, "ckv": G_CKV}
            if stage in col:
                return gains[:, col[stage] + j:col[stage] + j + 1]
            if stage == "mix_o" and j < GLA_H * 4:
                return half_gla[:, j % 4:j % 4 + 1]
            return 0.5

        def source(stage, j, t):
            a, base = {"x_o": (xres, 0), "cq": (proj, 3 * FOXW), "ckv": (proj, 3 * FOXW + QRANK),
                       "mix_e": (gate[0], 0), "mix_o": (gate[1], 0)}[stage]
            return a[:, t, base + j * P:base + (j + 1) * P]

        def spans(v):
            if HEADS[v][0] == "mem":
                return [(0, 0, SEQ), (1, SEQ, SEQ)]
            return [(0, 0, P), (1, P, SEQ)]

        def blocks(v):
            return [(t, k) for t, _, n in spans(v) for k in range(n // P)]

        def depth(v):
            return 1 if v >= V_MEM1 else 2

        def buf(v, two, one):
            return two[v % 2] if v < V_MEM1 else one

        def p_of(v):
            return buf(v, p0, p1)

        def pt_of(v):
            return buf(v, pt0, pt1)

        def qk_of(v):
            return (qk0 if v < V_MEM1 else qk1)[v % 2]

        def values(v, k):
            kind, h, layer = HEADS[v]
            if kind == "fox":
                return proj[:, k, 2 * FOXW + h * HD:2 * FOXW + (h + 1) * HD]
            if kind == "mla":
                c = MLA_H * MLA_Q + h * MLA_KV + HD
                return proj[:, k, c:c + HD]
            return mv[layer][:, k, h * HD:(h + 1) * HD]

        def mix_col(v):
            kind, h, _ = HEADS[v]
            return {"fox": MIX_FOX, "mla": MIX_MLA, "mem": MIX_MEM}[kind] + h * HD

        gate_panels = [(s, i) for s in STREAMS if s.name in GATES for i in range(s.n)]
        gate_index = {(s.name, i): k for k, (s, i) in enumerate(gate_panels)}

        def gate_dst(s, i):
            layer = 0 if s.chunk0 < AT["mq_o"].chunk0 else 1
            c = {"fg": MIX_FOX, "mg": MIX_MLA, "memg_e": MIX_MEM, "gg": 0, "memg_o": MIX_MEM}[s.name] + i * PW
            return gate[layer][:, :, c:c + PW]

        def norm_of(s):
            return NORMS.index({"e_w_mem_kv": "mem", "o_w_mem_kv": "mem", "e_w_in": "x_e", "o_w_in": "x_o",
                                "e_ckv_ff": "x_e", "o_mq_ga": "x_o",
                                "e_mla_w_uq": "cq", "e_mla_w_ukv": "ckv"}[s.w])

        def copy_dst(s, i, t, q):
            w = s.cols[0][1]
            if s.name in ("mem_e", "mem_o"):
                layer = int(s.name == "mem_o")
                if i == 1:
                    return mv[layer][:, t, :]
                return mk[layer][:, t, :]
            if s.name in ("mq_e", "mq_o"):
                return mq[:, t, i * w:(i + 1) * w]
            base = {"fox": 0, "gqkv": 0, "uq": 0, "ukv": MLA_H * MLA_Q, "cq": 3 * FOXW,
                    "ckv": 3 * FOXW + QRANK}[s.name]
            return proj[:, t, bass.ds(lin(base + i * PW, 2 * PW, q), w)]

        def run_streams(eng, chunk, side_work, lag):
            def side(s, i, c, q):
                back = c - lag
                if q is None:
                    side_work(s.chunk0 + i * s.kc + back, None)
                elif back in (-1, s.kc - 1):
                    side_work(s.chunk0 + i * s.kc + back, q)

            for s in STREAMS:
                begin, pairs = looped(s)

                def panel(i, q):
                    for c in range(s.kc):
                        if lag:
                            side(s, i, c, q)
                        chunk(s, i, c, q)
                        if not lag:
                            side(s, i, c, q)
                i = 0
                while i < s.n:
                    if i == begin and pairs:
                        with eng.Fori(0, pairs) as q:
                            panel(begin, q)
                            panel(begin + 1, q)
                        i += 2 * pairs
                    else:
                        panel(i, None)
                        i += 1
            for n in range(CHUNKS - lag, CHUNKS + 1):
                side_work(n, None)

        def chunk_no(s, i, c, q):
            return lin(s.chunk0 + i * s.kc + c, 2 * s.kc, q)

        def slot(ring, s, i, c):
            n, w = s.chunk0 + i * s.kc + c, s.cols[i][1]
            return ring[:, n % RING, 0:2 * w].rearrange("p (k n) -> p k n", k=2)

        block = ctx.enter_context(nc.Block())

        @block.sync
        def _(sp):
            def load_mem_t(i):
                k0, k1 = MEM_T_CUT[i], MEM_T_CUT[i + 1]
                sp.dma_start(mem_t[:, k0:k1, :],
                             t_in["mem_t"][P * k0:P * k1, :].rearrange("(k p) m -> p k m", p=P)
                             ).then_inc(mem_t_in[i], 16)

            def columns(dst, name, i, done):
                cols = slice(i * PW, (i + 1) * PW)
                sp.dma_start(dst[:, :, cols],
                             t_in[name][0, :, cols].rearrange("(t p) n -> p t n", p=P)).then_inc(done[i], 16)

            def load(s, i, c, q):
                n = s.chunk0 + i * s.kc + c
                if n >= RING:
                    sp.wait_ge(lo_ready, chunk_no(s, i, c, q) - RING + 1)
                c0, w = s.cols[i]
                kt = s.ktiles[c]
                src = t_in[s.w][0, kt * P:(kt + 2) * P, bass.ds(lin(c0, 2 * PW, q), w)]
                src = src.rearrange("(k p) n -> p k n", p=P)
                sp.dma_start(slot(raw, s, i, c), src).then_inc(raw_in[n % RING], 16)

            def side_work(n, q):
                if 0 <= n < len(MEM_T_CUT) - 2:
                    load_mem_t(n + 1)
                if 3 <= n < 7:
                    columns(mem_rows, "mem", n - 3, mem_rows_in)
                if 15 <= n < 19:
                    if n == 15:
                        sp.wait_ge(sq_ready, 1)
                    k0, k1 = 4 * (n - 15), 4 * (n - 14)
                    sp.dma_start(x_t[:, k0:k1, :], t_in["x_t"][P * k0:P * k1, :].rearrange("(k p) m -> p k m", p=P)
                                 ).then_inc(x_t_in[n - 15], 16)
                if 19 <= n < 23:
                    columns(xres, "x", n - 19, x_in)
                if n == 24:
                    sp.dma_start(pos_i[:, :], t_in["pos"]).then_inc(small_in, 16)
                    sp.dma_start(freq[:, :], t_in["freq"]).then_inc(small_in, 16)
                    sp.dma_start(fbias[:, :], t_in["e_fox_b_f"].rearrange("a h -> h a")).then_inc(small_in, 16)
                if n == AT["mq_o"].chunk0:
                    sp.wait_ge(score_ready, V_MLA)
                    sp.dma_start(wa2[:, :], t_in["o_gla_w_a2"][0]).then_inc(wa2_in, 16)
                if n == AT["out2_o"].chunk0 - 8:
                    sp.wait_ge(gla_out_ready, GLA_H * TT)
                    sp.dma_start(gain_row[:, :], t_in["final_norm_w"].partition_broadcast(P)).then_inc(row_in, 16)

            load_mem_t(0)
            run_streams(sp, load, side_work, 0)
            half = D // 2
            for t in range(TT):
                for i, ready in enumerate((left_ready, right_ready)):
                    sp.wait_ge(ready, t + 1)
                    sp.dma_start(out[0, t * P:(t + 1) * P, i * half:(i + 1) * half],
                                 y[:, t, i * half:(i + 1) * half]).then_inc(out_done, 16)
            sp.wait_ge(out_done, 16 * 2 * TT)

        @block.gpsimd
        def _(pool):
            link = linker(pool, pool_step)
            g = nc.gpsimd
            link(g.memset(ident[:, :], 0.0))
            link(g.affine_select(out=ident[:, :], in_=ident[:, :], compare_op=ALU.not_equal, fill=1.0, base=0,
                                 pattern=[[-1, P]], channel_multiplier=1))
            g.memset(mhalf[:, :], -0.5)
            g.memset(half_pi[:, :], float(np.pi / 2))
            g.memset(ones[:, :], 1.0).then_inc(consts_ready, 1)
            link(g.memset(fox_mask[:, :], 0.0))
            link(g.affine_select(out=fox_mask[:, :], in_=fox_mask[:, :], compare_op=ALU.is_ge, fill=NEG, base=0,
                                 pattern=[[-1, P]], channel_multiplier=1))
            link(g.memset(mla_mask[:, :], 0.0))
            link(g.memset(mla_mask[0:CHUNK, CHUNK:P], NEG))
            link(g.memset(gla_mask[:, :], 1.0))
            for r in range(0, P, CHUNK):
                link(g.affine_select(out=gla_mask[r:r + CHUNK, :], in_=gla_mask[r:r + CHUNK, :],
                                     compare_op=ALU.is_ge, fill=0.0, base=0, pattern=[[1, CHUNK]],
                                     channel_multiplier=-1))
            link(g.memset(sel_f[:, :], 0.0))
            for base in (0, -32):
                link(g.affine_select(out=sel_f[:, :], in_=sel_f[:, :], compare_op=ALU.not_equal, fill=1.0,
                                     base=base, pattern=[[-1, FOX_H]], channel_multiplier=1))
            g.memset(c_zero[:, :], 0.0).then_inc(masks_ready, 1)

            def norm(k, n, width):
                pool.wait_ge(sq_ready, k + 1)
                total = ssq[:, k, :, 0:1]
                if n == 4:
                    link(g.tensor_tensor(ntmp[:, :, 0:2], ssq[:, k, :, 0:2], ssq[:, k, :, 2:4], ALU.add))
                    link(g.tensor_tensor(ntmp[:, :, 2:3], ntmp[:, :, 0:1], ntmp[:, :, 1:2], ALU.add))
                    total = ntmp[:, :, 2:3]
                link(g.tensor_scalar(ntmp[:, :, 3:4], total, 1.0 / width, EPS, ALU.mult, ALU.add))
                link(g.tensor_tensor(rms[:, k, :], ntmp[:, :, 3], mhalf[:, :], ALU.pow))
                g.tensor_scalar(rms_half[:, k, :], rms[:, k, :], 0.5, 0.0, ALU.mult,
                                ALU.add).then_inc(rms_ready, 1)

            def rotate(dst1, dst2, x1, x2, c, s, a, b):
                link(g.tensor_tensor(a, x1, c, ALU.mult))
                link(g.tensor_tensor(b, x2, s, ALU.mult))
                link(g.tensor_tensor(dst1, a, b, ALU.subtract))
                link(g.tensor_tensor(a, x1, s, ALU.mult))
                link(g.tensor_tensor(b, x2, c, ALU.mult))
                return g.tensor_tensor(dst2, a, b, ALU.add)

            H2 = ROPE // 2
            norm(0, 4, D)
            norm(1, 4, D)
            norm(2, 1, KVRANK)
            norm(3, 1, QRANK)
            pool.wait_ge(trig_ready, 1)
            link(g.memset(k_rot[:, :, :, :, :], 0.0))
            wait_evac(pool, "ckv")
            kc = KR_AT
            for t in range(TT):
                for z in range(2):
                    last = rotate(k_rot[:, t, z, z, 0:H2], k_rot[:, t, z, z, H2:ROPE],
                                  proj[:, t, kc:kc + H2], proj[:, t, kc + H2:kc + ROPE],
                                  cos[:, t, :], sin[:, t, :], kr_a[:, :], kr_b[:, :])
                    if (t, z) == (TT - 1, 1):
                        last.then_inc(rope_k_ready, 1)
                    else:
                        link(last)
            wait_evac(pool, "uq")
            wait_evac(pool, "uq", 1)
            for t in range(TT):
                q4 = proj[:, t, 0:MLA_H * MLA_Q].rearrange("p (h d) -> p h d", h=MLA_H)
                r4 = q_rot[:, t, :].rearrange("p (h d) -> p h d", h=MLA_H)
                last = rotate(r4[:, :, 0:H2], r4[:, :, H2:ROPE], q4[:, :, HD:HD + H2], q4[:, :, HD + H2:MLA_Q],
                              cos[:, t:t + 1, :].to_broadcast([P, MLA_H, H2]),
                              sin[:, t:t + 1, :].to_broadcast([P, MLA_H, H2]),
                              rope_a[:, :, :], rope_b[:, :, :])
                if t == TT - 1:
                    last.then_inc(rope_q_ready, 1)
                else:
                    link(last)
            norm(4, 4, D)
            k = NORMS.index("gla0")
            for i in range(GLA_H * TT):
                pool.wait_ge(sq_ready, k + i + 1)
                link(g.tensor_scalar(ntmp[:, 0, 3:4], ssq[:, k + i, 0, 0:1], 1.0 / GLA_DV, EPS, ALU.mult, ALU.add))
                link(g.tensor_tensor(ntmp[:, 0, 2:3], ntmp[:, 0, 3:4], mhalf[:, 0:1], ALU.pow))
                g.tensor_tensor(rms[:, k + i, 0:1], ntmp[:, 0, 2:3], rms[:, 4, i % TT:i % TT + 1],
                                ALU.mult).then_inc(rms_ready, 1)
            k = len(NORMS) - 1
            for t in range(TT):
                pool.wait_ge(mean_ready, t + 1)
                g.tensor_tensor(rms[:, k, t:t + 1], mean[:, t:t + 1], mhalf[:, 0:1], ALU.pow).then_inc(rms_ready, 1)

        @block.scalar
        def _(act):
            link = linker(act, act_step)
            a = nc.scalar
            a.dma_start(gains[:, :], t_in["gains"]).then_inc(gains_in, 16)

            def step_trig():
                act.wait_ge(angle_ready, 1)
                act.wait_ge(consts_ready, 1)
                a.activation(sin[:, :, :], t_ang[:, :, :], ACT.Sin)
                a.activation(cos[:, :, :], t_n[:, :, :], ACT.Sin, bias=half_pi[:, 0:1],
                             scale=-1.0).then_inc(trig_ready, 1)

            def split_hi(s, i, c, q):
                n = s.chunk0 + i * s.kc + c
                act.wait_ge(raw_in[n % RING], lin(16 * (n // RING + 1), 16 * 2 * s.kc // RING, q))
                if n >= RING:
                    act.wait_ge(chunk_used, chunk_no(s, i, c, q) - RING + 1)
                a.activation(slot(hi, s, i, c), slot(raw, s, i, c), ACT.Copy).then_inc(hi_ready, 1)

            def move_out(s, i, q):
                if s.name.startswith("out"):
                    return
                act.wait_ge(chunk_used, chunk_no(s, i, s.kc - 1, q) + 1)
                k = norm_of(s)
                act.wait_ge(rms_ready, k + 1)
                b = acc[(s.panel0 + i) % 2]
                w = s.cols[i][1]
                if s.name in GATES:
                    g = gate_index[s.name, i]
                    if g:
                        s1_, i1_ = gate_panels[g - 1]
                        wait_evac(act, s1_.name, i1_)
                    for t in range(TT):
                        a.activation(th[t][:, :], b[t][:, :], ACT.Tanh,
                                     scale=rms_half[:, k, t:t + 1]).then_inc(tanh_ready, 1)
                    return
                if s.name == "uq" and i == 0:
                    act.wait_ge(out_ready, FOX_H)
                for t in range(TT):
                    a.activation(copy_dst(s, i, t, q), b[t][:, 0:w], ACT.Copy,
                                 scale=rms[:, k, t:t + 1]).then_inc(acc_free[(s.panel0 + i) % 2], 1)

            def final_squares(j, t):
                k, count = NORMS.index("final"), TT * j + t
                if count:
                    act.wait_ge(final_sq_ready, count)
                a.activation(junk[:, :], xres[:, t, j * PW:(j + 1) * PW], ACT.Square,
                             accum_out=ssq[:, k, t, j:j + 1]).then_inc(final_sq_ready, 1)

            def squares(name, *part):
                k = NORMS.index(name)
                if name in ("cq", "ckv"):
                    wait_evac(act, name)
                    c, w = {"cq": (3 * FOXW, QRANK), "ckv": (3 * FOXW + QRANK, KVRANK)}[name]
                    act.wait_ge(sq_ready, k)
                    link(a.activation(junk[:, 0:w], proj[:, 0, c:c + w], ACT.Square, accum_out=ssq[:, k, 0, 0:1]))
                    a.activation(junk[:, 0:w], proj[:, 1, c:c + w], ACT.Square,
                                 accum_out=ssq[:, k, 1, 0:1]).then_inc(sq_ready, 1)
                    return
                src = mem_rows if name == "mem" else xres
                if name == "mem":
                    act.wait_ge(mem_rows_in[part[0]], 16)
                elif name == "x_e":
                    act.wait_ge(x_in[part[0]], 16)
                else:
                    wait_evac(act, "out2_e" if name == "x_o" else "out2_o", part[0])
                if k:
                    act.wait_ge(sq_ready, k)
                if name == "final":
                    for t in range(TT):
                        final_squares(part[0], t)
                    return
                for j in part:
                    for t in range(TT):
                        ins = a.activation(junk[:, :], src[:, t, j * PW:(j + 1) * PW], ACT.Square,
                                           accum_out=ssq[:, k, t, j:j + 1])
                        if (j, t) == (3, TT - 1):
                            ins.then_inc(sq_ready, 1)
                        else:
                            link(ins)

            def step_t(stage, j):
                u = TP["T", stage, j]
                act.wait_ge(tp_ready, u + 1)
                if stage == "mix_o" and j == 0:
                    act.wait_ge(sel_ready, 1)
                a.activation(act_hi[region_of(stage)][:, slot_of(stage, j), :], tp("T", stage, j)[:, 0:SEQ],
                             ACT.Copy, scale=gain_of(stage, j)).then_inc(t_hi_ready, 1)

            def step_s(stage, j):
                if S_INDEX[stage, j] == 0:
                    act.wait_ge(gains_in, 16)
                src = mem_t
                if stage == "x_e":
                    act.wait_ge(chunk_used, AT["mem_o"].chunk0)
                    act.wait_ge(x_t_in[j // 4], 16)
                    src = x_t
                else:
                    piece = max(i for i, k in enumerate(MEM_T_CUT) if k <= j)
                    act.wait_ge(mem_t_in[piece], 16)
                a.activation(act_hi[int(stage == "mem_o")][:, j, :], src[:, j, :], ACT.Copy,
                             scale=gain_of(stage, j)).then_inc(staged_hi, 1)

            def step_a(v):
                kind, h, _ = HEADS[v]
                scale = float((HD + ROPE) ** -0.5 if kind == "mla" else HD ** -0.5)
                if v >= 2:
                    act.wait_ge(score_ready, v - 1)
                act.wait_ge(tp_ready, TP["A", v] + 1)
                ps, dst = tp("A", v), qk_of(v)
                q = a.activation(dst[:, 0:SEQ], ps[:, 0:SEQ], ACT.Copy, scale=scale)
                if kind == "mem":
                    q.then_inc(tp_free[TP["A", v] % 2], 1)
                    return
                a.activation(dst[:, SEQ:2 * SEQ], ps[:, SEQ:2 * SEQ],
                             ACT.Copy).then_inc(tp_free[TP["A", v] % 2], 1)
                if ("Ar", v) in TP:
                    act.wait_ge(tp_ready, TP["Ar", v] + 1)
                    if h >= 4:
                        act.wait_ge(score_ready, v - 2)
                    a.activation(q_rot_t[h // 2 % 2][:, :], tp("Ar", v)[:, 0:SEQ], ACT.Copy,
                                 scale=scale).then_inc(tp_free[TP["Ar", v] % 2], 1)

            def step_b(v):
                act.wait_ge(max_ready, v + 1)
                d = depth(v)
                if v == V_MEM1:
                    act.wait_ge(out_ready, V_MLA)
                elif v >= d:
                    act.wait_ge(tp_ready, TP["D", v - d] + 1)
                for t, c, n in spans(v):
                    last = a.activation(p_of(v)[:, c:c + n], sc("B", v)[:, c:c + n], ACT.Exp,
                                        bias=neg_max[:, v, t:t + 1], accum_out=rsum[:, v, t:t + 1])
                last.then_inc(exp_ready, 1)

            def step_ff(part):
                if part == 0:
                    act.wait_ge(fox_abs_ready, 1)
                    a.activation(fs[:, :], fa[:, :], ACT.Exp, scale=-1.0).then_inc(fox_exp_ready, 1)

            def step_gz(h):
                u = TP["Gz", h]
                act.wait_ge(tp_ready, u + 1)
                if h:
                    act.wait_ge(gla_att_ready, h)
                for kk in range(2):
                    k = G_BA + 2 * h + kk
                    z = a.activation(g_z[:, kk * SEQ:(kk + 1) * SEQ], tp("Gz", h)[:, kk * SEQ:(kk + 1) * SEQ],
                                     ACT.Identity, bias=gains[:, k:k + 1])
                z.then_inc(tp_free[u % 2], 1)
                act.wait_ge(tp_free[u % 2], u // 2 + 1)
                link(a.activation(g_a[:, :], g_z[:, :], ACT.Abs))
                link(a.activation(g_a[:, :], g_a[:, :], ACT.Exp, scale=-1.0))
                a.activation(g_a[:, :], g_a[:, :], ACT.Ln, bias=ones[:, 0:1]).then_inc(gla_log_ready, 1)

            def step_gd(h):
                act.wait_ge(gla_cum_ready, h + 1)
                a.activation(g_ep[:, :], g_cum[:, :], ACT.Exp, scale=1.0 / TAU)
                a.activation(g_en[:, :], g_cum[:, :], ACT.Exp, scale=-1.0 / TAU).then_inc(gla_exp_ready, 1)
                act.wait_ge(gla_end_ready, h + 1)
                a.activation(g_a[:, :], g_a[:, :], ACT.Exp, scale=1.0 / TAU).then_inc(gla_decay_ready, 1)

            def step_go(h, t):
                i = TT * h + t
                act.wait_ge(gla_out_ready, i + 1)
                act.wait_ge(sq_ready, NORMS.index("gla0") + i)
                a.activation(junk[:, :], sc("Go", h, t)[:, :], ACT.Square,
                             accum_out=ssq[:, NORMS.index("gla0") + i, 0, 0:1]).then_inc(sq_ready, 1)

            steps = {"T": step_t, "S": step_s, "A": step_a, "B": step_b, "ff": step_ff, "trig": step_trig,
                     "Gz": step_gz, "Gd": step_gd, "sq": squares,
                     "G0": lambda h: step_go(h, 0), "G1": lambda h: step_go(h, 1)}

            def side_work(n, q):
                if n in PANEL_OF:
                    move_out(*PANEL_OF[n], q)
                if q is None:
                    for step, arg in AFTER.get(n, ()):
                        if step in steps:
                            steps[step](*arg)

            for step, arg in BEFORE:
                if step in steps:
                    steps[step](*arg)
            run_streams(act, split_hi, side_work, LAG)
            k = len(NORMS) - 1
            for t in range(TT):
                act.wait_ge(resid_ready, t + 1)
                final_squares(LAST, t)
                act.wait_ge(rms_ready, k + t + 1)
                act.wait_ge(y_ready, LAST + t + 1)
                a.activation(y[:, t, D // 2:D], y[:, t, D // 2:D], ACT.Copy,
                             scale=rms[:, k, t:t + 1]).then_inc(right_ready, 1)

        @block.vector
        def _(dve):
            link = linker(dve, dve_step)
            d = nc.vector
            def step_trig():
                dve.wait_ge(small_in, 16 * 3)
                dve.wait_ge(gains_in, 16)
                link(d.tensor_copy(pos_f[:, :], pos_i[:, :]))
                for t in range(TT):
                    last = d.tensor_scalar(t_ang[:, t, :], freq[:, :], pos_f[:, t:t + 1], None, ALU.mult)
                link(last)
                link(d.tensor_scalar(t_n[:, :, :], t_ang[:, :, :], float(1 / (2 * np.pi)), None, ALU.mult))
                magic = float(1.5 * 2 ** 23)
                link(d.tensor_scalar(t_n[:, :, :], t_n[:, :, :], magic, magic, ALU.add, ALU.subtract))
                rest, parts = 2 * np.pi, []
                for i in range(5):
                    grid = 2.0 ** (-3 - 6 * i)
                    part = np.floor(rest / grid) * grid if i < 4 else rest
                    parts.append(float(part))
                    rest -= part
                for part in parts:
                    link(d.scalar_tensor_tensor(t_ang[:, :, :], t_n[:, :, :], -part, t_ang[:, :, :],
                                                ALU.mult, ALU.add))
                top_angle = 3.1415925
                link(d.tensor_scalar(t_ang[:, :, :], t_ang[:, :, :], top_angle, -top_angle, ALU.min, ALU.max))
                d.scalar_tensor_tensor(t_n[:, :, :], t_ang[:, :, :], -1.0, t_ang[:, :, :], ALU.mult,
                                       ALU.max).then_inc(angle_ready, 1)
                d.tensor_scalar(half_gla[:, :], gains[:, G_GLA:G_GLA + 4], 0.5, None, ALU.mult).then_inc(sel_ready, 1)

            def split_lo(s, i, c, q):
                n = s.chunk0 + i * s.kc + c
                dve.wait_ge(hi_ready, chunk_no(s, i, c, q) + 1)
                if n >= RING:
                    dve.wait_ge(chunk_used, chunk_no(s, i, c, q) - RING + 1)
                d.tensor_tensor(slot(lo, s, i, c), slot(raw, s, i, c), slot(hi, s, i, c).bitcast(F32),
                                ALU.subtract).then_inc(lo_ready, 1)

            def move_out(s, i, q):
                m = (s.panel0 + i) % 2
                if s.name in GATES:
                    g = gate_index[s.name, i]
                    dst = gate_dst(s, i)
                    for t in range(TT):
                        dve.wait_ge(tanh_ready, TT * g + t + 1)
                        d.scalar_tensor_tensor(dst[:, t, :], th[t][:, :], 1.0, acc[m][t][:, :], ALU.add,
                                               ALU.mult).then_inc(acc_free[m], 1)
                elif (s.name, i) == ("out2_o", LAST):
                    return
                elif s.name.startswith("out"):
                    dve.wait_ge(chunk_used, chunk_no(s, i, s.kc - 1, q) + 1)
                    if s.name[3] == "2":
                        wait_evac(dve, s.name.replace("2", "1"), i)
                    for t in range(TT):
                        x = xres[:, t, i * PW:(i + 1) * PW]
                        d.tensor_tensor(x, acc[m][t][:, :], x, ALU.add).then_inc(acc_free[m], 1)

            def step_t(stage, j):
                r, at = region_of(stage), slot_of(stage, j)
                dve.wait_ge(t_hi_ready, T_INDEX[stage, j] + 1)
                d.scalar_tensor_tensor(act_lo[r][:, at, :], tp("T", stage, j)[:, 0:SEQ], gain_of(stage, j),
                                       act_hi[r][:, at, :].bitcast(F32), ALU.mult,
                                       ALU.subtract).then_inc(tp_free[TP["T", stage, j] % 2], 1)

            def step_s(stage, j):
                r, src = int(stage == "mem_o"), x_t if stage == "x_e" else mem_t
                dve.wait_ge(staged_hi, S_INDEX[stage, j] + 1)
                d.scalar_tensor_tensor(act_lo[r][:, j, :], src[:, j, :], gain_of(stage, j),
                                       act_hi[r][:, j, :].bitcast(F32), ALU.mult,
                                       ALU.subtract).then_inc(staged_lo, 1)

            def step_mk(layer, i):
                u = TP["mk", layer, i]
                dve.wait_ge(tp_ready, u + 1)
                d.tensor_copy(mkt[layer][:, 2 * i:2 * i + 2, :].rearrange("p h m -> p (h m)"),
                              tp("mk", layer, i)[:, :]).then_inc(tp_free[u % 2], 1)

            def step_kr():
                u = TP["kr",]
                dve.wait_ge(tp_ready, u + 1)
                d.tensor_copy(k_rot_t[:, :, :].rearrange("p z m -> p (z m)"),
                              tp("kr")[:, :]).then_inc(tp_free[u % 2], 1)

            def ff_abs():
                u = TP["ffT",]
                dve.wait_ge(tp_ready, u + 1)
                d.tensor_scalar(fz[:, :], tp("ffT")[0:FOX_H, 0:SEQ], fbias[:, 0:1], None,
                                ALU.add).then_inc(tp_free[u % 2], 1)
                dve.wait_ge(tp_free[u % 2], u // 2 + 1)
                d.scalar_tensor_tensor(fa[:, :], fz[:, :], -1.0, fz[:, :], ALU.mult,
                                       ALU.max).then_inc(fox_abs_ready, 1)

            def ff_series():
                dve.wait_ge(fox_exp_ready, 1)
                link(d.tensor_scalar(fa[:, :], fs[:, :], 2.0, None, ALU.add))
                link(d.reciprocal(fa[:, :], fa[:, :]))
                link(d.tensor_tensor(fs[:, :], fs[:, :], fa[:, :], ALU.mult))
                link(d.tensor_tensor(fa[:, :], fs[:, :], fs[:, :], ALU.mult))
                link(d.tensor_scalar(fp[:, :], fa[:, :], 1.0 / 17, None, ALU.mult))

            def ff_series_end():
                for odd in range(15, 1, -2):
                    link(d.scalar_tensor_tensor(fp[:, :], fp[:, :], 1.0 / odd, fa[:, :], ALU.add, ALU.mult))
                link(d.scalar_tensor_tensor(fp[:, :], fp[:, :], 1.0, fs[:, :], ALU.add, ALU.mult))

            def ff_sum():
                link(d.tensor_scalar(fz[:, :], fz[:, :], 0.0, None, ALU.min))
                link(d.scalar_tensor_tensor(fz[:, :], fp[:, :], -2.0, fz[:, :], ALU.mult, ALU.add))
                link(d.memset(fa[:, :], 1.0))
                link(d.tensor_tensor_scan(fp[:, :], fa[:, :], fz[:, :], 0.0, ALU.mult, ALU.add))
                dve.wait_ge(masks_ready, 1)
                link(d.tensor_copy(c_pos[:, :], c_zero[:, :]))
                link(d.tensor_copy(c_pos[0:FOX_H, :], fp[:, :]))
                link(d.tensor_tensor(c_pos[32:32 + FOX_H, :], fp[:, :], c_pos[0:FOX_H, :].bitcast(F32),
                                     ALU.subtract))
                link(d.tensor_scalar(c_neg[:, :], c_pos[:, :].bitcast(F32), -1.0, None, ALU.mult))
                d.tensor_copy(ident_b[:, :], ident[:, :])
                d.tensor_copy(sel[:, :], sel_f[:, :]).then_inc(c_ready, 1)

            def step_b(v):
                dve.wait_ge(score_ready, v + 1)
                for t, c, n in spans(v):
                    last = d.tensor_reduce(neg_max[:, v, t:t + 1], sc("B", v)[:, c:c + n], AX.X, ALU.max,
                                           negate=True)
                last.then_inc(max_ready, 1)

            def step_d(v):
                u, n = TP["D", v], len(blocks(v)) * P
                dve.wait_ge(tp_ready, u + 1)
                if v >= depth(v):
                    dve.wait_ge(out_ready, v - depth(v) + 1)
                d.tensor_copy(pt_of(v)[:, 0:n], tp("D", v)[:, 0:n]).then_inc(tp_free[u % 2], 1)

            def step_e(v):
                layer = HEADS[v][2]
                k = NORMS.index("x_o" if layer else "x_e")
                dve.wait_ge(exp_ready, v + 1)
                dve.wait_ge(rms_ready, k + 1)
                link(d.reciprocal(rinv[:, v, :], rsum[:, v, :]))
                link(d.tensor_tensor(rinv[:, v, :], rinv[:, v, :], rms[:, k, :], ALU.mult))
                dve.wait_ge(out_ready, v + 1)
                c = mix_col(v)
                for t in range(TT):
                    g = gate[layer][:, t, c:c + HD]
                    last = d.scalar_tensor_tensor(g, sc("B", v)[:, t * P:(t + 1) * P], rinv[:, v, t:t + 1], g,
                                                  ALU.mult, ALU.mult)
                last.then_inc(sc_free[SC["B", v] % 2], 1)

            def step_ga_t():
                u = TP["gaT",]
                dve.wait_ge(tp_ready, u + 1)
                d.tensor_copy(ga_t[:, :], tp("gaT")[0:GRANK, 0:SEQ]).then_inc(tp_free[u % 2], 1)
                link(d.memset(reset[:, :], 1.0))
                link(d.memset(reset[:, :].rearrange("p (c k) -> p c k", k=CHUNK)[:, :, 0:1], 0.0))
                link(d.memset(g_att[CHUNK:P, 0:TT, 0:CHUNK], 0.0))

            def step_gz(h):
                dve.wait_ge(gla_log_ready, h + 1)
                link(d.scalar_tensor_tensor(g_z[:, :], g_z[:, :], 0.0, g_a[:, :], ALU.min, ALU.subtract))
                d.tensor_tensor_scan(g_cum[:, :], reset[:, :], g_z[:, :], 0.0, ALU.mult,
                                     ALU.add).then_inc(gla_cum_ready, 1)
                dve.wait_ge(gla_cum_ready, h + 1)
                cum = g_cum[:, :].rearrange("p (c k) -> p c k", k=CHUNK)
                d.tensor_tensor(g_a[:, :].rearrange("p (c k) -> p c k", k=CHUNK),
                                cum[:, :, CHUNK - 1:CHUNK].to_broadcast([P, 2 * SEQ // CHUNK, CHUNK]), cum,
                                ALU.subtract).then_inc(gla_end_ready, 1)

            def decay_of(kk, c):
                at = kk * SEQ + (c + 1) * CHUNK - 1
                return g_ep[:, at:at + 1]

            def step_gq(h):
                u = TP["Gq", h]
                dve.wait_ge(tp_ready, u + 1)
                dve.wait_ge(gla_exp_ready, h + 1)
                d.scalar_tensor_tensor(g_qd[:, :], tp("Gq", h)[:, :], float(GLA_DK ** -0.5), g_ep[:, :],
                                       ALU.mult, ALU.mult).then_inc(tp_free[u % 2], 1)
                dve.wait_ge(tp_free[u % 2], u // 2 + 1)
                if h:
                    dve.wait_ge(gla_att_ready, h)
                qd = g_qd[:, :].rearrange("p (k c n) -> p k c n", k=2, n=CHUNK)
                qs = g_qs[:, :].rearrange("p (k c n) -> p k c n", k=2, n=CHUNK)
                d.tensor_copy(qs[:, :, 0, :], qd[:, :, 2, :])
                for kk in range(2):
                    last = d.tensor_scalar(qs[:, kk, 1, :], qd[:, kk, 3, :], decay_of(kk, 2), None, ALU.mult)
                last.then_inc(gla_q_ready, 1)

            def step_gk(h):
                u = TP["Gk", h]
                dve.wait_ge(tp_ready, u + 1)
                dve.wait_ge(gla_decay_ready, h + 1)
                link(d.tensor_tensor(g_a[:, :], tp("Gk", h)[:, :], g_a[:, :], ALU.mult))
                ke = g_a[:, :].rearrange("p (k c n) -> p k c n", k=2, n=CHUNK)
                kt = g_ke_t[:, :].rearrange("p (k c n) -> p k c n", k=2, n=CHUNK)
                d.tensor_copy(kt[:, :, 1, :], ke[:, :, 1, :])
                for kk in range(2):
                    d.tensor_scalar(kt[:, kk, 0, :], ke[:, kk, 0, :], decay_of(kk, 1), None, ALU.mult)
                d.tensor_tensor(g_en[:, :], tp("Gk", h)[:, :], g_en[:, :], ALU.mult).then_inc(tp_free[u % 2], 1)

            def step_ga(h):
                b = sc("Ga", h)[:, 0:TT * P].rearrange("p (t n) -> p t n", t=TT)
                dve.wait_ge(gla_att_ready, h + 1)
                for r in (0, CHUNK):
                    rows, cols = slice(r, r + CHUNK), slice(r, r + CHUNK)
                    d.tensor_tensor(g_att[rows, 0:TT, cols], b[rows, :, cols],
                                    gla_mask[rows, :].unsqueeze(1).to_broadcast([CHUNK, TT, CHUNK]), ALU.mult)
                d.tensor_copy(g_att[0:CHUNK, 0:TT, CHUNK:P], b[0:CHUNK, :, CHUNK:P])
                d.tensor_copy(g_att[:, TT, :],
                              sc("Ga", h)[:, TT * P:(TT + 1) * P]).then_inc(sc_free[SC["Ga", h] % 2], 1)

            def step_go(h, t):
                i = TT * h + t
                k = NORMS.index("gla0") + i
                dve.wait_ge(rms_ready, k + 1)
                g = gate[1][:, t, h * GLA_DV:(h + 1) * GLA_DV]
                d.scalar_tensor_tensor(g, sc("Go", h, t)[:, :], rms[:, k, 0:1], g, ALU.mult,
                                       ALU.mult).then_inc(sc_free[SC["Go", h, t] % 2], 1)

            def step_y(i):
                cols = slice(i * PW, (i + 1) * PW)
                wait_evac(dve, "out2_o", i)
                dve.wait_ge(row_in, 16)
                for t in range(TT):
                    last = d.tensor_tensor(y[:, t, cols], xres[:, t, cols], gain_row[:, cols], ALU.mult)
                last.then_inc(y_ready, 1)

            steps = {"T": step_t, "S": step_s, "mk": step_mk, "kr": step_kr, "B": step_b, "D": step_d,
                     "ff": lambda i: (ff_abs, ff_series, ff_series_end, ff_sum)[i](), "trig": step_trig,
                     "y": step_y, "E": step_e, "gaT": step_ga_t, "Gz": step_gz, "Gq": step_gq, "Gk": step_gk,
                     "Ga": step_ga,
                     "G0": lambda h: step_go(h, 0), "G1": lambda h: step_go(h, 1)}

            def side_work(n, q):
                if n in PANEL_OF:
                    move_out(*PANEL_OF[n], q)
                if q is None:
                    for step, arg in AFTER.get(n, ()):
                        if step in steps:
                            steps[step](*arg)

            for step, arg in BEFORE:
                if step in steps:
                    steps[step](*arg)
            run_streams(dve, split_lo, side_work, LAG)
            k, cols = len(NORMS) - 1, slice(LAST * PW, D)
            dve.wait_ge(final_sq_ready, TT * LAST)
            link(d.tensor_tensor(mean[:, :], ssq[:, k, :, 0], ssq[:, k, :, 1], ALU.add))
            link(d.scalar_tensor_tensor(mean[:, :], mean[:, :], EPS * D, ssq[:, k, :, 2], ALU.add, ALU.add))
            wait_evac(dve, "out1_o", LAST)
            for t in range(TT):
                dve.wait_ge(last_sum_ready, t + 1)
                x, total = xres[:, t, cols], acc[(AT["out2_o"].panel0 + LAST) % 2][t]
                d.tensor_tensor(x, total[:, :], x, ALU.add).then_inc(resid_ready, 1)
                dve.wait_ge(resid_ready, t + 1)
                d.tensor_tensor(y[:, t, cols], x, gain_row[:, cols], ALU.mult).then_inc(y_ready, 1)
                dve.wait_ge(final_sq_ready, TT * LAST + t + 1)
                d.tensor_scalar(mean[:, t:t + 1], ssq[:, k, t, LAST:LAST + 1], mean[:, t:t + 1], 1.0 / D, ALU.add,
                                ALU.mult).then_inc(mean_ready, 1)
                dve.wait_ge(rms_ready, k + t + 1)
                dve.wait_ge(y_ready, LAST + t + 1)
                d.tensor_scalar(y[:, t, 0:D // 2], y[:, t, 0:D // 2], rms[:, k, t:t + 1], None,
                                ALU.mult).then_inc(left_ready, 1)

        @block.tensor
        def _(pe):
            mm = nc.tensor.matmul
            pe.wait_ge(consts_ready, 1)

            def tr(dst, src):
                return nc.tensor.transpose(dst, src, ident[:, :])

            def take_tp(*key):
                u = TP[key]
                if u >= 2:
                    pe.wait_ge(tp_free[u % 2], u // 2)
                return tp(*key)

            def take_sc(*key):
                u = SC[key]
                if u >= 2:
                    pe.wait_ge(sc_free[u % 2], u // 2)
                return sc(*key)

            def project(s, i, c, q):
                w = s.cols[i][1]
                m = s.panel0 + i
                if c == 0 and m >= 2:
                    pe.wait_ge(acc_free[m % 2], lin(2 * (m // 2), 2, q))
                if i == 0 and s.ready and q is None:
                    for key in s.ready(c):
                        if key in S_INDEX:
                            pe.wait_ge(staged_lo, S_INDEX[key] + 1)
                        else:
                            wait_tp_free(pe, "T", *key)
                pe.wait_ge(lo_ready, chunk_no(s, i, c, q) + 1)

                def product(t, c, j):
                    k = s.slots[c] + j
                    first, end = (c == 0 and j == 0), (c == s.kc - 1 and j == 1)
                    wh, wl = slot(hi, s, i, c)[:, j, :], slot(lo, s, i, c)[:, j, :]
                    xh = act_hi[s.act][:, k, t * P:(t + 1) * P]
                    xl = act_lo[s.act][:, k, t * P:(t + 1) * P]
                    o = acc[m % 2][t][:, 0:w]
                    mm(o, xh, wh, start=first, stop=False)
                    mm(o, xh, wl, start=False, stop=False)
                    return mm(o, xl, wh, start=False, stop=end)

                if (s.name, i) == ("out2_o", LAST):
                    if c == s.kc - 1:
                        for t in range(TT):
                            for c_ in range(s.kc):
                                for j in range(2):
                                    last = product(t, c_, j)
                            last.then_inc(last_sum_ready, 1)
                    return
                for j in range(2):
                    for t in range(TT):
                        last = product(t, c, j)
                last.then_inc(chunk_used, 1)

            def step_t(stage, j):
                b = take_tp("T", stage, j)
                if stage == "x_o":
                    pe_wait_resid(j)
                if stage in ("cq", "ckv"):
                    wait_evac(pe, stage)
                if stage == "mix_e":
                    v = (j if j < FOX_H else V_MLA + j - FOX_H if j < 16 else V_MEM0 + j - 16)
                    pe.wait_ge(sc_free[SC["B", v] % 2], SC["B", v] // 2 + 1)
                if stage == "mix_o" and j < 16:
                    for t in range(TT):
                        u = SC["Go", j // 4, t]
                        pe.wait_ge(sc_free[u % 2], u // 2 + 1)
                if stage == "mix_o" and j >= 16:
                    u = SC["B", V_MEM1 + j - 16]
                    pe.wait_ge(sc_free[u % 2], u // 2 + 1)
                for t in range(TT):
                    last = tr(b[:, t * P:(t + 1) * P], source(stage, j, t))
                last.then_inc(tp_ready, 1)

            def pe_wait_resid(j):
                wait_evac(pe, "out2_e", j // 4)

            def step_mk(layer, i):
                b = take_tp("mk", layer, i)
                wait_evac(pe, "mem_o" if layer else "mem_e", 0)
                for h in range(2):
                    for t in range(TT):
                        c = (2 * i + h) * HD
                        last = tr(b[:, h * SEQ + t * P:h * SEQ + (t + 1) * P], mk[layer][:, t, c:c + HD])
                last.then_inc(tp_ready, 1)

            def step_ff(part):
                if part:
                    return
                b = take_tp("ffT")
                wait_evac(pe, "ckv")
                for t in range(TT):
                    last = tr(b[0:FOX_H, t * P:(t + 1) * P], proj[:, t, FF_AT:FF_AT + FOX_H])
                last.then_inc(tp_ready, 1)

            def step_kr():
                b = take_tp("kr")
                pe.wait_ge(rope_k_ready, 1)
                for z in range(2):
                    for t in range(TT):
                        last = tr(b[:, z * SEQ + t * P:z * SEQ + (t + 1) * P],
                                  k_rot[:, t, z, :, :].rearrange("p z d -> p (z d)"))
                last.then_inc(tp_ready, 1)

            def step_a(v):
                kind, h, layer = HEADS[v]
                b = take_tp("A", v)
                if kind == "fox":
                    wait_evac(pe, "fox")
                    q, k = (proj, h * HD), (proj, FOXW + h * HD)
                elif kind == "mla":
                    wait_evac(pe, "ukv")
                    wait_evac(pe, "ukv", 2)
                    q, k = (proj, h * MLA_Q), (proj, MLA_H * MLA_Q + h * MLA_KV)
                else:
                    wait_evac(pe, "mq_o" if layer else "mq_e")
                    q, k = (mq, h * HD), None
                for t in range(TT):
                    last = tr(b[:, t * P:(t + 1) * P], q[0][:, t, q[1]:q[1] + HD])
                if k:
                    for t in range(TT):
                        last = tr(b[:, SEQ + t * P:SEQ + (t + 1) * P], k[0][:, t, k[1]:k[1] + HD])
                last.then_inc(tp_ready, 1)
                if ("Ar", v) in TP:
                    b = take_tp("Ar", v)
                    pe.wait_ge(rope_q_ready, 1)
                    for t in range(TT):
                        last = tr(b[:, t * P:(t + 1) * P], q_rot[:, t, h // 2 * P:(h // 2 + 1) * P])
                    last.then_inc(tp_ready, 1)

            def step_b(v):
                kind, h, layer = HEADS[v]
                b = take_sc("B", v)
                wait_tp_free(pe, "A", v)
                qk = qk_of(v)
                if kind == "fox":
                    pe.wait_ge(c_ready, 1)
                if kind == "mla":
                    wait_tp_free(pe, "Ar", v - h % 2)
                    wait_tp_free(pe, "kr")
                for t, c, n in spans(v):
                    o, q = b[:, c:c + n], qk[:, t * P:(t + 1) * P]
                    if kind == "mem":
                        last = mm(o, q, mkt[layer][:, h, :], start=True, stop=True)
                        continue
                    mm(o, q, qk[:, SEQ:SEQ + n], start=True, stop=False)
                    mm(b[:, c + n - P:c + n], ident_b[:, :], (fox_mask if kind == "fox" else mla_mask)[:, :],
                       start=False, stop=False)
                    if kind == "fox":
                        one = sel[:, h:h + 1]
                        mm(o, c_pos[:, t * P:(t + 1) * P], one.to_broadcast([P, n]), start=False, stop=False)
                        last = mm(o, one.to_broadcast([P, P]), c_neg[:, 0:n], start=False, stop=True)
                    else:
                        last = mm(o, q_rot_t[h // 2 % 2][:, t * P:(t + 1) * P], k_rot_t[:, h % 2, 0:n],
                                  start=False, stop=True)
                last.then_inc(score_ready, 1)

            def step_d(v):
                b = take_tp("D", v)
                pe.wait_ge(exp_ready, v + 1)
                for i in range(len(blocks(v))):
                    last = tr(b[:, i * P:(i + 1) * P], p_of(v)[:, i * P:(i + 1) * P])
                last.then_inc(tp_ready, 1)

            def step_e(v):
                wait_tp_free(pe, "D", v)
                b, bl = sc("B", v), blocks(v)
                for i, (t, k) in enumerate(bl):
                    last = mm(b[:, t * P:(t + 1) * P], pt_of(v)[:, i * P:(i + 1) * P], values(v, k),
                              start=(k == 0), stop=(i + 1 == len(bl) or bl[i + 1][0] != t))
                last.then_inc(out_ready, 1)

            def step_ga_t():
                b = take_tp("gaT")
                wait_evac(pe, "mq_o")
                for t in range(TT):
                    last = tr(b[0:GRANK, t * P:(t + 1) * P], mq[:, t, MEMW:MQGA])
                last.then_inc(tp_ready, 1)

            def step_gz(h):
                b = take_tp("Gz", h)
                wait_tp_free(pe, "gaT")
                pe.wait_ge(wa2_in, 16)
                for kk in range(2):
                    c = h * GLA_DK + kk * P
                    last = mm(b[:, kk * SEQ:(kk + 1) * SEQ], wa2[:, c:c + P], ga_t[:, :], start=True, stop=True)
                last.then_inc(tp_ready, 1)

            def step_gqk(step, h, base):
                b = take_tp(step, h)
                wait_evac(pe, "gqkv", 2)
                wait_evac(pe, "gqkv", 3)
                for kk in range(2):
                    for t in range(TT):
                        c = base + h * GLA_DK + kk * P
                        last = tr(b[:, kk * SEQ + t * P:kk * SEQ + (t + 1) * P], proj[:, t, c:c + P])
                last.then_inc(tp_ready, 1)

            def step_ga(h):
                b = take_sc("Ga", h)
                wait_tp_free(pe, "Gq", h)
                wait_tp_free(pe, "Gk", h)
                for t in range(TT):
                    for keys, r, n in ((g_en, 0, 0), (g_a, 0, CHUNK), (g_en, CHUNK, CHUNK)):
                        for kk in range(2):
                            at = kk * SEQ + t * P
                            last = mm(b[r:r + CHUNK, t * P + n:t * P + n + CHUNK],
                                      keys[:, at + r:at + r + CHUNK], g_qd[:, at + n:at + n + CHUNK],
                                      start=(kk == 0), stop=(kk == 1))
                pe.wait_ge(gla_q_ready, h + 1)
                for kk in range(2):
                    at = slice(kk * P, (kk + 1) * P)
                    last = mm(b[:, TT * P:(TT + 1) * P], g_ke_t[:, at], g_qs[:, at], start=(kk == 0), stop=(kk == 1))
                last.then_inc(gla_att_ready, 1)

            def step_g0(h):
                at = 2 * GLA_H * GLA_DK + h * GLA_DV
                b = take_sc("Go", h, 0)
                wait_evac(pe, "gqkv", 6)
                wait_evac(pe, "gqkv", 7)
                pe.wait_ge(sc_free[SC["Ga", h] % 2], SC["Ga", h] // 2 + 1)
                mm(b[:, :], g_att[:, 0, :], proj[:, 0, at:at + GLA_DV], start=True,
                   stop=True).then_inc(gla_out_ready, 1)

            def step_g1(h):
                at = 2 * GLA_H * GLA_DK + h * GLA_DV
                b = take_sc("Go", h, 1)
                mm(b[:, :], g_att[:, TT, :], proj[:, 0, at:at + GLA_DV], start=True, stop=False)
                mm(b[:, :], g_att[:, 1, :], proj[:, 1, at:at + GLA_DV], start=False,
                   stop=True).then_inc(gla_out_ready, 1)

            steps = {"T": step_t, "mk": step_mk, "ff": step_ff, "kr": step_kr, "A": step_a, "B": step_b,
                     "D": step_d, "E": step_e, "gaT": step_ga_t, "Gz": step_gz,
                     "Gq": lambda h: step_gqk("Gq", h, 0),
                     "Gk": lambda h: step_gqk("Gk", h, GLA_H * GLA_DK), "Ga": step_ga,
                     "G0": step_g0, "G1": step_g1}

            def side_work(n, q):
                if q is None:
                    for step, arg in AFTER.get(n, ()):
                        if step in steps:
                            steps[step](*arg)

            for step, arg in BEFORE:
                if step in steps:
                    steps[step](*arg)
            run_streams(pe, project, side_work, 0)


WEIGHTS = ["x", "mem", "e_w_in", "e_fox_b_f", "e_mla_w_uq", "e_mla_w_ukv", "e_w_mem_kv", "e_w_out",
           "o_w_in", "o_gla_w_a2", "o_w_mem_kv", "o_w_out", "final_norm_w"]


def kernel(**inputs):
    import concourse.bacc as bacc
    from concourse.bass_utils import run_bass_kernel_spmd

    arrays = {name: np.ascontiguousarray(inputs[name]) for name in WEIGHTS}

    def columns(name):
        return np.asarray(inputs[name])[0].reshape(-1, P).T

    arrays["gains"] = np.ascontiguousarray(np.concatenate([columns(n) for n in (
        "e_norm_w", "o_norm_w", "e_mem_norm_w", "o_mem_norm_w", "e_mla_q_norm_w", "e_mla_kv_norm_w",
        "o_gla_norm_w", "o_gla_b_a")], axis=1))
    arrays["pos"] = np.ascontiguousarray(np.asarray(inputs["positions"]).reshape(TT, P).T)
    arrays["x_t"] = np.ascontiguousarray(arrays["x"][0].T)
    arrays["mem_t"] = np.ascontiguousarray(arrays["mem"][0].T)

    def packed(name, *cols):
        return np.ascontiguousarray(np.concatenate([arrays[name][:, :, c:c + n] for c, n in cols], axis=2))

    arrays["e_ckv_ff"] = packed("e_w_in", (E_CKV, KVRANK + ROPE), (E_FF, FOX_H))
    arrays["o_mq_ga"] = packed("o_w_in", (O_MQ, MEMW), (O_GA, GRANK))
    f = np.float32(1.0) / (np.float32(10000.0) ** (np.arange(0, ROPE, 2, dtype=np.float32) / np.float32(ROPE)))
    arrays["freq"] = np.ascontiguousarray(np.broadcast_to(f.astype(np.float32), (P, ROPE // 2)))

    nc = bacc.Bacc("TRN2", target_bir_lowering=False, num_devices=1)
    t_in = {name: nc.dram_tensor(f"in_{name}", a.shape, mybir.dt.from_np(a.dtype), kind="ExternalInput").ap()
            for name, a in arrays.items()}
    out = nc.dram_tensor("out_0", (1, SEQ, D), F32, kind="ExternalOutput").ap()
    build(nc, t_in, out)
    r = run_bass_kernel_spmd(nc, [{f"in_{name}": a for name, a in arrays.items()}], core_ids=[0])
    return r.results[0]["out_0"]
```
